# Optimizing a Trainium2 kernel written in Bass

```python
import math
import jax, jax.numpy as jnp
from jax import lax
import numpy as np

D_MODEL = 1024
BATCH = 1
SEQ = 256
DEPTH = 2

D_MIX = D_MODEL
HEAD_DIM = 64
RET_HEADS = 4
RET_WIDTH = RET_HEADS * HEAD_DIM
RET_CHUNK = 128
ROPE_BASE = 10000.0
NSA_HEADS = 8
NSA_KV_HEADS = 2
NSA_GROUP = NSA_HEADS // NSA_KV_HEADS
NSA_WIDTH = NSA_HEADS * HEAD_DIM
NSA_KV_WIDTH = NSA_KV_HEADS * HEAD_DIM
CMP_LEN = 32
CMP_STRIDE = 16
SEL_LEN = 64
N_SELECT = 16
WINDOW = 512
NSA_QBLOCK = 64
N_BRANCH = 3
FORCE_SCORE = 1.0e4
LRU_WIDTH = D_MIX - RET_WIDTH - NSA_WIDTH
LRU_BLOCKS = 4
LRU_BLOCK_DIM = LRU_WIDTH // LRU_BLOCKS
CONV_WIDTH = 4
LRU_C = 8.0
DEEPNORM_ALPHA = (2.0 * DEPTH) ** 0.25
DEEPNORM_BETA = (8.0 * DEPTH) ** -0.25
LN_EPS = 1e-5

IN_SIZES = (RET_WIDTH,) * 4 + (NSA_WIDTH,) + (NSA_KV_WIDTH,) * 6 + (NSA_WIDTH, NSA_HEADS * N_BRANCH, LRU_WIDTH, LRU_WIDTH)
D_IN = sum(IN_SIZES)
IN_SPLIT_POINTS = tuple(int(v) for v in np.cumsum(IN_SIZES)[:-1])


def _normalize(x):
    xf = x.astype(jnp.float32)
    mu = jnp.mean(xf, axis=-1, keepdims=True)
    var = jnp.mean(jnp.square(xf - mu), axis=-1, keepdims=True)
    return (xf - mu) * lax.rsqrt(var + LN_EPS)

def layer_norm(x, g, b):
    return (_normalize(x) * g.astype(jnp.float32) + b.astype(jnp.float32)).astype(x.dtype)

def rotary(x, pos):
    half = x.shape[-1] // 2
    inv = 1.0 / (ROPE_BASE ** (jnp.arange(half, dtype=jnp.float32) / half))
    ang = pos.astype(jnp.float32)[:, None] * inv[None, :]
    cos, sin = jnp.cos(ang), jnp.sin(ang)
    x1, x2 = x[..., :half], x[..., half:]
    return jnp.concatenate([x1 * cos - x2 * sin, x1 * sin + x2 * cos], axis=-1).astype(x.dtype)

def masked_softmax(s, mask):
    logits = jnp.where(mask, s.astype(jnp.float32), -1e30)
    return jax.nn.softmax(logits, axis=-1)

def retention(q, k, v):
    B, S, _ = q.shape
    dt = q.dtype
    H, d, C = RET_HEADS, HEAD_DIM, RET_CHUNK
    nc = S // C

    def heads(t):
        return t.reshape(B, S, H, d).transpose(0, 2, 1, 3)

    pos = jnp.arange(S)
    qh = rotary(heads(q), pos)
    kh = rotary(heads(k), pos) * (d ** -0.5)
    vh = heads(v)
    log_g = jnp.log(1.0 - 2.0 ** (-5.0 - jnp.arange(H, dtype=jnp.float32)))
    idx = jnp.arange(C, dtype=jnp.float32)
    diff = idx[:, None] - idx[None, :]
    inner_decay = jnp.where(diff >= 0, jnp.exp(jnp.maximum(diff, 0.0)[None] * log_g[:, None, None]), 0.0).astype(dt)
    key_decay = jnp.exp((C - 1.0 - idx)[None, :] * log_g[:, None]).astype(dt)
    query_decay = jnp.exp((idx + 1.0)[None, :] * log_g[:, None]).astype(dt)
    chunk_decay = jnp.exp(C * log_g).astype(dt)

    qc = qh.reshape(B, H, nc, C, d)
    kc = kh.reshape(B, H, nc, C, d)
    vc = vh.reshape(B, H, nc, C, d)
    scores = jnp.einsum('bhnid,bhnjd->bhnij', qc, kc) * inner_decay[None, :, None]
    inner = jnp.einsum('bhnij,bhnjd->bhnid', scores, vc)
    kv = jnp.einsum('bhnjd,bhnje->nbhde', kc * key_decay[None, :, None, :, None], vc)

    def step(state, kv_c):
        return state * chunk_decay[None, :, None, None] + kv_c, state

    _, states = lax.scan(step, jnp.zeros((B, H, d, d), dt), kv)
    cross = jnp.einsum('bhnid,nbhde->bhnie', qc, states) * query_decay[None, :, None, :, None]
    y = (inner + cross).reshape(B, H, S, d)
    y = _normalize(y).astype(dt)
    return y.transpose(0, 2, 1, 3).reshape(B, S, RET_WIDTH)

def nsa(xq, k_c, v_c, k_s, v_s, k_w, v_w, gate_logits, cmp_pos, cmp_w):
    B, S, _ = xq.shape
    dt = xq.dtype
    G, R, dh, QB = NSA_KV_HEADS, NSA_GROUP, HEAD_DIM, NSA_QBLOCK
    q = xq.reshape(B, S, G, R, dh).transpose(0, 2, 3, 1, 4) * (dh ** -0.5)

    def kvh(t):
        return t.reshape(B, S, G, dh).transpose(0, 2, 1, 3)

    n_cmp = (S - CMP_LEN) // CMP_STRIDE + 1
    tok = np.arange(n_cmp)[:, None] * CMP_STRIDE + np.arange(CMP_LEN)[None, :]

    def compress(t, pos, w):
        blocks = t[:, :, tok] + pos
        return blocks.reshape(B, G, n_cmp, CMP_LEN * dh) @ w

    kc = compress(kvh(k_c), cmp_pos[0], cmp_w[0])
    vc = compress(kvh(v_c), cmp_pos[1], cmp_w[1])
    cmp_end = np.arange(n_cmp) * CMP_STRIDE + CMP_LEN - 1

    n_sel = S // SEL_LEN
    ci = np.arange(n_cmp)[:, None]
    sj = np.arange(n_sel)[None, :]
    overlap = np.minimum(ci * CMP_STRIDE + CMP_LEN, sj * SEL_LEN + SEL_LEN) - np.maximum(ci * CMP_STRIDE, sj * SEL_LEN)
    sel_map = jnp.asarray(np.clip(overlap, 0, None) / CMP_STRIDE, dtype=jnp.float32)
    top = min(N_SELECT, n_sel)
    ks_blocks = kvh(k_s).reshape(B, G, n_sel, SEL_LEN, dh)
    vs_blocks = kvh(v_s).reshape(B, G, n_sel, SEL_LEN, dh)
    gather = jax.vmap(jax.vmap(lambda blk, ix: blk[ix]))

    pad = ((0, 0), (0, 0), (WINDOW, 0), (0, 0))
    kw = jnp.pad(kvh(k_w), pad)
    vw = jnp.pad(kvh(v_w), pad)

    gates = jax.nn.sigmoid(gate_logits.astype(jnp.float32)).astype(dt)
    gates = gates.reshape(B, S, G, R, N_BRANCH).transpose(0, 2, 3, 1, 4)

    def block(i):
        start = i * QB
        t = start + jnp.arange(QB)
        qb = lax.dynamic_slice_in_dim(q, start, QB, axis=3)
        gb = lax.dynamic_slice_in_dim(gates, start, QB, axis=3)
        m_c = cmp_end[None, :] <= t[:, None]
        p_c = masked_softmax(jnp.einsum('bgrqd,bgnd->bgrqn', qb, kc), m_c)
        p_c = p_c * jnp.any(m_c, axis=-1)[:, None]
        o_c = jnp.einsum('bgrqn,bgnd->bgrqd', p_c.astype(dt), vc)
        imp = jnp.einsum('bgrqn,nj->bgqj', p_c, sel_map)
        j = jnp.arange(n_sel)[None, :]
        cur = (t // SEL_LEN)[:, None]
        forced = (j == 0) | (j == cur) | (j == cur - 1)
        causal = j * SEL_LEN <= t[:, None]
        imp = jnp.where(forced, FORCE_SCORE, jnp.where(causal, imp, -FORCE_SCORE))
        _, idx = lax.top_k(imp, top)
        k_sel = gather(ks_blocks, idx).reshape(B, G, QB, top * SEL_LEN, dh)
        v_sel = gather(vs_blocks, idx).reshape(B, G, QB, top * SEL_LEN, dh)
        kpos = (idx[..., None] * SEL_LEN + jnp.arange(SEL_LEN)).reshape(B, G, QB, top * SEL_LEN)
        m_s = (kpos <= t[:, None])[:, :, None]
        p_s = masked_softmax(jnp.einsum('bgrqd,bgqkd->bgrqk', qb, k_sel), m_s)
        o_s = jnp.einsum('bgrqk,bgqkd->bgrqd', p_s.astype(dt), v_sel)
        kwb = lax.dynamic_slice_in_dim(kw, start, WINDOW + QB, axis=2)
        vwb = lax.dynamic_slice_in_dim(vw, start, WINDOW + QB, axis=2)
        jpos = start - WINDOW + jnp.arange(WINDOW + QB)
        m_w = (jpos[None, :] >= 0) & (jpos[None, :] <= t[:, None]) & (jpos[None, :] > t[:, None] - WINDOW)
        p_w = masked_softmax(jnp.einsum('bgrqd,bgkd->bgrqk', qb, kwb), m_w)
        o_w = jnp.einsum('bgrqk,bgkd->bgrqd', p_w.astype(dt), vwb)
        return gb[..., 0:1] * o_c + gb[..., 1:2] * o_s + gb[..., 2:3] * o_w

    out = lax.map(block, jnp.arange(S // QB))
    return out.transpose(1, 0, 4, 2, 3, 5).reshape(B, S, NSA_WIDTH)

def rg_lru(x, conv_w, conv_b, w_a, b_a, w_x, b_x, lam):
    B, S, C = x.shape
    xc = lax.conv_general_dilated(x, conv_w[:, None, :], window_strides=(1,),
                                  padding=((CONV_WIDTH - 1, 0),),
                                  dimension_numbers=('NWC', 'WIO', 'NWC'),
                                  feature_group_count=C) + conv_b
    xb = xc.reshape(B, S, LRU_BLOCKS, LRU_BLOCK_DIM)
    r = jax.nn.sigmoid((jnp.einsum('bsnd,nde->bsne', xb, w_a).reshape(B, S, C) + b_a).astype(jnp.float32))
    i = jax.nn.sigmoid((jnp.einsum('bsnd,nde->bsne', xb, w_x).reshape(B, S, C) + b_x).astype(jnp.float32))
    log_a = -LRU_C * r * jax.nn.softplus(-lam.astype(jnp.float32))
    a = jnp.exp(log_a)
    u = jnp.sqrt(-jnp.expm1(2.0 * log_a)) * (i * xc.astype(jnp.float32))

    def combine(lhs, rhs):
        a1, b1 = lhs
        a2, b2 = rhs
        return a1 * a2, a2 * b1 + b2

    _, h = lax.associative_scan(combine, (a, u), axis=1)
    return h.astype(x.dtype)

def hybrid_layer(x, w_in, w_out, ln_g, ln_b, cmp_pos, cmp_w, conv_w, conv_b, w_a, b_a, w_x, b_x, lam):
    proj = x @ w_in
    (rq, rk, rv, rg, nq, nkc, nvc, nks, nvs, nkw, nvw, ng, ngl, lx, lg) = jnp.split(proj, IN_SPLIT_POINTS, axis=-1)
    y_ret = retention(rq, rk, rv) * jax.nn.silu(rg)
    y_nsa = nsa(nq, nkc, nvc, nks, nvs, nkw, nvw, ngl, cmp_pos, cmp_w) * jax.nn.silu(ng)
    y_lru = rg_lru(lx, conv_w, conv_b, w_a, b_a, w_x, b_x, lam) * jax.nn.silu(lg)
    y = jnp.concatenate([y_ret, y_nsa, y_lru], axis=-1) @ w_out
    return layer_norm(DEEPNORM_ALPHA * x + y, ln_g, ln_b)

def first_inputs(seed: int = 0) -> dict:
    key = jax.random.key(seed)
    ks = jax.random.split(key, 16)
    f32 = jnp.float32
    x = jax.random.normal(ks[0], (BATCH, SEQ, D_MODEL), f32)
    w_in = jax.random.normal(ks[1], (DEPTH, D_MODEL, D_IN), f32) * D_MODEL ** -0.5
    w_out = jax.random.normal(ks[2], (DEPTH, D_MIX, D_MODEL), f32) * (D_MIX ** -0.5) * DEEPNORM_BETA
    ln_g = 1.0 + 0.02 * jax.random.normal(ks[3], (DEPTH, D_MODEL), f32)
    ln_b = 0.02 * jax.random.normal(ks[4], (DEPTH, D_MODEL), f32)
    nsa_cmp_pos = 0.1 * jax.random.normal(ks[5], (DEPTH, 2, CMP_LEN, HEAD_DIM), f32)
    nsa_cmp_w = jax.random.normal(ks[6], (DEPTH, 2, CMP_LEN * HEAD_DIM, HEAD_DIM), f32) * (CMP_LEN * HEAD_DIM) ** -0.5
    lru_conv_w = jax.random.normal(ks[7], (DEPTH, CONV_WIDTH, LRU_WIDTH), f32) * CONV_WIDTH ** -0.5
    lru_conv_b = 0.02 * jax.random.normal(ks[8], (DEPTH, LRU_WIDTH), f32)
    lru_w_a = jax.random.normal(ks[9], (DEPTH, LRU_BLOCKS, LRU_BLOCK_DIM, LRU_BLOCK_DIM), f32) * LRU_BLOCK_DIM ** -0.5
    lru_b_a = 0.02 * jax.random.normal(ks[10], (DEPTH, LRU_WIDTH), f32)
    lru_w_x = jax.random.normal(ks[11], (DEPTH, LRU_BLOCKS, LRU_BLOCK_DIM, LRU_BLOCK_DIM), f32) * LRU_BLOCK_DIM ** -0.5
    lru_b_x = 0.02 * jax.random.normal(ks[12], (DEPTH, LRU_WIDTH), f32)
    u = jax.random.uniform(ks[13], (DEPTH, LRU_WIDTH), f32, minval=0.9, maxval=0.999)
    a0 = u ** (1.0 / LRU_C)
    lru_lambda = jnp.log(a0) - jnp.log1p(-a0)
    return {"x": x, "w_in": w_in, "w_out": w_out, "ln_g": ln_g, "ln_b": ln_b,
            "nsa_cmp_pos": nsa_cmp_pos, "nsa_cmp_w": nsa_cmp_w,
            "lru_conv_w": lru_conv_w, "lru_conv_b": lru_conv_b,
            "lru_w_a": lru_w_a, "lru_b_a": lru_b_a, "lru_w_x": lru_w_x, "lru_b_x": lru_b_x,
            "lru_lambda": lru_lambda}

def first_block(x, w_in, w_out, ln_g, ln_b, nsa_cmp_pos, nsa_cmp_w, lru_conv_w, lru_conv_b,
              lru_w_a, lru_b_a, lru_w_x, lru_b_x, lru_lambda):
    for l in range(DEPTH):
        x = hybrid_layer(x, w_in[l], w_out[l], ln_g[l], ln_b[l], nsa_cmp_pos[l], nsa_cmp_w[l],
                         lru_conv_w[l], lru_conv_b[l], lru_w_a[l], lru_b_a[l], lru_w_x[l], lru_b_x[l],
                         lru_lambda[l])
    return x


DEPTH_2 = 1

GRID_W = 64
CTX_LEN = 256
EPS = 1e-6

MLSTM_HEADS = 4
MLSTM_DH = 128
MLSTM_W = MLSTM_HEADS * MLSTM_DH
MLSTM_GATES = 2 * 2 * MLSTM_HEADS
MLSTM_CHUNK = 128

ATTN_Q_HEADS = 8
ATTN_KV_HEADS = 2
ATTN_GROUP = ATTN_Q_HEADS // ATTN_KV_HEADS
ATTN_DH = 64
ATTN_Q_W = ATTN_Q_HEADS * ATTN_DH
ATTN_KV_W = ATTN_KV_HEADS * ATTN_DH
WINDOW_2 = 128
ATTN_BLOCK = 128
ROPE_AXIS_FREQS = ATTN_DH // 4

N_BRANCH_2 = 2
IN_SIZES_2 = (MLSTM_W, MLSTM_W, MLSTM_W, MLSTM_W, MLSTM_GATES,
            ATTN_Q_W, ATTN_KV_W, ATTN_KV_W, N_BRANCH_2 * D_MODEL)
D_IN_2 = 4 * MLSTM_W + MLSTM_GATES + ATTN_Q_W + 2 * ATTN_KV_W + N_BRANCH_2 * D_MODEL

PEER_HEADS = 8
PEER_N_KEYS = 128
PEER_N_EXPERTS = PEER_N_KEYS * PEER_N_KEYS
PEER_KEY_DIM = 256
PEER_HALF = PEER_KEY_DIM // 2
PEER_TOPK = 16
PEER_BLOCK = 128


def _rms(x, g):
    xf = x.astype(jnp.float32)
    y = xf * lax.rsqrt(jnp.mean(xf * xf, axis=-1, keepdims=True) + EPS)
    return y.astype(x.dtype) * g

def _modulate(x, g, shift, scale):
    return _rms(x, g) * (1 + scale) + shift

def _adaln(cond, w, b):
    mod = jax.nn.silu(cond) @ w + b
    return tuple(m[:, None, :] for m in jnp.split(mod, 6, axis=-1))

def _split_in(p):
    idx = []
    acc = 0
    for s in IN_SIZES_2[:-1]:
        acc += s
        idx.append(acc)
    return jnp.split(p, idx, axis=-1)

def _axial_rope(T):
    rows = T // GRID_W
    row = jnp.broadcast_to(jnp.arange(rows)[:, None], (rows, GRID_W)).reshape(T)
    col = jnp.broadcast_to(jnp.arange(GRID_W)[None, :], (rows, GRID_W)).reshape(T)
    inv = ROPE_BASE ** (-jnp.arange(ROPE_AXIS_FREQS, dtype=jnp.float32) / ROPE_AXIS_FREQS)
    ang = jnp.concatenate([row[:, None].astype(jnp.float32) * inv,
                           col[:, None].astype(jnp.float32) * inv], axis=-1)
    return jnp.cos(ang), jnp.sin(ang)

def _rope(t, cos, sin):
    t1, t2 = jnp.split(t, 2, axis=-1)
    c = cos[None, :, None, :]
    s = sin[None, :, None, :]
    return jnp.concatenate([t1 * c - t2 * s, t2 * c + t1 * s], axis=-1).astype(t.dtype)

def _chunk_seq(t, reverse):
    if reverse:
        t = jnp.flip(t, axis=1)
    B, T = t.shape[:2]
    t = jnp.moveaxis(t, 2, 1)
    return t.reshape((B, t.shape[1], T // MLSTM_CHUNK, MLSTM_CHUNK) + t.shape[3:])

def _unchunk(h, reverse):
    B, H = h.shape[:2]
    h = jnp.moveaxis(h.reshape(B, H, -1, h.shape[-1]), 1, 2)
    return jnp.flip(h, axis=1) if reverse else h

def _mlstm_summaries(k, v, li, lf):
    b = jnp.cumsum(lf, axis=-1)
    a = b[..., -1]
    w_log = a[..., None] - b + li
    m_loc = jnp.max(w_log, axis=-1)
    w = jnp.exp(w_log - m_loc[..., None])
    C_loc = jnp.einsum('bhcs,bhcsk,bhcsv->bhckv', w, k, v)
    n_loc = jnp.einsum('bhcs,bhcsk->bhck', w, k)
    return b, a, m_loc, C_loc, n_loc

def _mlstm_scan(a, m_loc, C_loc, n_loc, state0):
    def step(carry, inp):
        C, n, m = carry
        a_c, m_c, C_c, n_c = inp
        m_new = jnp.maximum(a_c + m, m_c)
        d_old = jnp.exp(a_c + m - m_new)
        d_new = jnp.exp(m_c - m_new)
        C_new = d_old[..., None, None] * C + d_new[..., None, None] * C_c
        n_new = d_old[..., None] * n + d_new[..., None] * n_c
        return (C_new, n_new, m_new), (C, n, m)
    xs = tuple(jnp.moveaxis(t, 2, 0) for t in (a, m_loc, C_loc, n_loc))
    final, starts = lax.scan(step, state0, xs)
    starts = tuple(jnp.moveaxis(t, 0, 2) for t in starts)
    return starts, final

def _mlstm_outputs(q, k, v, li, b, starts):
    C_s, n_s, m_s = starts
    L = q.shape[-2]
    log_inter = b + m_s[..., None]
    log_d = b[..., :, None] - b[..., None, :] + li[..., None, :]
    seen = jnp.tril(jnp.ones((L, L), dtype=bool))
    log_d = jnp.where(seen, log_d, -jnp.inf)
    m_t = jnp.maximum(log_inter, jnp.max(log_d, axis=-1))
    s = jnp.einsum('bhctk,bhcsk->bhcts', q, k) * jnp.exp(log_d - m_t[..., None])
    inter = jnp.exp(log_inter - m_t)
    num = (jnp.einsum('bhcts,bhcsv->bhctv', s, v)
           + inter[..., None] * jnp.einsum('bhctk,bhckv->bhctv', q, C_s))
    den = jnp.sum(s, axis=-1) + inter * jnp.einsum('bhctk,bhck->bhct', q, n_s)
    return num / jnp.maximum(jnp.abs(den), jnp.exp(-m_t))[..., None]

def _mlstm_direction(ctx_in, lat_in, reverse, with_ctx_out):
    qc, kc, vc, ic, fc = (_chunk_seq(t, reverse) for t in ctx_in)
    ql, kl, vl, il, fl = (_chunk_seq(t, reverse) for t in lat_in)
    B, H = qc.shape[:2]
    state0 = (jnp.zeros((B, H, MLSTM_DH, MLSTM_DH), jnp.float32),
              jnp.zeros((B, H, MLSTM_DH), jnp.float32),
              jnp.zeros((B, H), jnp.float32))
    bc, ac, mc, Cc, nc = _mlstm_summaries(kc, vc, ic, fc)
    starts_c, final_c = _mlstm_scan(ac, mc, Cc, nc, state0)
    bl, al, ml, Cl, nl = _mlstm_summaries(kl, vl, il, fl)
    starts_l, _ = _mlstm_scan(al, ml, Cl, nl, final_c)
    h_lat = _unchunk(_mlstm_outputs(ql, kl, vl, il, bl, starts_l), reverse)
    h_ctx = _unchunk(_mlstm_outputs(qc, kc, vc, ic, bc, starts_c), reverse) if with_ctx_out else None
    return h_lat, h_ctx

def _mlstm_branch(parts_lat, parts_ctx, b_mgates, norm_g, with_ctx_out):
    def prep(parts):
        q, k, v, o, gates = parts
        B, T = q.shape[:2]
        hd = lambda t: t.astype(jnp.float32).reshape(B, T, MLSTM_HEADS, MLSTM_DH)
        g = (gates.astype(jnp.float32) + b_mgates.astype(jnp.float32)).reshape(B, T, 2, 2, MLSTM_HEADS)
        return hd(q), hd(k) * (MLSTM_DH ** -0.5), hd(v), o, g

    ql, kl, vl, ol, gl = prep(parts_lat)
    qc, kc, vc, oc, gc = prep(parts_ctx)
    hs_lat, hs_ctx = [], []
    for d, reverse in enumerate((False, True)):
        lat_in = (ql, kl, vl, gl[:, :, d, 0], jax.nn.log_sigmoid(gl[:, :, d, 1]))
        ctx_in = (qc, kc, vc, gc[:, :, d, 0], jax.nn.log_sigmoid(gc[:, :, d, 1]))
        hl, hc = _mlstm_direction(ctx_in, lat_in, reverse, with_ctx_out)
        hs_lat.append(hl)
        hs_ctx.append(hc)

    def finish(h, o):
        B, T = h.shape[:2]
        hn = h * lax.rsqrt(jnp.mean(h * h, axis=-1, keepdims=True) + EPS)
        return hn.reshape(B, T, MLSTM_W).astype(o.dtype) * norm_g * jax.nn.sigmoid(o)

    m_lat = finish(hs_lat[0] + hs_lat[1], ol)
    m_ctx = finish(hs_ctx[0] + hs_ctx[1], oc) if with_ctx_out else None
    return m_lat, m_ctx

def _softmax_with_sink(logits, sink_b):
    sink_col = jnp.broadcast_to(sink_b, logits.shape[:-1] + (1,))
    return jax.nn.softmax(jnp.concatenate([logits, sink_col], axis=-1), axis=-1)[..., :-1]

def _window_attention(q, k, v, kc, vc, sink):
    B, T = q.shape[:2]
    nb = T // ATTN_BLOCK
    scale = ATTN_DH ** -0.5
    qb = q.reshape(B, nb, ATTN_BLOCK, ATTN_KV_HEADS, ATTN_GROUP, ATTN_DH)

    def band(t):
        tp = jnp.pad(t, ((0, 0), (ATTN_BLOCK, ATTN_BLOCK), (0, 0), (0, 0)))
        tp = tp.reshape(B, nb + 2, ATTN_BLOCK, ATTN_KV_HEADS, ATTN_DH)
        return jnp.concatenate([tp[:, :-2], tp[:, 1:-1], tp[:, 2:]], axis=2)

    kw, vw = band(k), band(v)
    qi = jnp.arange(ATTN_BLOCK)[:, None]
    kj = jnp.arange(3 * ATTN_BLOCK)[None, :]
    key_pos = jnp.arange(nb)[:, None, None] * ATTN_BLOCK - ATTN_BLOCK + kj[None]
    mask = (jnp.abs(kj - ATTN_BLOCK - qi) <= WINDOW_2)[None] & (key_pos >= 0) & (key_pos < T)
    s_loc = jnp.einsum('bnqhgd,bnkhd->bnhgqk', qb, kw).astype(jnp.float32) * scale
    s_loc = jnp.where(mask[None, :, None, None], s_loc, -jnp.inf)
    s_ctx = jnp.einsum('bnqhgd,bchd->bnhgqc', qb, kc).astype(jnp.float32) * scale
    sink_b = sink.astype(jnp.float32).reshape(ATTN_KV_HEADS, ATTN_GROUP, 1, 1)
    p = _softmax_with_sink(jnp.concatenate([s_loc, s_ctx], axis=-1), sink_b)
    p_loc = p[..., :3 * ATTN_BLOCK].astype(v.dtype)
    p_ctx = p[..., 3 * ATTN_BLOCK:].astype(v.dtype)
    out = (jnp.einsum('bnhgqk,bnkhd->bnqhgd', p_loc, vw)
           + jnp.einsum('bnhgqc,bchd->bnqhgd', p_ctx, vc))
    return out.reshape(B, T, ATTN_Q_W)

def _context_attention(qc, kc, vc, sink):
    B, Lc = qc.shape[:2]
    qg = qc.reshape(B, Lc, ATTN_KV_HEADS, ATTN_GROUP, ATTN_DH)
    s = jnp.einsum('bqhgd,bkhd->bhgqk', qg, kc).astype(jnp.float32) * (ATTN_DH ** -0.5)
    sink_b = sink.astype(jnp.float32).reshape(ATTN_KV_HEADS, ATTN_GROUP, 1, 1)
    p = _softmax_with_sink(s, sink_b).astype(vc.dtype)
    return jnp.einsum('bhgqk,bkhd->bqhgd', p, vc).reshape(B, Lc, ATTN_Q_W)

def _attn_branch(parts_lat, parts_ctx, q_g, k_g, sink, cos, sin, with_ctx_out):
    def heads(t, h):
        return t.reshape(t.shape[0], t.shape[1], h, ATTN_DH)
    ql, kl, vl = parts_lat
    qc, kc, vc = parts_ctx
    ql = _rope(_rms(heads(ql, ATTN_Q_HEADS), q_g), cos, sin)
    kl = _rope(_rms(heads(kl, ATTN_KV_HEADS), k_g), cos, sin)
    vl = heads(vl, ATTN_KV_HEADS)
    kc = _rms(heads(kc, ATTN_KV_HEADS), k_g)
    vc = heads(vc, ATTN_KV_HEADS)
    a_lat = _window_attention(ql, kl, vl, kc, vc, sink)
    a_ctx = None
    if with_ctx_out:
        a_ctx = _context_attention(_rms(heads(qc, ATTN_Q_HEADS), q_g), kc, vc, sink)
    return a_lat, a_ctx

def _token_mixer(h_lat, h_ctx, w_in, b_mgates, mlstm_norm_g, q_g, k_g, sink,
                 w_bm, w_ba, w_out, cos, sin, with_ctx_out):
    pl = _split_in(h_lat @ w_in)
    pc = _split_in(h_ctx @ w_in)
    m_lat, m_ctx = _mlstm_branch(pl[:5], pc[:5], b_mgates, mlstm_norm_g, with_ctx_out)
    a_lat, a_ctx = _attn_branch(pl[5:8], pc[5:8], q_g, k_g, sink, cos, sin, with_ctx_out)

    def merge(m, a, gates):
        g_m, g_a = jnp.split(gates, 2, axis=-1)
        return (jax.nn.sigmoid(g_m) * (m @ w_bm) + jax.nn.sigmoid(g_a) * (a @ w_ba)) @ w_out

    y_lat = merge(m_lat, a_lat, pl[8])
    y_ctx = merge(m_ctx, a_ctx, pc[8]) if with_ctx_out else None
    return y_lat, y_ctx

def _peer(h, w_query, sub_keys, expert_u, expert_v):
    B, T, D = h.shape
    tok = h.reshape(-1, PEER_BLOCK, D)

    def block(xb):
        q = (xb @ w_query).reshape(PEER_BLOCK, PEER_HEADS, 2, PEER_HALF)
        s = jnp.einsum('mhpd,hpnd->mhpn', q, sub_keys).astype(jnp.float32)
        s1, i1 = lax.top_k(s[:, :, 0], PEER_TOPK)
        s2, i2 = lax.top_k(s[:, :, 1], PEER_TOPK)
        cand = (s1[..., :, None] + s2[..., None, :]).reshape(PEER_BLOCK, PEER_HEADS, PEER_TOPK * PEER_TOPK)
        cidx = (i1[..., :, None] * PEER_N_KEYS + i2[..., None, :]).reshape(PEER_BLOCK, PEER_HEADS, PEER_TOPK * PEER_TOPK)
        top, pos = lax.top_k(cand, PEER_TOPK)
        idx = jnp.take_along_axis(cidx, pos, axis=-1)
        g = jax.nn.softmax(top, axis=-1)
        act = jax.nn.gelu(jnp.einsum('mhkd,md->mhk', expert_u[idx], xb).astype(jnp.float32))
        w = (g * act).astype(xb.dtype)
        return jnp.einsum('mhk,mhkd->md', w, expert_v[idx])

    return lax.map(block, tok).reshape(B, T, D)

def second_inputs(seed: int = 0) -> dict:
    key = jax.random.key(seed)
    ks = jax.random.split(key, 24)
    f32 = jnp.float32

    def nrm(k, shape, s):
        return jax.random.normal(k, shape, f32) * s

    gate_base = jnp.tile(jnp.concatenate([jnp.zeros((MLSTM_HEADS,), f32),
                                          jnp.linspace(3.0, 6.0, MLSTM_HEADS, dtype=f32)]), 2)
    return {
        'x': nrm(ks[0], (BATCH, SEQ, D_MODEL), 1.0),
        'c': nrm(ks[1], (BATCH, D_MODEL), 1.0),
        'ctx': nrm(ks[2], (BATCH, CTX_LEN, D_MODEL), 1.0),
        'c_ctx': nrm(ks[3], (D_MODEL,), 1.0),
        'w_ada': nrm(ks[4], (DEPTH_2, D_MODEL, 6 * D_MODEL), D_MODEL ** -0.5),
        'b_ada': nrm(ks[5], (DEPTH_2, 6 * D_MODEL), 0.02),
        'norm_mix_g': 1.0 + nrm(ks[6], (DEPTH_2, D_MODEL), 0.02),
        'norm_ffn_g': 1.0 + nrm(ks[7], (DEPTH_2, D_MODEL), 0.02),
        'w_in': nrm(ks[8], (DEPTH_2, D_MODEL, D_IN_2), D_MODEL ** -0.5),
        'b_mgates': gate_base + nrm(ks[9], (DEPTH_2, MLSTM_GATES), 0.1),
        'mlstm_norm_g': 1.0 + nrm(ks[10], (DEPTH_2, MLSTM_W), 0.02),
        'attn_q_norm_g': 1.0 + nrm(ks[11], (DEPTH_2, ATTN_DH), 0.02),
        'attn_k_norm_g': 1.0 + nrm(ks[12], (DEPTH_2, ATTN_DH), 0.02),
        'attn_sink': nrm(ks[13], (DEPTH_2, ATTN_Q_HEADS), 0.5),
        'w_branch_m': nrm(ks[14], (DEPTH_2, MLSTM_W, D_MODEL), MLSTM_W ** -0.5),
        'w_branch_a': nrm(ks[15], (DEPTH_2, ATTN_Q_W, D_MODEL), ATTN_Q_W ** -0.5),
        'w_out': nrm(ks[16], (DEPTH_2, D_MODEL, D_MODEL), D_MODEL ** -0.5),
        'peer_w_query': nrm(ks[17], (DEPTH_2, D_MODEL, PEER_HEADS * PEER_KEY_DIM), D_MODEL ** -0.5),
        'peer_sub_keys': nrm(ks[18], (DEPTH_2, PEER_HEADS, 2, PEER_N_KEYS, PEER_HALF), PEER_HALF ** -0.5),
        'peer_u': nrm(ks[19], (DEPTH_2, PEER_N_EXPERTS, D_MODEL), D_MODEL ** -0.5),
        'peer_v': nrm(ks[20], (DEPTH_2, PEER_N_EXPERTS, D_MODEL), 0.5),
    }

def second_block(x, c, ctx, c_ctx, w_ada, b_ada, norm_mix_g, norm_ffn_g, w_in, b_mgates,
              mlstm_norm_g, attn_q_norm_g, attn_k_norm_g, attn_sink, w_branch_m, w_branch_a,
              w_out, peer_w_query, peer_sub_keys, peer_u, peer_v):
    T = x.shape[1]
    cos, sin = _axial_rope(T)
    for layer in range(DEPTH_2):
        update_ctx = layer + 1 < DEPTH_2
        sh1, sc1, g1, sh2, sc2, g2 = _adaln(c, w_ada[layer], b_ada[layer])
        csh1, csc1, cg1, csh2, csc2, cg2 = _adaln(c_ctx[None], w_ada[layer], b_ada[layer])
        h_lat = _modulate(x, norm_mix_g[layer], sh1, sc1)
        h_ctx = _modulate(ctx, norm_mix_g[layer], csh1, csc1)
        y_lat, y_ctx = _token_mixer(h_lat, h_ctx, w_in[layer], b_mgates[layer], mlstm_norm_g[layer],
                                    attn_q_norm_g[layer], attn_k_norm_g[layer], attn_sink[layer],
                                    w_branch_m[layer], w_branch_a[layer], w_out[layer],
                                    cos, sin, update_ctx)
        x = x + g1 * y_lat
        x = x + g2 * _peer(_modulate(x, norm_ffn_g[layer], sh2, sc2), peer_w_query[layer],
                           peer_sub_keys[layer], peer_u[layer], peer_v[layer])
        if update_ctx:
            ctx = ctx + cg1 * y_ctx
            ctx = ctx + cg2 * _peer(_modulate(ctx, norm_ffn_g[layer], csh2, csc2), peer_w_query[layer],
                                    peer_sub_keys[layer], peer_u[layer], peer_v[layer])
    return x


def setup_inputs(seed=0):
    out = dict(first_inputs(seed))
    for name, value in second_inputs(seed + 1).items():
        if name != "x":
            out[name + "_2"] = value
    return out


def reference(
    x, w_in, w_out, ln_g, ln_b, nsa_cmp_pos, nsa_cmp_w, lru_conv_w, lru_conv_b, lru_w_a,
    lru_b_a, lru_w_x, lru_b_x, lru_lambda, c_2, ctx_2, c_ctx_2, w_ada_2, b_ada_2, norm_mix_g_2,
    norm_ffn_g_2, w_in_2, b_mgates_2, mlstm_norm_g_2, attn_q_norm_g_2, attn_k_norm_g_2,
    attn_sink_2, w_branch_m_2, w_branch_a_2, w_out_2, peer_w_query_2, peer_sub_keys_2, peer_u_2,
    peer_v_2,
):
    x = first_block(
        x, w_in, w_out, ln_g, ln_b, nsa_cmp_pos, nsa_cmp_w, lru_conv_w, lru_conv_b, lru_w_a,
        lru_b_a, lru_w_x, lru_b_x, lru_lambda,
    )
    return second_block(
        x, c_2, ctx_2, c_ctx_2, w_ada_2, b_ada_2, norm_mix_g_2, norm_ffn_g_2, w_in_2,
        b_mgates_2, mlstm_norm_g_2, attn_q_norm_g_2, attn_k_norm_g_2, attn_sink_2, w_branch_m_2,
        w_branch_a_2, w_out_2, peer_w_query_2, peer_sub_keys_2, peer_u_2, peer_v_2,
    )


_drawn_inputs = setup_inputs


def setup_inputs(seed=0):
    import zlib

    import numpy as np

    out = dict(_drawn_inputs(seed))
    spreads = {}
    factors = {'lru_b_a': 8.0,
     'lru_b_x': 8.0,
     'norm_mix_g_2': 3.138,
     'mlstm_norm_g_2': 16.994,
     'attn_q_norm_g_2': 8.0,
     'attn_k_norm_g_2': 8.0,
     'attn_sink_2': 8.0,
     'norm_ffn_g_2': 4.5}
    for name, (base, spread) in spreads.items():
        noise = np.random.default_rng([zlib.crc32(name.encode()), seed]).standard_normal(out[name].shape)
        drawn = base * np.exp(spread * noise) if base else spread * noise
        out[name] = __import__('jax').numpy.asarray(drawn.astype(out[name].dtype))
    for name, factor in factors.items():
        out[name] = (out[name] * factor).astype(out[name].dtype)
    return out
```

```python
import concourse.bass as bass
from concourse import mybir
from contextlib import ExitStack
import numpy as np

F32 = mybir.dt.float32
I32 = mybir.dt.int32
U32 = mybir.dt.uint32
ALU = mybir.AluOpType
ACT = mybir.ActivationFunctionType
AX = mybir.AxisListType

P = 128
D = 1024
KC = D // P
S = 256
TT = S // P
DEPTH = 2
HD = 64
EPS_LN = 1e-5
EPS_RMS = 1e-6
ALPHA = (2.0 * DEPTH) ** 0.25
NEG = -1e30
CMP_N = 15
CMP_L = 32
CMP_S = 16
LRU_C = 8.0
MH = 4
MD = 128
K_SCALE = MD ** -0.5
SLOT = KC * 512
NW = 3
ARENA = 28600
SMALL = 800
NBANK = 6
NACC = 2
EH = 8
TOPK = 16
NKEY = 128
RING = 8
STEPS = 62
CREDIT = 64
ATANH = [1.0 / (2 * k + 1) for k in range(1, 8)]

C_ID = 0
C_TRIL = C_ID + P
C_TRIU = C_TRIL + P
C_DECAY = C_TRIU + P
C_COSA = C_DECAY + 2 * 4 * P
C_SINA = C_COSA + TT * HD
C_COSB = C_SINA + TT * HD
C_SINB = C_COSB + TT * HD
C_MM = C_SINB + TT * HD
C_CMASK = C_MM + 4 * 512
C_ANY = C_CMASK + TT * CMP_N
C_IOTA = C_ANY + TT
C_NEGHALF = C_IOTA + TOPK
C_ZERO = C_NEGHALF + 8
C_END = C_ZERO + P

V_LRU = 0
V_POS = V_LRU + DEPTH * 16
V_WG = V_POS + DEPTH * 2 * CMP_L
V_MG = V_WG + DEPTH * 2 * 2 * HD
V_COND = V_MG + 2
V_END = V_COND + KC * 2


def constants():
    c = np.zeros((P, C_END), np.float32)
    i = np.arange(P)
    c[:, C_ID:C_ID + P] = np.eye(P)
    tril = np.where(i[None, :] <= i[:, None], 0.0, NEG)
    triu = np.where(i[None, :] >= i[:, None], 0.0, NEG)
    c[:, C_TRIL:C_TRIL + P] = tril
    c[:, C_TRIU:C_TRIU + P] = triu
    for h in range(4):
        lg = np.log(1.0 - 2.0 ** (-5.0 - h))
        diff = i[None, :] - i[:, None]
        diag = np.where(diff >= 0, np.exp(np.maximum(diff, 0) * lg), 0.0) * HD ** -0.5
        off = np.exp((diff + P) * lg) * HD ** -0.5
        c[:, C_DECAY + h * P:C_DECAY + (h + 1) * P] = diag
        c[:, C_DECAY + (4 + h) * P:C_DECAY + (5 + h) * P] = off
    half = HD // 2
    pos = np.arange(S)
    inv = (1.0 / (np.float32(10000.0) ** (np.arange(half, dtype=np.float32) / half))).astype(np.float32)
    ang_a = pos.astype(np.float32)[:, None] * inv
    nf = HD // 4
    inv_b = (np.float32(10000.0) ** (-np.arange(nf, dtype=np.float32) / nf)).astype(np.float32)
    ang_b = np.concatenate([(pos // 64).astype(np.float32)[:, None] * inv_b,
                            (pos % 64).astype(np.float32)[:, None] * inv_b], 1)
    for ang, cc, cs in ((ang_a, C_COSA, C_SINA), (ang_b, C_COSB, C_SINB)):
        cos, sin = np.cos(ang), np.sin(ang)
        for t in range(TT):
            r = slice(t * P, (t + 1) * P)
            c[:, cc + t * HD:cc + (t + 1) * HD] = np.concatenate([cos[r], cos[r]], 1)
            c[:, cs + t * HD:cs + (t + 1) * HD] = np.concatenate([-sin[r], sin[r]], 1)
    full = np.full((P, P), NEG)
    zero = np.zeros((P, P))
    masks = {(0, 0): [zero, zero, tril, full], (0, 1): [zero, zero, zero, tril],
             (1, 0): [zero, zero, triu, zero], (1, 1): [zero, zero, full, triu]}
    for (d, t), m in masks.items():
        at = C_MM + (d * TT + t) * 512
        c[:, at:at + 512] = np.concatenate(m, 1)
    ends = np.arange(CMP_N) * CMP_S + CMP_L - 1
    for t in range(TT):
        tok = t * P + i
        ok = ends[None, :] <= tok[:, None]
        c[:, C_CMASK + t * CMP_N:C_CMASK + (t + 1) * CMP_N] = np.where(ok, 0.0, NEG)
        c[:, C_ANY + t] = ok.any(1)
    c[:, C_IOTA:C_IOTA + TOPK] = np.arange(TOPK)
    c[:, C_NEGHALF:C_NEGHALF + 8] = -0.5
    return c


def view(ap, offset, dims):
    return bass.AP(ap.tensor, ap.offset + offset, [list(ap.ap[0])] + [list(d) for d in dims])


def every(ap, n, axis=1):
    dims = [list(d) for d in ap.ap]
    dims.insert(axis, [0, n])
    return bass.AP(ap.tensor, ap.offset, dims)


def program(nc, a, out):
    ctx = ExitStack()
    sems = {}

    def sem(name):
        if name not in sems:
            sems[name] = ctx.enter_context(nc.semaphore(name))
        return sems[name]

    def sb(name, width, dt=F32):
        return ctx.enter_context(nc.sbuf_tensor(name, [P, width], dt))

    with ctx:
        const = sb("const", C_END)
        par = sb("par", V_END)
        wring = sb("wring", NW * SLOT)
        x = sb("x", TT * D)
        hT_all = sb("hT", KC * 512)
        small = sb("small", SMALL)
        arena = sb("arena", ARENA)
        used = {"a": 0, "s": 0}

        def take_small(n):
            at = used["s"]
            used["s"] += n
            assert used["s"] <= SMALL
            return small[:, at:at + n]

        def take(n, at=None):
            if at is None:
                at = used["a"]
                used["a"] += n
                assert used["a"] <= ARENA, used
            return arena[:, at:at + n]

        psum = [ctx.enter_context(nc.psum_tensor(f"bank{b}", [P, 512], F32)) for b in range(NBANK + NACC)]
        bank_full = [sem(f"bank_full{b}") for b in range(NBANK + NACC)]
        bank_free = [sem(f"bank_free{b}") for b in range(NBANK + NACC)]

        ident = const[:, C_ID:C_ID + P]
        x3 = x[:, :].rearrange("p (t d) -> p t d", t=TT)
        hT = hT_all[:, :].rearrange("p (k s) -> p k s", k=KC)
        xT = hT[:, :, S:2 * S]

        qT = take(4 * S).rearrange("p (r s) -> p r s", r=4)
        kT = take(2 * S).rearrange("p (b s) -> p b s", b=2)
        blocksT = take(2 * CMP_L * CMP_N).rearrange("p (b l n) -> p b l n", b=2, l=CMP_L)
        lru_x = take(2 * (S + 3)).rearrange("p (b s) -> p b s", b=2)
        lru_gate = take(2 * S).rearrange("p (b s) -> p b s", b=2)
        rot = take(TT * 512).rearrange("p (t c) -> p t c", t=TT)
        retT = take(4 * S).rearrange("p (b s) -> p b s", b=4)
        ret_v = take(TT * S).rearrange("p (t c) -> p t c", t=TT)
        ret_g = take(TT * S).rearrange("p (t c) -> p t c", t=TT)
        nsa_v = take(TT * 256).rearrange("p (t c) -> p t c", t=TT)
        nsa_gt = take(TT * 24).rearrange("p (t c) -> p t c", t=TT)
        nsa_g = take(TT * 512).rearrange("p (t c) -> p t c", t=TT)
        ret_s = take(3 * 512).rearrange("p (j c) -> p j c", j=3)
        probs = take(3 * 512).rearrange("p (j c) -> p j c", j=3)
        cmp_s = take(TT * 8 * CMP_N).rearrange("p (t h n) -> p t h n", t=TT, h=8)
        probsT = take(2 * 512).rearrange("p (j c) -> p j c", j=2)
        cmpT = take(TT * 8 * P).rearrange("p (t h s) -> p t h s", t=TT, h=8)
        kcT = take(CMP_N)
        vc = take(P)
        conv = take(2 * S).rearrange("p (b s) -> p b s", b=2)
        lru_r = take(2 * S).rearrange("p (b s) -> p b s", b=2)
        lru_i = take(2 * S).rearrange("p (b s) -> p b s", b=2)
        lru_a = take(2 * S).rearrange("p (b s) -> p b s", b=2)
        lru_t = take(2 * S).rearrange("p (b s) -> p b s", b=2)
        lru_h = take(2 * S).rearrange("p (b s) -> p b s", b=2)
        y = take(TT * 768).rearrange("p (t c) -> p t c", t=TT)
        yT = take(KC * S).rearrange("p (k s) -> p k s", k=KC)
        ln_gb = take(2 * D).rearrange("p (j d) -> p j d", j=2)
        z = take(TT * D).rearrange("p (t d) -> p t d", t=TT)
        tmp_a = take(512)
        tmp_b = take(512)
        tanh_buf = take(2 * 512).rearrange("p (j c) -> p j c", j=2)

        used["a"] = 0
        mod = take(6 * D).rearrange("p (m d) -> p m d", m=6)
        cmod = take(2 * D).rearrange("p (m d) -> p m d", m=2)
        hc_x = take(TT * D).rearrange("p (t d) -> p t d", t=TT)
        hl = take(TT * D).rearrange("p (t d) -> p t d", t=TT)
        gvec = take(D)
        mkT = take(MH * 512).rearrange("p (h s) -> p h s", h=MH)
        mv = take(4 * 512).rearrange("p (t c) -> p t c", t=4)
        akv = take(4 * 256).rearrange("p (t c) -> p t c", t=4)
        mqT = take(MH * S).rearrange("p (h s) -> p h s", h=MH)
        mo_t = take(TT * 512).rearrange("p (t c) -> p t c", t=TT)
        aq = take(TT * 512).rearrange("p (t c) -> p t c", t=TT)
        aqT = take(4 * S).rearrange("p (r s) -> p r s", r=4)
        akT = take(512)
        probs2 = take(3 * 512).rearrange("p (j c) -> p j c", j=3)
        probs2T = take(2 * 512).rearrange("p (j c) -> p j c", j=2)
        a_lat = take(TT * 512).rearrange("p (t c) -> p t c", t=TT)
        rt_a = take(512)
        rt_b = take(512)
        norm_g = take(512)
        m_lat = aqT.rearrange("p r s -> p (r s)").rearrange("p (t c) -> p t c", t=TT)
        at = 8 * D
        rows = [arena[0:8, at + j * 512:at + (j + 1) * 512] for j in range(8)]
        dw = arena[:, 6 * D:8 * D].rearrange("p (j c) -> p j c", j=4)
        mT = mkT[:, 0:2, :].rearrange("p a (b s) -> p (a b) s", b=2)
        aT = mkT[:, 2:4, :].rearrange("p a (b s) -> p (a b) s", b=2)
        mrg = mv.rearrange("p (t k) c -> p t (k c)", t=TT)
        mrgT = arena[:, 10 * D:12 * D].rearrange("p (k s) -> p k s", k=KC)
        gate_t = probs2[:, 0:2, :]
        branch_u = probs2T

        used["a"] = 6 * D
        h2 = take(TT * D).rearrange("p (t d) -> p t d", t=TT)
        pqT = take(16 * S).rearrange("p (l s) -> p l s", l=16)
        score = take(TT * 16 * NKEY).rearrange("p (t l n) -> p t l n", t=TT, l=16)
        head_s = take(2 * NKEY)
        cand = take(TOPK * TOPK)
        hot = take(TOPK * TOPK)
        work = take(TOPK * TOPK)
        tops = take(2 * TOPK)
        topi = take(2 * TOPK).bitcast(U32)
        topf = take(2 * TOPK)
        best = take(TOPK)
        bexp = take(TOPK)
        bpos = take(TOPK).bitcast(U32)
        bhl = take(2 * TOPK).bitcast(U32)
        fhl = take(2 * TOPK)
        sel1 = take(TOPK)
        sel2 = take(TOPK)
        esum = take(4)
        idx_next = take(2 * TOPK).bitcast(I32)
        gate_next = take(2 * TOPK)
        idx_u = take(2 * TOPK).bitcast(I32)
        idx_v = take(2 * TOPK).bitcast(I32)
        dots = take(2 * TOPK)
        d_a = take(TOPK)
        d_b = take(TOPK)
        wcur = take(2 * TOPK)
        diag = take(4 * P).rearrange("p (j c) -> p j c", j=4)
        u_ring = wring[:, 0:RING * D].rearrange("p (r d) -> p r d", r=RING)
        v_ring = ([wring[:, (RING + r) * D:(RING + r + 1) * D] for r in range(4)]
                  + [arena[:, r * D:(r + 1) * D] for r in range(4)])

        neg_max = take_small(4 * 2).rearrange("p (j b) -> p j b", j=4)
        sums = take_small(TT * 24).rearrange("p (t h b) -> p t h b", t=TT, h=8)
        gates3 = take_small(TT * 24).rearrange("p (t h b) -> p t h b", t=TT, h=8)
        coef = take_small(6)
        cmax = take_small(8)
        sp4 = take_small(DEPTH * 2)
        hbias = take_small(DEPTH * 4)
        stat = take_small(16)
        stat2 = take_small(16)
        var = take_small(16)
        rstd = take_small(16)
        bn = take_small(12).rearrange("p (j c) -> p j c", j=2)
        mvar = take_small(2)
        half8 = const[:, C_NEGHALF:C_NEGHALF + 8]
        cond_t = take_small(KC * 2).rearrange("p (k j) -> p k j", j=2)
        cond = take_small(KC * 2).rearrange("p (k j) -> p k j", j=2)
        sink = take_small(8)
        negsink = take_small(8)
        qk_g = take_small(2 * HD).rearrange("p (j d) -> p j d", j=2)
        nmA = take_small(TT * 8).rearrange("p (t h) -> p t h", t=TT)
        den = take_small(TT * 8).rearrange("p (t h) -> p t h", t=TT)
        es = take_small(8)
        fcol = take_small(2 * TT * 8).rearrange("p (d t c) -> p d t c", d=2, t=TT)
        mu = take_small(4)
        negmu = take_small(4)
        flo_in = take_small(4)
        flo_e = take_small(4)
        mden = take_small(4)
        mabs = take_small(4)
        mrec = take_small(4)
        wg2 = take_small(KC * 16).rearrange("p (k c) -> p k c", k=KC)
        lam_a = take_small(4)
        lam_b = take_small(4)
        lam_c = take_small(4)
        lam_d = take_small(4)
        lam_e = take_small(4)
        lam_f = take_small(4)
        sumsq = take_small(8)
        rsum = take_small(8)

        jobs = {}
        count = {"rot": 0, "acc": 0}
        chunk_last = {}

        class Done:
            def __init__(self, bank, nth):
                self.bank, self.nth = bank, nth

        def full(eng, name):
            j = jobs[name]
            eng.wait_ge(bank_full[j.bank], j.nth + 1)
            return psum[j.bank]

        def free(ins, name):
            ins.then_inc(bank_free[jobs[name].bank], 1)

        def taken(eng, name):
            j = jobs[name]
            eng.wait_ge(bank_free[j.bank], j.nth + 1)

        chunks = []
        for layer in range(DEPTH):
            chunks += [("w1", layer, c) for c in (0, 1, 2, 3, 4, 5, 6)]
            chunks += [("cmp", layer, 0), ("wo", layer, 0), ("wo", layer, 1)]
        chunks += [("ada", 0, c) for c in range(12)]
        chunks += [("w2", 0, c) for c in range(6)]
        chunks += [("br", 0, 0), ("w2", 0, 6), ("w2", 0, 7), ("br", 0, 1), ("w2", 0, 8), ("w2", 0, 9)]
        chunks += [("wo2", 0, 0), ("wo2", 0, 1)]
        chunks += [("pq", 0, c) for c in range(4)] + [("sk", 0, 0)]
        place = {c: (n % NW, n // NW) for n, c in enumerate(chunks)}
        w_full = [sem(f"w_full{s}") for s in range(NW)]

        def width(chunk):
            if chunk[0] == "w1" and chunk[2] == 4:
                return KC * 280
            if chunk[0] == "w2" and chunk[2] == 2:
                return KC * 256
            if chunk[0] == "sk":
                return 16 * NKEY
            return SLOT

        def slot(chunk):
            s = place[chunk][0]
            return wring[:, s * SLOT:s * SLOT + width(chunk)]

        block = ctx.enter_context(nc.Block())
        items = [(t, h) for t in range(TT) for h in range(8)]
        mitems = [(h, t) for h in range(MH) for t in range(TT)]

        @block.tensor
        def _(pe):
            def job(name, kind="rot"):
                n = count[kind]
                count[kind] += 1
                bank, nth = (n % NBANK, n // NBANK) if kind == "rot" else (NBANK + n % NACC, n // NACC)
                jobs[name] = Done(bank, nth)
                if nth:
                    pe.wait_ge(bank_free[bank], nth)
                return psum[bank]

            def finish(ins, name):
                ins.then_inc(bank_full[jobs[name].bank], 1)

            def weights(chunk):
                s, nth = place[chunk]
                pe.wait_ge(w_full[s], 16 * (nth + 1))
                return slot(chunk)

            def w_used(chunk, name):
                chunk_last[chunk] = name

            def project(name, lhs, w, cols):
                bank = job(name)
                n = len(lhs)
                for k in range(n):
                    ins = pe.matmul(bank[:, 0:cols], lhs[k], w[:, k, 0:cols], start=(k == 0), stop=(k == n - 1))
                finish(ins, name)

            def project_t(bank, at, w, col, rhs, n_tok):
                for k in range(KC):
                    ins = pe.matmul(bank[:, at:at + n_tok], w[:, k, col:col + P], rhs[:, k, :],
                                    start=(k == 0), stop=(k == KC - 1))
                return ins

            def transposes(name, blocks):
                bank = job(name)
                for j, blk in enumerate(blocks):
                    rows_in = blk.ap[0][1]
                    cols = blk.ap[-1][1]
                    ins = pe.transpose(bank[0:cols, j * P:j * P + rows_in], blk, ident[0:rows_in, 0:rows_in])
                finish(ins, name)

            pe.wait_ge(sem("in_const"), 32)
            for layer in range(DEPTH):
                L = layer
                for t in range(TT):
                    if layer == 0:
                        if t == 0:
                            pe.wait_ge(sem("in_x"), 16)
                    else:
                        pe.wait_ge(sem("x_next"), TT * (layer - 1) + t + 1)
                    for half in range(2):
                        transposes(("xT", L, t, half),
                                   [x3[:, t, (4 * half + j) * P:(4 * half + j + 1) * P] for j in range(4)])
                for t in range(TT):
                    for half in range(2):
                        taken(pe, ("xT", L, t, half))
                w = weights(("w1", L, 0)).rearrange("p (k c) -> p k c", k=KC)
                for n, name in enumerate(("lx", "lg")):
                    bank = job((name, L))
                    for b in range(2):
                        ins = project_t(bank, b * S, w, (2 * n + b) * P, xT, S)
                    finish(ins, (name, L))
                w_used(("w1", L, 0), ("lg", L))
                w = weights(("w1", L, 1)).rearrange("p (k c) -> p k c", k=KC)
                for t in range(TT):
                    project(("rqk", L, t), [xT[:, k, t * P:(t + 1) * P] for k in range(KC)], w, 512)
                w_used(("w1", L, 1), ("rqk", L, 1))
                w = weights(("w1", L, 2)).rearrange("p (k c) -> p k c", k=KC)
                for j in range(2):
                    bank = job(("q", L, j))
                    for b in range(2):
                        ins = project_t(bank, b * S, w, (2 * j + b) * P, xT, S)
                    finish(ins, ("q", L, j))
                w_used(("w1", L, 2), ("q", L, 1))
                w = weights(("w1", L, 3)).rearrange("p (k c) -> p k c", k=KC)
                for j, name in enumerate(("kcvc", "kskw")):
                    bank = job((name, L))
                    for b in range(2):
                        ins = project_t(bank, b * S, w, (2 * j + b) * P, xT, S)
                    finish(ins, (name, L))
                w_used(("w1", L, 3), ("kskw", L))
                pe.wait_ge(sem("conv"), L + 1)
                for n, name in enumerate(("lr", "li")):
                    bank = job((name, L))
                    for b in range(2):
                        for s in range(2):
                            r = slice(s * HD, (s + 1) * HD)
                            at = V_WG + ((L * 2 + n) * 2 + b) * HD
                            ins = pe.matmul(bank[r, b * S:(b + 1) * S], par[r, at:at + HD], conv[r, b, :],
                                            start=True, stop=True)
                    finish(ins, (name, L))
                for c, name, cols in ((4, "vg", 280), (5, "rvg", 512), (6, "ng", 512)):
                    w = weights(("w1", L, c)).rearrange("p (k c) -> p k c", k=KC)
                    for t in range(TT):
                        project((name, L, t), [xT[:, k, t * P:(t + 1) * P] for k in range(KC)], w, cols)
                    w_used(("w1", L, c), (name, L, 1))
                for t in range(TT):
                    pe.wait_ge(sem("rot"), TT * L + t + 1)
                    transposes(("rT", L, t), [rot[:, t, j * P:(j + 1) * P] for j in range(4)])
                w = weights(("cmp", L, 0)).rearrange("p (b l e) -> p b l e", b=2, l=CMP_L)
                taken(pe, ("kcvc", L))
                bank = job(("kc", L))
                for g in range(2):
                    r = slice(g * HD, (g + 1) * HD)
                    for l in range(CMP_L):
                        ins = pe.matmul(bank[r, 0:CMP_N], w[r, 0, l, :], blocksT[r, 0, l, :],
                                        start=(l == 0), stop=(l == CMP_L - 1))
                finish(ins, ("kc", L))
                for g in range(2):
                    bank = job(("vc", L, g))
                    r = slice(g * HD, (g + 1) * HD)
                    for l in range(CMP_L):
                        ins = pe.matmul(bank[0:CMP_N, 0:HD], blocksT[r, 1, l, :], w[r, 1, l, :],
                                        start=(l == 0), stop=(l == CMP_L - 1))
                    finish(ins, ("vc", L, g))
                w_used(("cmp", L, 0), ("vc", L, 1))
                for t in range(TT):
                    taken(pe, ("rT", L, t))
                for j, (s, t) in enumerate(((0, 0), (0, 1), (1, 1))):
                    for odd in range(2):
                        bank = job(("rs", L, j, odd))
                        r = slice(odd * HD, (odd + 1) * HD)
                        for n in range(2):
                            ins = pe.matmul(bank[:, n * P:(n + 1) * P], retT[r, 2 + n, s * P:(s + 1) * P],
                                            retT[r, n, t * P:(t + 1) * P], start=True, stop=True)
                        finish(ins, ("rs", L, j, odd))
                taken(pe, ("kc", L))
                for j in range(2):
                    taken(pe, ("q", L, j))
                for t in range(TT):
                    for g in range(2):
                        bank = job(("nc", L, t, g))
                        r = slice(g * HD, (g + 1) * HD)
                        for h in range(4):
                            ins = pe.matmul(bank[:, h * CMP_N:(h + 1) * CMP_N], qT[r, h, t * P:(t + 1) * P],
                                            kcT[r, :], start=True, stop=True)
                        finish(ins, ("nc", L, t, g))
                for j in range(3):
                    for odd in range(2):
                        taken(pe, ("rs", L, j, odd))
                for t in range(TT):
                    taken(pe, ("rvg", L, t))
                    bank = job(("ro", L, t))
                    keys = ((0, 0),) if t == 0 else ((0, 1), (1, 2))
                    for h in range(4):
                        for n, (s, j) in enumerate(keys):
                            ins = pe.matmul(bank[:, h * HD:(h + 1) * HD], ret_s[:, j, h * P:(h + 1) * P],
                                            ret_v[:, s, h * HD:(h + 1) * HD],
                                            start=(n == 0), stop=(n == len(keys) - 1))
                    finish(ins, ("ro", L, t))
                for t in range(TT):
                    pe.wait_ge(sem("cmp_probs"), TT * L + t + 1)
                    for half in range(2):
                        bank = job(("cT", L, t, half))
                        for j in range(4):
                            ins = pe.transpose(bank[0:CMP_N, j * P:(j + 1) * P], cmp_s[:, t, 4 * half + j, :], ident)
                        finish(ins, ("cT", L, t, half))
                taken(pe, ("kskw", L))
                for g in range(2):
                    taken(pe, ("vc", L, g))
                for t in range(TT):
                    taken(pe, ("vg", L, t))
                    for half in range(2):
                        taken(pe, ("cT", L, t, half))

                def nsa_scores(i):
                    t, h = items[i]
                    nk = (t + 1) * P
                    r = slice((h // 4) * HD, (h // 4 + 1) * HD)
                    bank = job(("ns", L, i))
                    ins = pe.matmul(bank[:, 0:2 * nk].rearrange("p (b k) -> p b k", b=2),
                                    qT[r, h % 4, t * P:(t + 1) * P], kT[r, :, 0:nk], start=True, stop=True)
                    finish(ins, ("ns", L, i))

                def nsa_transposes(i):
                    t, h = items[i]
                    taken(pe, ("ns", L, i))
                    transposes(("nT", L, i), [probs[:, i % 3, j * P:(j + 1) * P] for j in range(2 * (t + 1))])

                def nsa_values(i):
                    t, h = items[i]
                    g = slice((h // 4) * HD, (h // 4 + 1) * HD)
                    if h % 2 == 0:
                        job(("no", L, i // 2), "acc")
                    bank = psum[jobs[("no", L, i // 2)].bank]
                    taken(pe, ("nT", L, i))
                    at = (h % 2) * 3 * HD
                    pe.matmul(bank[:, at:at + HD], cmpT[0:CMP_N, t, h, :], vc[0:CMP_N, g], start=True, stop=True)
                    for b in range(2):
                        for s in range(t + 1):
                            blk = b * (t + 1) + s
                            ins = pe.matmul(bank[:, at + (b + 1) * HD:at + (b + 2) * HD],
                                            probsT[:, i % 2, blk * P:(blk + 1) * P],
                                            nsa_v[:, s, b * P + g.start:b * P + g.stop],
                                            start=(s == 0), stop=(s == t))
                    if h % 2:
                        finish(ins, ("no", L, i // 2))

                nsa_scores(0)
                nsa_scores(1)
                for i in range(len(items)):
                    if i + 2 < len(items):
                        nsa_scores(i + 2)
                    nsa_transposes(i)
                    if i:
                        nsa_values(i - 1)
                nsa_values(len(items) - 1)
                for t in range(TT):
                    pe.wait_ge(sem("y_ret"), TT * L + t + 1)
                    transposes(("yT", L, t, 0), [y[:, t, j * P:(j + 1) * P] for j in range(2)])
                    pe.wait_ge(sem("y_nsa"), TT * L + t + 1)
                    transposes(("yT", L, t, 1), [y[:, t, (2 + j) * P:(3 + j) * P] for j in range(4)])
                pe.wait_ge(sem("y_lru"), L + 1)
                for t in range(TT):
                    for half in range(2):
                        taken(pe, ("yT", L, t, half))
                for half in range(2):
                    w = weights(("wo", L, half)).rearrange("p (k c) -> p k c", k=KC)
                    for t in range(TT):
                        project(("wo", L, t, half), [yT[:, k, t * P:(t + 1) * P] for k in range(KC)], w, 512)
                    w_used(("wo", L, half), ("wo", L, 1, half))

            pe.wait_ge(sem("cond"), 1)
            for c in range(12):
                w = weights(("ada", 0, c)).rearrange("p (k c) -> p k c", k=KC)
                for j in range(2 if c < 4 else 1):
                    project(("ada", c, j), [cond[:, k, j:j + 1].to_broadcast([P, P]) for k in range(KC)], w, 512)
                w_used(("ada", 0, c), ("ada", c, 1 if c < 4 else 0))
            for tt in range(4):
                src = hc_x[:, tt, :] if tt < 2 else hl[:, tt - 2, :]
                pe.wait_ge(sem("h_rows"), tt + 1)
                for half in range(2):
                    transposes(("hT", tt, half), [src[:, (4 * half + j) * P:(4 * half + j + 1) * P] for j in range(4)])
            for tt in range(4):
                for half in range(2):
                    taken(pe, ("hT", tt, half))
            for n, name in enumerate(("gi", "gf")):
                bank = job((name,))
                for k in range(KC):
                    ins = pe.matmul(bank[0:8, :], wg2[:, k, n * 8:(n + 1) * 8], hT[:, k, :],
                                    start=(k == 0), stop=(k == KC - 1))
                finish(ins, (name,))
            w = weights(("w2", 0, 0)).rearrange("p (k c) -> p k c", k=KC)
            for h in range(MH):
                bank = job(("mk", h))
                finish(project_t(bank, 0, w, h * P, hT, 512), ("mk", h))
            w_used(("w2", 0, 0), ("mk", MH - 1))
            w = weights(("w2", 0, 1)).rearrange("p (k c) -> p k c", k=KC)
            for tt in range(4):
                project(("mv", tt), [hT[:, k, tt * P:(tt + 1) * P] for k in range(KC)], w, 512)
            w_used(("w2", 0, 1), ("mv", 3))
            w = weights(("w2", 0, 2)).rearrange("p (k c) -> p k c", k=KC)
            for tt in range(4):
                project(("akv", tt), [hT[:, k, tt * P:(tt + 1) * P] for k in range(KC)], w, 256)
            w_used(("w2", 0, 2), ("akv", 3))
            hlT = hT[:, :, S:2 * S]
            w = weights(("w2", 0, 3)).rearrange("p (k c) -> p k c", k=KC)
            for j in range(2):
                bank = job(("mq", j))
                for b in range(2):
                    ins = project_t(bank, b * S, w, (2 * j + b) * P, hlT, S)
                finish(ins, ("mq", j))
            w_used(("w2", 0, 3), ("mq", 1))
            for c, name in ((4, "aq"), (5, "mog")):
                w = weights(("w2", 0, c)).rearrange("p (k c) -> p k c", k=KC)
                for t in range(TT):
                    project((name, t), [hlT[:, k, t * P:(t + 1) * P] for k in range(KC)], w, 512)
                w_used(("w2", 0, c), (name, 1))
            pe.wait_ge(sem("ak"), 1)
            transposes(("akT",), [akv[:, tt, 0:P] for tt in range(4)])
            for t in range(TT):
                pe.wait_ge(sem("aq"), t + 1)
                transposes(("aqT", t), [aq[:, t, j * P:(j + 1) * P] for j in range(4)])
            pe.wait_ge(sem("gate_rows"), 1)
            bank = job(("fc",))
            for d in range(2):
                for t in range(TT):
                    at = (d * TT + t) * 8
                    ins = pe.transpose(bank[:, at:at + 8], rows[3 + d][:, S + t * P:S + (t + 1) * P], ident[0:8, 0:8])
            finish(ins, ("fc",))
            taken(pe, ("akT",))
            taken(pe, ("aqT", 0))
            taken(pe, ("aqT", 1))

            def attn_scores(i):
                t, h = items[i]
                r = slice((h // 4) * HD, (h // 4 + 1) * HD)
                bank = job(("as", i))
                finish(pe.matmul(bank[:, :], aqT[r, h % 4, t * P:(t + 1) * P], akT[r, :], start=True, stop=True),
                       ("as", i))

            def attn_values(i):
                t, h = items[i]
                if h == 0:
                    job(("ao", t), "acc")
                bank = psum[jobs[("ao", t)].bank]
                taken(pe, ("aT_", i))
                for s in range(4):
                    at = P + (h // 4) * HD
                    ins = pe.matmul(bank[:, h * HD:(h + 1) * HD], probs2T[:, i % 2, s * P:(s + 1) * P],
                                    akv[:, s, at:at + HD], start=(s == 0), stop=(s == 3))
                if h == 7:
                    finish(ins, ("ao", t))

            attn_scores(0)
            attn_scores(1)
            for i in range(len(items)):
                if i + 2 < len(items):
                    attn_scores(i + 2)
                taken(pe, ("as", i))
                transposes(("aT_", i), [probs2[:, i % 3, j * P:(j + 1) * P] for j in range(4)])
                if i:
                    attn_values(i - 1)
            attn_values(len(items) - 1)

            for h in range(MH):
                taken(pe, ("mk", h))
                taken(pe, ("mv", h))
            for j in range(2):
                taken(pe, ("mq", j))

            def key_rows(h):
                for d in range(2):
                    c = d * 4 + h
                    bank = job(("G", d, h))
                    finish(pe.matmul(bank[:, :], ident[0:8, c:c + 1].to_broadcast([8, P]), rows[5 + d],
                                     start=True, stop=True), ("G", d, h))

            def mlstm_scores(h):
                for t in range(TT):
                    bank = job(("qk", h, t))
                    finish(pe.matmul(bank[:, :], mqT[:, h, t * P:(t + 1) * P], mkT[:, h, :], start=True, stop=True),
                           ("qk", h, t))

            def mlstm_values(i):
                h, t = mitems[i]
                pe.wait_ge(sem("mlstm_s"), i + 1)
                transposes(("mT_", i), [probs2[:, i % 2, j * P:(j + 1) * P] for j in range(4)])
                if h == 0:
                    job(("mo", t), "acc")
                bank = psum[jobs[("mo", t)].bank]
                taken(pe, ("mT_", i))
                for s in range(4):
                    ins = pe.matmul(bank[:, h * P:(h + 1) * P], probs2T[:, i % 2, s * P:(s + 1) * P],
                                    mv[:, s, h * P:(h + 1) * P], start=(s == 0), stop=(s == 3))
                if h == MH - 1:
                    finish(ins, ("mo", t))

            key_rows(0)
            mlstm_scores(0)
            for h in range(MH):
                if h + 1 < MH:
                    key_rows(h + 1)
                for t in range(TT):
                    mlstm_values(TT * h + t)
                if h + 1 < MH:
                    mlstm_scores(h + 1)
            for t in range(TT):
                taken(pe, ("ao", t))
                transposes(("aT", t), [a_lat[:, t, j * P:(j + 1) * P] for j in range(4)])
            for t in range(TT):
                pe.wait_ge(sem("m_lat"), t + 1)
                transposes(("mT", t), [m_lat[:, t, j * P:(j + 1) * P] for j in range(4)])
            for t in range(TT):
                taken(pe, ("aT", t))
                taken(pe, ("mT", t))
            for half in range(2):
                wb = weights(("br", 0, half)).rearrange("p (k c) -> p k c", k=KC)
                for n, (g, src) in enumerate((("gm", mT), ("ga", aT))):
                    chunk = ("w2", 0, 6 + 2 * half + n)
                    w = weights(chunk).rearrange("p (k c) -> p k c", k=KC)
                    for t in range(TT):
                        project((g, half, t), [hlT[:, k, t * P:(t + 1) * P] for k in range(KC)], w, 512)
                        project(("b" + g, half, t), [src[:, k, t * P:(t + 1) * P] for k in range(4)],
                                wb[:, 4 * n:4 * n + 4, :], 512)
                    w_used(chunk, (g, half, 1))
                w_used(("br", 0, half), ("bga", half, 1))
            for t in range(TT):
                for half in range(2):
                    pe.wait_ge(sem("mrg"), half * TT + t + 1)
                    transposes(("gT", t, half), [mrg[:, t, (4 * half + j) * P:(4 * half + j + 1) * P] for j in range(4)])
            for t in range(TT):
                for half in range(2):
                    taken(pe, ("gT", t, half))
            for half in range(2):
                w = weights(("wo2", 0, half)).rearrange("p (k c) -> p k c", k=KC)
                for t in range(TT):
                    project(("wo2", half, t), [mrgT[:, k, t * P:(t + 1) * P] for k in range(KC)], w, 512)
                w_used(("wo2", 0, half), ("wo2", half, 1))
            for t in range(TT):
                pe.wait_ge(sem("h2"), t + 1)
                for half in range(2):
                    transposes(("pT", t, half), [h2[:, t, (4 * half + j) * P:(4 * half + j + 1) * P] for j in range(4)])
            for t in range(TT):
                for half in range(2):
                    taken(pe, ("pT", t, half))
            for c in range(4):
                w = weights(("pq", 0, c)).rearrange("p (k c) -> p k c", k=KC)
                for j in range(2):
                    bank = job(("pq", 2 * c + j))
                    for b in range(2):
                        ins = project_t(bank, b * S, w, (2 * j + b) * P, xT, S)
                    finish(ins, ("pq", 2 * c + j))
                w_used(("pq", 0, c), ("pq", 2 * c + 1))
            w = weights(("sk", 0, 0)).rearrange("p (l n) -> p l n", l=16)
            for j in range(8):
                taken(pe, ("pq", j))
            for t in range(TT):
                for j in range(4):
                    bank = job(("ps", t, j))
                    for b in range(4):
                        ins = pe.matmul(bank[:, b * P:(b + 1) * P], pqT[:, 4 * j + b, t * P:(t + 1) * P],
                                        w[:, 4 * j + b, :], start=True, stop=True)
                    finish(ins, ("ps", t, j))
            w_used(("sk", 0, 0), ("ps", 1, 3))
            for t in range(TT):
                sums_of = [job(("pv", t, half)) for half in range(2)]
                for half in range(2):
                    pe.matmul(sums_of[half][:, :], const[0:1, C_ZERO:C_ZERO + P], h2[0:1, t, half * 512:(half + 1) * 512],
                              start=True, stop=False)
                with pe.Fori(0, EH // 2) as it:
                    for n in range(2 * TOPK):
                        at = t * EH * TOPK + n
                        pe.wait_ge(sem(f"v_full{n % RING}"), it * (16 * 2 * TOPK // RING) + 16 * (at // RING + 1))
                        pe.wait_ge(sem("diag_ready"), it * (2 * TOPK) + (CREDIT + at + 1))
                        for half in range(2):
                            ins = pe.matmul(sums_of[half][:, :], diag[:, n % 4, :], v_ring[n % RING][:, half * 512:(half + 1) * 512],
                                            start=False, stop=False, skip_group_check=True)
                        ins.then_inc(sem("v_used"), 1)
                for half in range(2):
                    finish(pe.matmul(sums_of[half][:, :], const[0:1, C_ZERO:C_ZERO + P], h2[0:1, t, half * 512:(half + 1) * 512],
                                     start=False, stop=True), ("pv", t, half))

        @block.sync
        def _(sp):
            sp.dma_start(x3, a["x"].rearrange("(t p) d -> p t d", p=P)).then_inc(sem("in_x"), 16)
            sp.dma_start(const[:, :], a["const"]).then_inc(sem("in_const"), 16)
            sp.dma_start(par[:, :], a["par"]).then_inc(sem("in_const"), 16)
            sp.dma_start(wg2, a["wg2"]).then_inc(sem("in_small"), 16)
            sp.dma_start(sink, a["sink"].to_broadcast([P, 8])).then_inc(sem("in_small"), 16)
            sp.dma_start(qk_g[:, 0, :], a["q_g"].to_broadcast([P, HD])).then_inc(sem("in_small"), 16)
            sp.dma_start(qk_g[:, 1, :], a["k_g"].to_broadcast([P, HD])).then_inc(sem("in_small"), 16)
            for chunk in chunks:
                s, nth = place[chunk]
                if nth:
                    full(sp, chunk_last[chunks[chunks.index(chunk) - NW]])
                kind, L, c = chunk
                dst = slot(chunk)
                src = {"cmp": lambda: a["cmp"][L], "w1": lambda: a["w1b"][L] if c == 4 else a["w1"][L, c if c < 4 else c - 1],
                       "wo": lambda: a["wo"][L, c], "ada": lambda: a["ada"][c],
                       "w2": lambda: a["w2b"] if c == 2 else a["w2"][c if c < 2 else c - 1],
                       "br": lambda: a["br"][c], "wo2": lambda: a["wo2"][c], "pq": lambda: a["pq"][c],
                       "sk": lambda: a["sk"]}[kind]()
                sp.dma_start(dst, src).then_inc(w_full[s], 16)
                if kind == "w1" and c == (3 if L else 0):
                    if L:
                        sp.wait_ge(sem("x_next"), TT * L)
                    for j, name in enumerate(("ln_g", "ln_b")):
                        sp.dma_start(ln_gb[:, j, :], a[name][L:L + 1, :].to_broadcast([P, D])).then_inc(sem("in_ln"), 16)
                if chunk == ("ada", 0, 2):
                    sp.wait_ge(sem("x_next"), TT * DEPTH)
                    sp.dma_start(cmod.rearrange("p m d -> p (m d)"), a["b_ada"][:, 0:2 * D].to_broadcast([P, 2 * D])).then_inc(sem("in_mod"), 16)
                    sp.dma_start(mod.rearrange("p m d -> p (m d)"), a["b_ada"].to_broadcast([P, 6 * D])).then_inc(sem("in_mod"), 16)
                    sp.dma_start(gvec, a["g_mix"].to_broadcast([P, D])).then_inc(sem("in_gmix"), 16)
                    sp.dma_start(hc_x, a["ctx"].rearrange("(t p) d -> p t d", p=P)).then_inc(sem("in_ctx"), 16)
                    sp.dma_start(norm_g, a["norm_g"].to_broadcast([P, 512])).then_inc(sem("in_ctx"), 16)
                if chunk == ("w2", 0, 0):
                    sp.wait_ge(sem("sc_mix"), 2)
                    sp.dma_start(gvec, a["g_ffn"].to_broadcast([P, D])).then_inc(sem("in_gffn"), 16)
            for t in range(TT):
                sp.wait_ge(sem("result"), t + 1)
                sp.dma_start(out[t * P:(t + 1) * P, :], x3[:, t, :]).then_inc(sem("stored"), 16)
            sp.wait_ge(sem("stored"), 16 * TT)

        @block.scalar
        def _(act):
            def link(ins, name, counts={}):
                counts[name] = counts.get(name, 0) + 1
                ins.then_inc(sem(name), 1)
                act.wait_ge(sem(name), counts[name])

            def copy(dst, src, scale=1.0):
                return act.activation(dst, src, ACT.Copy, scale=scale)

            act.wait_ge(sem("lam_abs"), 1)
            act.activation(lam_c, lam_b, ACT.Exp, scale=-1.0).then_inc(sem("lam_exp"), 1)
            act.wait_ge(sem("in_const"), 32)
            act.activation(cond_t.rearrange("p k j -> p (k j)"), par[:, V_COND:V_COND + 2 * KC], ACT.Tanh,
                           scale=0.5).then_inc(sem("cond_tanh"), 1)
            for L in range(DEPTH):
                for t in range(TT):
                    bank = full(act, ("xT", L, t, 0))
                    free(copy(xT[:, 0:4, t * P:(t + 1) * P], bank[:, :].rearrange("p (j s) -> p j s", j=4)), ("xT", L, t, 0))
                if L == 0:
                    act.wait_ge(sem("lru_pad"), 1)
                bank = full(act, ("lx", L))
                free(copy(lru_x[:, :, 3:3 + S], bank[:, :].rearrange("p (b s) -> p b s", b=2)), ("lx", L))
                bank = full(act, ("lg", L))
                act.activation(tanh_buf[:, 0, :], bank[:, :], ACT.Tanh, scale=0.5).then_inc(sem("lg_tanh"), 1)
                for j in range(2):
                    bank = full(act, ("q", L, j))
                    free(copy(qT[:, 2 * j:2 * j + 2, :], bank[:, :].rearrange("p (b s) -> p b s", b=2), HD ** -0.5), ("q", L, j))
                bank = full(act, ("kskw", L))
                free(copy(kT, bank[:, :].rearrange("p (b s) -> p b s", b=2)), ("kskw", L))
                for name, dst, col in (("lr", lru_r, 0), ("li", lru_i, 2)):
                    bank = full(act, (name, L))
                    for b in range(2):
                        ins = act.activation(dst[:, b, :], bank[:, b * S:(b + 1) * S], ACT.Tanh, scale=0.5,
                                             bias=hbias[:, L * 4 + col + b:L * 4 + col + b + 1])
                    free(ins, (name, L))
                for t in range(TT):
                    bank = full(act, ("vg", L, t))
                    copy(nsa_v[:, t, :], bank[:, 0:256])
                    free(act.activation(nsa_gt[:, t, :], bank[:, 256:280], ACT.Tanh, scale=0.5), ("vg", L, t))
                act.wait_ge(sem("lru_la"), L + 1)
                act.activation(lru_a, lru_r, ACT.Exp).then_inc(sem("lru_a"), 1)
                act.activation(lru_t, lru_r, ACT.Tanh).then_inc(sem("lru_a"), 1)
                for t in range(TT):
                    bank = full(act, ("rvg", L, t))
                    copy(ret_v[:, t, :], bank[:, 0:S])
                    if t:
                        taken(act, ("lg", L))
                    act.activation(tanh_buf[:, 1 - t, 0:S], bank[:, S:2 * S], ACT.Tanh, scale=0.5).then_inc(sem("rg_tanh"), 1)
                for t in range(TT):
                    bank = full(act, ("ng", L, t))
                    taken(act, ("rvg", L, t))
                    act.activation(tanh_buf[:, 1 - t, :], bank[:, :], ACT.Tanh, scale=0.5).then_inc(sem("ng_tanh"), 1)
                for t in range(TT):
                    bank = full(act, ("rT", L, t))
                    free(copy(retT[:, :, t * P:(t + 1) * P], bank[:, :].rearrange("p (j s) -> p j s", j=4)), ("rT", L, t))
                act.wait_ge(sem("lru_v"), L + 1)
                act.activation(lru_t, lru_t, ACT.Sqrt).then_inc(sem("lru_sq"), 1)
                bank = full(act, ("kc", L))
                free(copy(kcT, bank[:, 0:CMP_N]), ("kc", L))
                for g in range(2):
                    bank = full(act, ("vc", L, g))
                    free(copy(vc[0:CMP_N, g * HD:(g + 1) * HD], bank[0:CMP_N, 0:HD]), ("vc", L, g))
                for t in range(TT):
                    act.wait_ge(sem("cmp_sub"), TT * L + t + 1)
                    act.activation(cmp_s[:, t, :, :], cmp_s[:, t, :, :], ACT.Exp).then_inc(sem("cmp_probs"), 1)
                for t in range(TT):
                    for half in range(2):
                        bank = full(act, ("cT", L, t, half))
                        free(copy(cmpT[0:CMP_N, t, 4 * half:4 * half + 4, :],
                                  bank[0:CMP_N, :].rearrange("p (j s) -> p j s", j=4)), ("cT", L, t, half))

                def exps(i):
                    t, h = items[i]
                    nk = (t + 1) * P
                    bank = full(act, ("ns", L, i))
                    act.wait_ge(sem("nsa_max"), 16 * L + i + 1)
                    for b in range(2):
                        ins = act.activation(probs[:, i % 3, b * nk:(b + 1) * nk], bank[:, b * nk:(b + 1) * nk],
                                             ACT.Exp, bias=neg_max[:, i % 4, b:b + 1],
                                             accum_out=sums[:, t, h, b + 1:b + 2])
                    free(ins, ("ns", L, i))

                exps(0)
                exps(1)
                for i in range(len(items)):
                    if i + 2 < len(items):
                        exps(i + 2)
                    if i % 2:
                        bank = full(act, ("nT", L, i))
                        n = 2 * (items[i][0] + 1) * P
                        free(copy(probsT[:, 1, 0:n], bank[:, 0:n]), ("nT", L, i))
                for t in range(TT):
                    for half, (k0, n) in enumerate(((0, 2), (2, 4))):
                        bank = full(act, ("yT", L, t, half))
                        free(copy(yT[:, k0:k0 + n, t * P:(t + 1) * P],
                                  bank[:, 0:n * P].rearrange("p (j s) -> p j s", j=n)), ("yT", L, t, half))

            for tt in range(4):
                src = hc_x[:, tt, :] if tt < 2 else x3[:, tt - 2, :]
                if tt == 0:
                    act.wait_ge(sem("in_ctx"), 32)
                if tt == 2:
                    act.wait_ge(sem("x_next"), TT * DEPTH)
                    act.wait_ge(sem("rms_sq"), 2)
                act.activation(hl[:, tt % 2, :], src, ACT.Square, accum_out=sumsq[:, tt:tt + 1]).then_inc(sem("rms_sq"), 1)
            for tt in range(4):
                bank = full(act, ("hT", tt, 0))
                free(copy(hT[:, 0:4, tt * P:(tt + 1) * P], bank[:, :].rearrange("p (j s) -> p j s", j=4)), ("hT", tt, 0))
            for n, name in enumerate(("gi", "gf")):
                bank = full(act, (name,))
                for tt in range(4):
                    taken(act, ("hT", tt, 1))
                free(act.activation(rows[n], bank[0:8, :], ACT.Identity, bias=par[0:8, V_MG + n:V_MG + n + 1]), (name,))
            taken(act, ("gf",))
            link(act.activation(rt_a[0:8, :], rows[1], ACT.Abs), "fgate_abs")
            act.activation(rt_a[0:8, :], rt_a[0:8, :], ACT.Exp, scale=-1.0).then_inc(sem("fgate_exp"), 1)
            for h in range(MH):
                bank = full(act, ("mk", h))
                free(copy(mkT[:, h, :], bank[:, :], K_SCALE), ("mk", h))
            for tt in range(4):
                bank = full(act, ("mv", tt))
                free(copy(mv[:, tt, :], bank[:, :]), ("mv", tt))
            for j in range(2):
                bank = full(act, ("mq", j))
                free(copy(mqT[:, 2 * j:2 * j + 2, :], bank[:, :].rearrange("p (b s) -> p b s", b=2)), ("mq", j))
            for t in range(TT):
                bank = full(act, ("mog", t))
                free(act.activation(mo_t[:, t, :], bank[:, :], ACT.Tanh, scale=0.5), ("mog", t))
            bank = full(act, ("akT",))
            free(copy(akT, bank[:, :]), ("akT",))
            for t in range(TT):
                bank = full(act, ("aqT", t))
                free(copy(aqT[:, :, t * P:(t + 1) * P], bank[:, :].rearrange("p (j s) -> p j s", j=4)), ("aqT", t))
            bank = full(act, ("fc",))
            free(copy(fcol.rearrange("p d t c -> p (d t c)"), bank[:, 0:2 * TT * 8]), ("fc",))

            def attn_exp(i):
                t, h = items[i]
                bank = full(act, ("as", i))
                act.wait_ge(sem("attn_max"), i + 1)
                free(act.activation(probs2[:, i % 3, :], bank[:, :], ACT.Exp, bias=nmA[:, t, h:h + 1],
                                    accum_out=den[:, t, h:h + 1]), ("as", i))

            attn_exp(0)
            attn_exp(1)
            for i in range(len(items)):
                if i + 2 < len(items):
                    attn_exp(i + 2)
                if i % 2:
                    bank = full(act, ("aT_", i))
                    free(copy(probs2T[:, 1, :], bank[:, :]), ("aT_", i))
                if i % 8 == 7:
                    t = i // 8
                    act.wait_ge(sem("sink_sub"), t + 1)
                    act.activation(es, es, ACT.Exp).then_inc(sem("sink_exp"), 1)
            for h in range(MH):
                act.wait_ge(sem("mlstm_mu"), h + 1)
                for j in range(4):
                    act.activation(dw[:, j, :], dw[:, j, :], ACT.Exp, bias=negmu[:, j:j + 1]).then_inc(sem("mlstm_w"), 1)
                act.activation(flo_e, flo_in, ACT.Exp).then_inc(sem("mlstm_w"), 1)
                for t in range(TT):
                    i = TT * h + t
                    bank = full(act, ("mT_", i))
                    free(copy(probs2T[:, i % 2, :], bank[:, :]), ("mT_", i))
            for t in range(TT):
                bank = full(act, ("mo", t))
                act.activation(dw[:, t, :], bank[:, :], ACT.Square).then_inc(sem("mlstm_sq"), 1)
            for name, dst in (("aT", aT), ("mT", mT)):
                for t in range(TT):
                    bank = full(act, (name, t))
                    free(copy(dst[:, :, t * P:(t + 1) * P], bank[:, :].rearrange("p (j s) -> p j s", j=4)), (name, t))
            for half in range(2):
                for n, g in enumerate(("gm", "ga")):
                    for t in range(TT):
                        i = half * 4 + n * 2 + t
                        bank = full(act, (g, half, t))
                        if i >= 2:
                            before = [("b" + g_, h_, t_) for h_ in range(2) for g_ in ("gm", "ga") for t_ in range(TT)]
                            taken(act, before[i - 2])
                        free(act.activation(gate_t[:, i % 2, :], bank[:, :], ACT.Tanh, scale=0.5), (g, half, t))
            for t in range(TT):
                bank = full(act, ("gT", t, 0))
                free(copy(mrgT[:, 0:4, t * P:(t + 1) * P], bank[:, :].rearrange("p (j s) -> p j s", j=4)), ("gT", t, 0))
            for t in range(TT):
                act.wait_ge(sem("x1"), t + 1)
                act.activation(h2[:, t, :], x3[:, t, :], ACT.Square, accum_out=sumsq[:, t:t + 1]).then_inc(sem("rms_sq"), 1)
            for t in range(TT):
                bank = full(act, ("pT", t, 0))
                free(copy(xT[:, 0:4, t * P:(t + 1) * P], bank[:, :].rearrange("p (j s) -> p j s", j=4)), ("pT", t, 0))
            for j in range(0, 8, 2):
                bank = full(act, ("pq", j))
                free(copy(pqT[:, 2 * j:2 * j + 2, :], bank[:, :].rearrange("p (b s) -> p b s", b=2)), ("pq", j))
            for t in range(TT):
                for j in range(4):
                    bank = full(act, ("ps", t, j))
                    free(copy(score[:, t, 4 * j:4 * j + 4, :], bank[:, :].rearrange("p (b n) -> p b n", b=4)), ("ps", t, j))
                    taken(act, ("ps", t, j))
                    act.sem_inc(sem("scores"), 1)
            act.sem_inc(sem("diag_ready"), CREDIT)
            for n in range(2):
                act.wait_ge(sem("top_sub"), n + 1)
                act.activation(bexp, best, ACT.Exp, bias=esum[:, 0:1], accum_out=esum[:, 1:2]).then_inc(sem("top_exp"), 1)

            def expert_head(it, head, more):
                s = head % 2
                act.wait_ge(sem("gelu_in"), it * 2 + (head + 1))
                act.activation(d_b, d_a, ACT.Tanh).then_inc(sem("gelu_tanh"), 1)
                if more:
                    act.wait_ge(sem("top_sub"), it * 2 + (head + 3))
                    act.activation(bexp, best, ACT.Exp, bias=esum[:, 0:1], accum_out=esum[:, 1:2]).then_inc(sem("top_exp"), 1)
                act.wait_ge(sem("w_ready"), it * 2 + (head + 1))
                for r in range(TOPK):
                    at = head * TOPK + r
                    act.wait_ge(sem("v_used"), it * (2 * TOPK) + (CREDIT + at + 1 - 4))
                    act.activation(diag[:, r % 4, :], ident, ACT.Copy, scale=wcur[:, s * TOPK + r:s * TOPK + r + 1]
                                   ).then_inc(sem("diag_ready"), 1)

            with act.Fori(0, TT * EH // 2 - 1) as it:
                for s in range(2):
                    expert_head(it, s, True)
            for s in range(2):
                expert_head(0, TT * EH - 2 + s, False)

        @block.vector
        def _(dve):
            counts = {}

            def link(ins, name="dve_step"):
                counts[name] = counts.get(name, 0) + 1
                ins.then_inc(sem(name), 1)
                dve.wait_ge(sem(name), counts[name])

            def tt(o, p, q, op):
                return dve.tensor_tensor(o, p, q, op)

            def ts(o, p, s1, op0, s2=None, op1=None):
                if op1 is None:
                    return dve.tensor_scalar(o, p, s1, None, op0)
                return dve.tensor_scalar(o, p, s1, s2, op0, op1)

            def stt(o, p, s, q, op0, op1):
                return dve.scalar_tensor_tensor(o, p, s, q, op0, op1)

            def inverse_root(cols):
                dve.sem_inc(sem("var_ready"), 1)
                counts["root"] = counts.get("root", 0) + 1
                dve.wait_ge(sem("root_done"), counts["root"])

            def log1p_half(e, s, s2, yv):
                link(ts(s, e, 2.0, ALU.add))
                link(dve.reciprocal(s, s))
                link(tt(s, e, s, ALU.mult))
                link(tt(s2, s, s, ALU.mult))
                link(ts(yv, s2, ATANH[-1], ALU.mult))
                for c in reversed(ATANH[:-1]):
                    link(stt(yv, yv, c, s2, ALU.add, ALU.mult))
                link(stt(yv, yv, 1.0, s, ALU.add, ALU.mult))

            link(dve.memset(lru_x[:, :, 0:3], 0.0), "lru_pad")
            dve.wait_ge(sem("in_const"), 32)
            lru_par = par[:, V_LRU:V_LRU + DEPTH * 16].rearrange("p (l c) -> p l c", l=DEPTH)
            lam = lru_par[:, :, 14:16]

            def lb(v):
                return v.rearrange("p (l b) -> p l b", l=DEPTH)

            link(ts(lb(lam_a), lam, -1.0, ALU.mult))
            link(tt(lb(lam_b), lb(lam_a), lam, ALU.max), "lam_abs")
            link(ts(hbias.rearrange("p (l b) -> p l b", l=DEPTH), lru_par[:, :, 10:14], 0.5, ALU.mult))
            dve.wait_ge(sem("lam_exp"), 1)
            log1p_half(lam_c, lam_d, lam_e, lam_f)
            link(ts(lam_a, lam_a, 0.0, ALU.max))
            link(stt(lam_a, lam_f, 2.0, lam_a, ALU.mult, ALU.add))
            link(ts(sp4, lam_a, -LRU_C / 2, ALU.mult))
            dve.wait_ge(sem("cond_tanh"), 1)
            link(stt(cond_t.rearrange("p k j -> p (k j)"), cond_t.rearrange("p k j -> p (k j)"), 1.0,
                     par[:, V_COND:V_COND + 2 * KC], ALU.add, ALU.mult))
            link(ts(cond.rearrange("p k j -> p (k j)"), cond_t.rearrange("p k j -> p (k j)"), 0.5, ALU.mult), "cond")

            def rope(dst, src, n, cos, sin, name):
                t1, t2 = rope_tmp
                v1 = t1[:, 0:n * HD].rearrange("p (n d) -> p n d", n=n)
                v2 = t2[:, 0:n * HD].rearrange("p (n a d) -> p n a d", n=n, a=2)
                tt(v1, src, every(cos, n), ALU.mult)
                swapped = src.rearrange("p n (a d) -> p n a d", a=2)[:, :, ::-1, :]
                ins = tt(v2, swapped, every(sin.rearrange("p (a d) -> p a d", a=2), n), ALU.mult)
                name[0](ins)
                link(tt(dst, v1, t2[:, 0:n * HD].rearrange("p (n d) -> p n d", n=n), ALU.add), name[1])

            for L in range(DEPTH):
                rope_tmp = (tmp_a, tmp_b)
                for t in range(TT):
                    bank = full(dve, ("xT", L, t, 1))
                    free(dve.tensor_copy(xT[:, 4:8, t * P:(t + 1) * P], bank[:, :].rearrange("p (j s) -> p j s", j=4)), ("xT", L, t, 1))
                taken(dve, ("lx", L))
                pc = V_LRU + L * 16
                for w in range(4):
                    for b in range(2):
                        tap = par[:, pc + b * 4 + w:pc + b * 4 + w + 1]
                        src = lru_x[:, b, w:w + S]
                        if w == 0:
                            ins = ts(conv[:, b, :], src, tap, ALU.mult, par[:, pc + 8 + b:pc + 9 + b], ALU.add)
                        else:
                            ins = stt(conv[:, b, :], src, tap, conv[:, b, :], ALU.mult, ALU.add)
                        if b == 1:
                            link(ins, "conv" if w == 3 else "dve_step")
                dve.wait_ge(sem("lg_tanh"), L + 1)
                bank = full(dve, ("lg", L))
                free(stt(lru_gate.rearrange("p b s -> p (b s)"), tanh_buf[:, 0, :], 1.0, bank[:, :], ALU.add, ALU.mult), ("lg", L))
                for t in range(TT):
                    bank = full(dve, ("rqk", L, t))
                    rope(rot[:, t, :].rearrange("p (n d) -> p n d", n=8), bank[:, :].rearrange("p (n d) -> p n d", n=8), 8,
                         const[:, C_COSA + t * HD:C_COSA + (t + 1) * HD], const[:, C_SINA + t * HD:C_SINA + (t + 1) * HD],
                         (lambda ins, nm=("rqk", L, t): (free(ins, nm), taken(dve, nm)), "rot"))
                bank = full(dve, ("kcvc", L))
                for b in range(2):
                    ins = tt(blocksT[:, b, :, :], view(bank[:, :], b * S, [[1, CMP_L], [CMP_S, CMP_N]]),
                             every(par[:, V_POS + (L * 2 + b) * CMP_L:V_POS + (L * 2 + b + 1) * CMP_L], CMP_N, 2), ALU.add)
                free(ins, ("kcvc", L))
                taken(dve, ("lr", L))
                for b in range(2):
                    ins = ts(lru_r[:, b, :], lru_r[:, b, :], 1.0, ALU.add, sp4[:, L * 2 + b:L * 2 + b + 1], ALU.mult)
                link(ins, "lru_la")
                taken(dve, ("li", L))
                link(stt(lru_i, lru_i, 1.0, conv, ALU.add, ALU.mult))
                dve.wait_ge(sem("lru_a"), 2 * (L + 1))
                link(ts(lru_r, lru_t, -1.0, ALU.mult, 1.0, ALU.add))
                link(dve.reciprocal(lru_r, lru_r))
                link(stt(lru_t, lru_t, -2.0, lru_r, ALU.mult, ALU.mult), "lru_v")
                for t in range(TT):
                    dve.wait_ge(sem("rg_tanh"), TT * L + t + 1)
                    bank = full(dve, ("rvg", L, t))
                    free(stt(ret_g[:, t, :], tanh_buf[:, 1 - t, 0:S], 1.0, bank[:, S:2 * S], ALU.add, ALU.mult), ("rvg", L, t))
                for t in range(TT):
                    dve.wait_ge(sem("ng_tanh"), TT * L + t + 1)
                    bank = full(dve, ("ng", L, t))
                    free(stt(nsa_g[:, t, :], tanh_buf[:, 1 - t, :], 1.0, bank[:, :], ALU.add, ALU.mult), ("ng", L, t))
                for j in range(3):
                    at = C_DECAY + (4 * P if j == 1 else 0)
                    for odd in range(2):
                        bank = full(dve, ("rs", L, j, odd))
                        free(tt(ret_s[:, j, :].rearrange("p (n o s) -> p n o s", n=2, o=2)[:, :, odd, :],
                                bank[:, 0:2 * P].rearrange("p (n s) -> p n s", n=2),
                                const[:, at:at + 4 * P].rearrange("p (n o s) -> p n o s", n=2, o=2)[:, :, odd, :],
                                ALU.mult), ("rs", L, j, odd))
                for t in range(TT):
                    cm = const[:, C_CMASK + t * CMP_N:C_CMASK + (t + 1) * CMP_N]
                    for g in range(2):
                        bank = full(dve, ("nc", L, t, g))
                        free(tt(cmp_s[:, t, 4 * g:4 * g + 4, :], bank[:, 0:4 * CMP_N].rearrange("p (h n) -> p h n", h=4),
                                every(cm, 4), ALU.add), ("nc", L, t, g))
                        taken(dve, ("nc", L, t, g))
                    link(dve.tensor_reduce(cmax, cmp_s[:, t, :, :], AX.X, ALU.max))
                    link(tt(cmp_s[:, t, :, :], cmp_s[:, t, :, :], every(cmax, CMP_N, 2), ALU.subtract), "cmp_sub")
                dve.wait_ge(sem("lru_sq"), L + 1)
                link(stt(lru_i, lru_i, 0.5, lru_t, ALU.mult, ALU.mult))
                for b in range(2):
                    ins = dve.tensor_tensor_scan(lru_h[:, b, :], lru_a[:, b, :], lru_i[:, b, :], 0.0, ALU.mult, ALU.add)
                link(ins)
                link(stt(yT[:, 6:8, :], lru_h, 0.5, lru_gate, ALU.mult, ALU.mult), "y_lru")
                for t in range(TT):
                    bank = full(dve, ("ro", L, t))
                    b3 = bank[:, 0:S].rearrange("p (h d) -> p h d", h=4)
                    centred = tmp_a[:, 0:S].rearrange("p (h d) -> p h d", h=4)
                    squares = tmp_b[:, 0:S].rearrange("p (h d) -> p h d", h=4)
                    link(dve.tensor_reduce(stat[:, 0:4], b3, AX.X, ALU.add))
                    link(ts(stat[:, 0:4], stat[:, 0:4], -1.0 / HD, ALU.mult))
                    free(tt(centred, b3, every(stat[:, 0:4], HD, 2), ALU.add), ("ro", L, t))
                    taken(dve, ("ro", L, t))
                    link(tt(squares, centred, centred, ALU.mult))
                    link(dve.tensor_reduce(stat2[:, 0:4], squares, AX.X, ALU.add))
                    link(ts(var[:, 0:4], stat2[:, 0:4], 1.0 / HD, ALU.mult, EPS_LN, ALU.add))
                    inverse_root(4)
                    link(tt(squares, centred, every(rstd[:, 0:4], HD, 2), ALU.mult))
                    link(stt(y[:, t, 0:S], tmp_b[:, 0:S], 0.5, ret_g[:, t, :], ALU.mult, ALU.mult), "y_ret")
                for t in range(TT):
                    dve.wait_ge(sem("cmp_probs"), TT * L + t + 1)
                    link(dve.tensor_reduce(sums[:, t, :, 0], cmp_s[:, t, :, :], AX.X, ALU.add))
                    taken(dve, ("vg", L, t))
                    link(ts(gates3[:, t, :, :].rearrange("p h b -> p (h b)"), nsa_gt[:, t, :], 1.0, ALU.add))
                    link(ts(gates3[:, t, :, 0], gates3[:, t, :, 0], const[:, C_ANY + t:C_ANY + t + 1], ALU.mult))

                def nsa_max(i):
                    t, h = items[i]
                    nk = (t + 1) * P
                    bank = full(dve, ("ns", L, i))
                    b3 = bank[:, 0:2 * nk].rearrange("p (b k) -> p b k", b=2)
                    link(tt(b3[:, :, t * P:nk], b3[:, :, t * P:nk], every(const[:, C_TRIL:C_TRIL + P], 2), ALU.add))
                    link(dve.tensor_reduce(neg_max[:, i % 4, :], b3, AX.X, ALU.max, negate=True), "nsa_max")

                def nsa_out(j):
                    t, h = items[2 * j]
                    bank = full(dve, ("no", L, j))
                    s6 = sums[:, t, h:h + 2, :].rearrange("p h b -> p (h b)")
                    link(dve.reciprocal(coef, s6))
                    link(tt(coef, coef, gates3[:, t, h:h + 2, :].rearrange("p h b -> p (h b)"), ALU.mult))
                    o6 = tmp_a[:, 0:6 * HD].rearrange("p (n d) -> p n d", n=6)
                    free(tt(o6, bank[:, 0:6 * HD].rearrange("p (n d) -> p n d", n=6), every(coef, HD, 2), ALU.mult), ("no", L, j))
                    taken(dve, ("no", L, j))
                    link(dve.tensor_reduce(tmp_b[:, 0:2 * HD].rearrange("p (h d) -> p h d", h=2),
                                           tmp_a[:, 0:6 * HD].rearrange("p (h b d) -> p h d b", h=2, b=3), AX.X, ALU.add))
                    ins = stt(y[:, t, S + h * HD:S + (h + 2) * HD], tmp_b[:, 0:2 * HD], 0.25, nsa_g[:, t, h * HD:(h + 2) * HD],
                              ALU.mult, ALU.mult)
                    link(ins, "y_nsa" if h == 6 else "dve_step")

                nsa_max(0)
                nsa_max(1)
                for i in range(len(items)):
                    if i + 2 < len(items):
                        nsa_max(i + 2)
                    if i % 2 == 0:
                        bank = full(dve, ("nT", L, i))
                        n = 2 * (items[i][0] + 1) * P
                        free(dve.tensor_copy(probsT[:, 0, 0:n], bank[:, 0:n]), ("nT", L, i))
                        if i:
                            nsa_out(i // 2 - 1)
                nsa_out(len(items) // 2 - 1)
                for half in range(2):
                    for t in range(TT):
                        bank = full(dve, ("wo", L, t, half))
                        c = slice(half * 512, (half + 1) * 512)
                        free(stt(z[:, t, c], x3[:, t, c], ALPHA, bank[:, :], ALU.mult, ALU.add), ("wo", L, t, half))
                        taken(dve, ("wo", L, t, half))
                dve.wait_ge(sem("in_ln"), 32 * (L + 1))
                for t in range(TT):
                    for j in range(2):
                        ins = dve.bn_stats(bn[:, j, :], z[:, t, j * 512:(j + 1) * 512])
                    link(ins)
                    link(dve.bn_aggr(mvar, bn))
                    link(ts(var[:, 0:1], mvar[:, 1:2], EPS_LN, ALU.add))
                    inverse_root(1)
                    link(ts(z[:, t, :], z[:, t, :], mvar[:, 0:1], ALU.subtract, rstd[:, 0:1], ALU.mult))
                    link(tt(z[:, t, :], z[:, t, :], ln_gb[:, 0, :], ALU.mult))
                    link(tt(x3[:, t, :], z[:, t, :], ln_gb[:, 1, :], ALU.add), "x_next")

            dve.wait_ge(sem("in_mod"), 32)
            dve.wait_ge(sem("in_gmix"), 16)
            dve.wait_ge(sem("in_ctx"), 32)

            def modulation(c, j):
                dst = (mod if j == 0 else cmod)[:, c // 2, (c % 2) * 512:(c % 2 + 1) * 512]
                bank = full(dve, ("ada", c, j))
                free(tt(dst, dst, bank[:, :], ALU.add), ("ada", c, j))

            def rms_rows(dst, src, ss, gain, shift, name):
                link(ts(var[:, 0:1], ss, 1.0 / D, ALU.mult, EPS_RMS, ALU.add))
                inverse_root(1)
                link(stt(dst, src, rstd[:, 0:1], gain, ALU.mult, ALU.mult))
                link(tt(dst, dst, shift, ALU.add), name)

            for c in range(4):
                for j in range(2):
                    modulation(c, j)
            for c in range(4):
                for j in range(2):
                    taken(dve, ("ada", c, j))
            link(stt(cmod[:, 1, :], cmod[:, 1, :], 1.0, gvec, ALU.add, ALU.mult), "sc_mix")
            link(stt(mod[:, 1, :], mod[:, 1, :], 1.0, gvec, ALU.add, ALU.mult), "sc_mix")
            for r in range(4):
                dve.wait_ge(sem("rms_sq"), r + 1)
                if r < 2:
                    rms_rows(hc_x[:, r, :], hc_x[:, r, :], sumsq[:, r:r + 1], cmod[:, 1, :], cmod[:, 0, :], "h_rows")
                else:
                    dve.wait_ge(sem("rms_sq"), 4)
                    rms_rows(hl[:, r - 2, :], x3[:, r - 2, :], sumsq[:, r:r + 1], mod[:, 1, :], mod[:, 0, :], "h_rows")
            for c in range(4, 12):
                modulation(c, 0)
            for r in range(4):
                bank = full(dve, ("hT", r, 1))
                free(dve.tensor_copy(hT[:, 4:8, r * P:(r + 1) * P], bank[:, :].rearrange("p (j s) -> p j s", j=4)), ("hT", r, 1))
            for r in range(4):
                taken(dve, ("hT", r, 1))
            dve.wait_ge(sem("fgate_exp"), 1)
            log1p_half(rt_a[0:8, :], rt_b[0:8, :], rows[7], rows[2])
            link(ts(rows[1], rows[1], 0.0, ALU.min))
            link(stt(rows[2], rows[2], -2.0, rows[1], ALU.mult, ALU.add))
            link(dve.memset(rows[7], 0.0))
            link(dve.tensor_tensor_scan(rows[3], rows[2], rows[7], 0.0, ALU.add, ALU.add))
            link(dve.tensor_tensor_scan(rows[4][:, S - 1::-1], rows[2][:, S - 1::-1], rows[7][:, 0:S], 0.0, ALU.add, ALU.add))
            link(dve.tensor_tensor_scan(rows[4][:, 2 * S - 1:S - 1:-1], rows[2][:, 2 * S - 1:S - 1:-1], rows[7][:, 0:S],
                                        rows[4][:, 0:1], ALU.add, ALU.add))
            link(tt(rows[5], rows[0], rows[3], ALU.subtract))
            link(tt(rows[6], rows[0], rows[4], ALU.subtract), "gate_rows")
            for r in range(4):
                bank = full(dve, ("akv", r))
                free(dve.tensor_copy(akv[:, r, :], bank[:, 0:256]), ("akv", r))
            for r in range(4):
                taken(dve, ("akv", r))
            dve.wait_ge(sem("in_small"), 64)
            rope_tmp = (rt_a, rt_b)
            k4 = akv[:, :, 0:P].rearrange("p t (n d) -> p t n d", n=2)
            sq4 = rt_a.rearrange("p (t n d) -> p t n d", t=4, n=2)
            link(tt(sq4, k4, k4, ALU.mult))
            link(dve.tensor_reduce(stat[:, 0:8], rt_a.rearrange("p (n d) -> p n d", n=8), AX.X, ALU.add))
            link(ts(var[:, 0:8], stat[:, 0:8], 1.0 / HD, ALU.mult, EPS_RMS, ALU.add))
            inverse_root(8)
            link(tt(k4, k4, every(rstd[:, 0:8].rearrange("p (t n) -> p t n", t=4), HD, 3), ALU.mult))
            link(tt(k4, k4, every(every(qk_g[:, 1, :], 2), 4), ALU.mult))
            for t in range(TT):
                src = akv[:, 2 + t, 0:P].rearrange("p (n d) -> p n d", n=2)
                rope(src, src, 2, const[:, C_COSB + t * HD:C_COSB + (t + 1) * HD], const[:, C_SINB + t * HD:C_SINB + (t + 1) * HD],
                     (link, "ak" if t else "dve_step"))
            for t in range(TT):
                bank = full(dve, ("aq", t))
                free(dve.tensor_copy(aq[:, t, :], bank[:, :]), ("aq", t))
                taken(dve, ("aq", t))
                q3 = aq[:, t, :].rearrange("p (n d) -> p n d", n=8)
                s3 = rt_a.rearrange("p (n d) -> p n d", n=8)
                link(tt(s3, q3, q3, ALU.mult))
                link(dve.tensor_reduce(stat[:, 0:8], s3, AX.X, ALU.add))
                link(ts(var[:, 0:8], stat[:, 0:8], 1.0 / HD, ALU.mult, EPS_RMS, ALU.add))
                inverse_root(8)
                link(tt(q3, q3, every(rstd[:, 0:8], HD, 2), ALU.mult))
                link(stt(q3, q3, HD ** -0.5, every(qk_g[:, 0, :], 8), ALU.mult, ALU.mult))
                cos = const[:, C_COSB + t * HD:C_COSB + (t + 1) * HD]
                sin = const[:, C_SINB + t * HD:C_SINB + (t + 1) * HD]
                tt(s3, q3, every(cos, 8), ALU.mult)
                link(tt(rt_b.rearrange("p (n a d) -> p n a d", n=8, a=2),
                        q3.rearrange("p n (a d) -> p n a d", a=2)[:, :, ::-1, :],
                        every(sin.rearrange("p (a d) -> p a d", a=2), 8), ALU.mult))
                link(tt(aq[:, t, :].rearrange("p (r g d) -> p g r d", r=4, g=2),
                        rt_a.rearrange("p (g r d) -> p g r d", g=2, r=4),
                        rt_b.rearrange("p (g r d) -> p g r d", g=2, r=4), ALU.add), "aq")
            link(ts(negsink, sink, -1.0, ALU.mult))

            def attn_max(i):
                t, h = items[i]
                bank = full(dve, ("as", i))
                edge, m = (slice(3 * P, 4 * P), C_TRIL) if t == 0 else (slice(2 * P, 3 * P), C_TRIU)
                link(tt(bank[:, edge], bank[:, edge], const[:, m:m + P], ALU.add))
                link(dve.tensor_reduce(stat[:, 0:1], bank[:, :], AX.X, ALU.max, negate=True))
                link(tt(nmA[:, t, h:h + 1], stat[:, 0:1], negsink[:, h:h + 1], ALU.min), "attn_max")

            def attn_out(t):
                bank = full(dve, ("ao", t))
                free(tt(a_lat[:, t, :].rearrange("p (h d) -> p h d", h=8), bank[:, :].rearrange("p (h d) -> p h d", h=8),
                        every(es, HD, 2), ALU.mult), ("ao", t))
                taken(dve, ("ao", t))

            attn_max(0)
            attn_max(1)
            for i in range(len(items)):
                if i + 2 < len(items):
                    attn_max(i + 2)
                if i % 2 == 0:
                    bank = full(dve, ("aT_", i))
                    free(dve.tensor_copy(probs2T[:, 0, :], bank[:, :]), ("aT_", i))
                    if i == 8:
                        attn_out(0)
                if i % 8 == 7:
                    t = i // 8
                    link(tt(es, nmA[:, t, :], sink, ALU.add), "sink_sub")
                    dve.wait_ge(sem("sink_exp"), t + 1)
                    link(tt(es, es, den[:, t, :], ALU.add))
                    link(dve.reciprocal(es, es))
            attn_out(1)
            taken(dve, ("fc",))
            full(dve, ("aT_", 15))
            for h in range(MH):
                for d in range(2):
                    bank = full(dve, ("G", d, h))
                    for t in range(TT):
                        m = C_MM + (d * TT + t) * 512
                        j = d * TT + t
                        ins = dve.tensor_tensor_reduce(out=dw[:, j, :], in0=bank[:, :], in1=const[:, m:m + 512], scale=1.0,
                                                       scalar=0.0, op0=ALU.add, op1=ALU.max, accum_out=mu[:, j:j + 1])
                    free(ins, ("G", d, h))
                    taken(dve, ("G", d, h))
                link(ts(negmu, mu, -1.0, ALU.mult))
                ft = view(fcol, h, [[TT * 8 + 4, 2], [8, TT]])
                link(stt(flo_in.rearrange("p (d t) -> p d t", d=2), ft, -1.0, negmu.rearrange("p (d t) -> p d t", d=2),
                         ALU.mult, ALU.add), "mlstm_mu")
                dve.wait_ge(sem("mlstm_w"), 5 * (h + 1))
                for t in range(TT):
                    bank = full(dve, ("qk", h, t))
                    for d in range(2):
                        j = d * TT + t
                        ins = dve.tensor_tensor_reduce(out=dw[:, j, :], in0=bank[:, :], in1=dw[:, j, :], scale=1.0,
                                                       scalar=0.0, op0=ALU.mult, op1=ALU.add, accum_out=mden[:, j:j + 1])
                    free(ins, ("qk", h, t))
                    taken(dve, ("qk", h, t))
                link(stt(mabs, mden, -1.0, mden, ALU.mult, ALU.max))
                link(tt(mabs, mabs, flo_e, ALU.max))
                link(dve.reciprocal(mrec, mabs))
                for t in range(TT):
                    i = TT * h + t
                    if i >= 2:
                        full(dve, ("mT_", i - 2))
                    link(ts(probs2[:, i % 2, :], dw[:, t, :], mrec[:, t:t + 1], ALU.mult))
                    link(stt(probs2[:, i % 2, :], dw[:, TT + t, :], mrec[:, TT + t:TT + t + 1], probs2[:, i % 2, :],
                             ALU.mult, ALU.add), "mlstm_s")
            for t in range(TT):
                dve.wait_ge(sem("mlstm_sq"), t + 1)
                link(dve.tensor_reduce(stat[:, 0:4], dw[:, t, :].rearrange("p (h d) -> p h d", h=MH), AX.X, ALU.add))
                link(ts(var[:, 0:4], stat[:, 0:4], 1.0 / MD, ALU.mult, EPS_RMS, ALU.add))
                inverse_root(4)
                bank = full(dve, ("mo", t))
                free(tt(rt_a.rearrange("p (h d) -> p h d", h=MH), bank[:, :].rearrange("p (h d) -> p h d", h=MH),
                        every(rstd[:, 0:4], MD, 2), ALU.mult), ("mo", t))
                taken(dve, ("mo", t))
                link(stt(rt_a, rt_a, 0.5, norm_g, ALU.mult, ALU.mult))
                taken(dve, ("mog", t))
                link(stt(m_lat[:, t, :], mo_t[:, t, :], 1.0, rt_a, ALU.add, ALU.mult), "m_lat")
            for half in range(2):
                c = slice(half * 512, (half + 1) * 512)
                for n, g in enumerate(("gm", "ga")):
                    for t in range(TT):
                        i = half * 4 + n * 2 + t
                        taken(dve, (g, half, t))
                        bank = full(dve, ("b" + g, half, t))
                        dst = mrg[:, t, c] if n == 0 else branch_u[:, 0, :]
                        free(stt(dst, gate_t[:, i % 2, :], 1.0, bank[:, :], ALU.add, ALU.mult), ("b" + g, half, t))
                        if n:
                            taken(dve, ("b" + g, half, t))
                            link(tt(mrg[:, t, c], mrg[:, t, c], branch_u[:, 0, :], ALU.add), "mrg")
            for t in range(TT):
                bank = full(dve, ("gT", t, 1))
                free(dve.tensor_copy(mrgT[:, 4:8, t * P:(t + 1) * P], bank[:, :].rearrange("p (j s) -> p j s", j=4)), ("gT", t, 1))
            for half in range(2):
                c = slice(half * 512, (half + 1) * 512)
                for t in range(TT):
                    bank = full(dve, ("wo2", half, t))
                    free(stt(rt_a, bank[:, :], 0.5, mod[:, 2, c], ALU.mult, ALU.mult), ("wo2", half, t))
                    taken(dve, ("wo2", half, t))
                    link(tt(x3[:, t, c], x3[:, t, c], rt_a, ALU.add), "x1" if half else "dve_step")
            dve.wait_ge(sem("in_gffn"), 16)
            link(stt(mod[:, 4, :], mod[:, 4, :], 1.0, gvec, ALU.add, ALU.mult))
            for t in range(TT):
                dve.wait_ge(sem("rms_sq"), 4 + t + 1)
                rms_rows(h2[:, t, :], x3[:, t, :], sumsq[:, t:t + 1], mod[:, 4, :], mod[:, 3, :], "h2")
            for t in range(TT):
                bank = full(dve, ("pT", t, 1))
                free(dve.tensor_copy(xT[:, 4:8, t * P:(t + 1) * P], bank[:, :].rearrange("p (j s) -> p j s", j=4)), ("pT", t, 1))
            for j in range(1, 8, 2):
                bank = full(dve, ("pq", j))
                free(dve.tensor_copy(pqT[:, 2 * j:2 * j + 2, :], bank[:, :].rearrange("p (b s) -> p b s", b=2)), ("pq", j))

            def step(ins):
                body["n"] += 1
                ins.then_inc(sem("expert_step"), 1)
                dve.wait_ge(sem("expert_step"), body["it"] * STEPS + (body["base"] + body["n"]))

            def step_go(ins):
                step(ins)
                dve.sem_inc(sem("top_go"), 1)

            def top16(values, indices, src, scratch):
                step_go(dve.max(values[:, 0:8], src))
                step_go(dve.max_index(indices[:, 0:8], values[:, 0:8], src))
                step_go(dve.match_replace(scratch, values[:, 0:8], src, -3e38))
                step_go(dve.max(values[:, 8:16], scratch))
                step(dve.max_index(indices[:, 8:16], values[:, 8:16], scratch))

            def choose(it, head):
                s = head % 2
                flat = score.rearrange("p t l n -> p (t l n)")
                step_go(dve.tensor_copy(head_s, flat[:, bass.ds(it * (4 * NKEY) + head * 2 * NKEY, 2 * NKEY)]))
                for half in range(2):
                    k = slice(half * TOPK, (half + 1) * TOPK)
                    if half:
                        dve.sem_inc(sem("top_go"), 1)
                    top16(tops[:, k], topi[:, k], head_s[:, half * NKEY:(half + 1) * NKEY], work[:, 0:NKEY])
                step(dve.tensor_copy(topf, topi))
                step_go(tt(cand.rearrange("p (a b) -> p a b", a=TOPK), every(tops[:, 0:TOPK], TOPK, 2),
                        every(tops[:, TOPK:2 * TOPK], TOPK), ALU.add))
                top16(best, bpos, cand, work)
                ts(bhl[:, 0:TOPK], bpos, 4, ALU.logical_shift_right)
                step(ts(bhl[:, TOPK:2 * TOPK], bpos, TOPK - 1, ALU.bitwise_and))
                step(dve.tensor_copy(fhl, bhl))
                hot3 = hot.rearrange("p (k a) -> p k a", k=TOPK)
                iota = const[:, C_IOTA:C_IOTA + TOPK]
                for half, dst in enumerate((sel1, sel2)):
                    k = slice(half * TOPK, (half + 1) * TOPK)
                    step(tt(hot3, every(fhl[:, k], TOPK, 2), every(iota, TOPK), ALU.is_equal))
                    step(tt(hot3, hot3, every(topf[:, k], TOPK), ALU.mult))
                    step(dve.tensor_reduce(dst, hot3, AX.X, ALU.add))
                dve.wait_ge(sem("idx_copied"), it * 2 + (CREDIT + head + 1 - 2))
                stt(idx_next[:, s * TOPK:(s + 1) * TOPK], sel1, float(NKEY), sel2, ALU.mult, ALU.add).then_inc(sem("idx_ready"), 1)
                ts(esum[:, 0:1], best[:, 0:1], -1.0, ALU.mult).then_inc(sem("top_sub"), 1)
                dve.wait_ge(sem("top_exp"), it * 2 + (head + 1))
                step(dve.reciprocal(esum[:, 2:3], esum[:, 1:2]))
                step(ts(gate_next[:, s * TOPK:(s + 1) * TOPK], bexp, esum[:, 2:3], ALU.mult, 0.5, ALU.mult))

            def weigh(it, t, head):
                s = head % 2
                for r in range(TOPK):
                    at = head * TOPK + r
                    dve.wait_ge(sem(f"u_full{r % RING}"), it * (16 * 2 * TOPK // RING) + 16 * (at // RING + 1))
                    row = u_ring[:, r % RING, :]
                    dve.tensor_tensor_reduce(out=row, in0=row, in1=h2[:, t, :], scale=1.0, scalar=0.0, op0=ALU.mult,
                                             op1=ALU.add, accum_out=dots[:, s * TOPK + r:s * TOPK + r + 1]).then_inc(sem("u_used"), 1)
                dve.wait_ge(sem("u_used"), it * (2 * TOPK) + (CREDIT + (head + 1) * TOPK))
                hd = dots[:, s * TOPK:(s + 1) * TOPK]
                wv = wcur[:, s * TOPK:(s + 1) * TOPK]
                step(tt(d_a, hd, hd, ALU.mult))
                step(ts(d_a, d_a, 0.044715, ALU.mult, 1.0, ALU.add))
                stt(d_a, d_a, 0.7978845608028654, hd, ALU.mult, ALU.mult).then_inc(sem("gelu_in"), 1)
                dve.wait_ge(sem("gelu_tanh"), it * 2 + (head + 1))
                step(stt(d_b, d_b, 1.0, hd, ALU.add, ALU.mult))
                dve.wait_ge(sem("diag_ready"), it * (2 * TOPK) + (CREDIT + (head - 1) * TOPK))
                tt(wv, d_b, gate_next[:, s * TOPK:(s + 1) * TOPK], ALU.mult).then_inc(sem("w_ready"), 1)
                dve.wait_ge(sem("w_ready"), it * 2 + (head + 1))

            def result(t):
                for half in range(2):
                    c = slice(half * 512, (half + 1) * 512)
                    bank = full(dve, ("pv", t, half))
                    free(tt(rt_a, bank[:, :], mod[:, 5, c], ALU.mult), ("pv", t, half))
                    taken(dve, ("pv", t, half))
                    link(tt(x3[:, t, c], x3[:, t, c], rt_a, ALU.add), "result" if half else "dve_step")

            dve.sem_inc(sem("u_used"), CREDIT)
            body = {"it": 0, "base": 0, "n": 0}
            for head in range(2):
                dve.wait_ge(sem("scores"), 1)
                choose(0, head)
            before = body["n"]
            for t in range(TT):
                with dve.Fori(0, EH // 2 - t) as it:
                    body.update(it=it, base=before + t * (EH // 2) * STEPS, n=0)
                    dve.wait_ge(sem("scores"), it + (t * EH // 2 + 2))
                    for s in range(2):
                        weigh(it, t, t * EH + s)
                        choose(it, t * EH + s + 2)
                    assert body["n"] == STEPS, body
            result(0)
            body.update(it=0, base=before + (TT * EH // 2 - 1) * STEPS, n=0)
            for s in range(2):
                weigh(0, TT - 1, TT * EH - 2 + s)
            result(1)

        @block.gpsimd
        def _(pool):
            asked = [0]

            def root(cols):
                asked[0] += 1
                pool.wait_ge(sem("var_ready"), asked[0])
                pool.tensor_tensor(rstd[:, 0:cols], var[:, 0:cols], half8[:, 0:cols], ALU.pow).then_inc(sem("root_done"), 1)

            pool.wait_ge(sem("in_const"), 32)
            for L in range(DEPTH):
                for cols in (4, 4, 1, 1):
                    root(cols)
            for cols in (1, 1, 1, 1, 8, 8, 8, 4, 4, 1, 1):
                root(cols)
            pool.sem_inc(sem("v_used"), CREDIT)
            pool.sem_inc(sem("idx_copied"), CREDIT)
            full(pool, ("ps", 1, 3))

            def indices(it, head):
                if head < TT * EH:
                    pool.wait_ge(sem("idx_ready"), it * 2 + (head + 1))
                    pool.wait_ge(sem("u_used"), it * (2 * TOPK) + (CREDIT + (head - 1) * TOPK))
                    s = head % 2
                    pool.sem_inc(sem("gather_go"), 1)
                    pool.tensor_copy(idx_u[:, s * TOPK:(s + 1) * TOPK], idx_next[:, s * TOPK:(s + 1) * TOPK]
                                     ).then_inc(sem("idx_copied"), 1)
                if head:
                    s = (head - 1) % 2
                    pool.wait_ge(sem("v_used"), it * (2 * TOPK) + (CREDIT + (head - 2) * TOPK))
                    pool.sem_inc(sem("gather_go"), 1)
                    pool.tensor_copy(idx_v[:, s * TOPK:(s + 1) * TOPK], idx_u[:, s * TOPK:(s + 1) * TOPK]
                                     ).then_inc(sem("idx_v_copied"), 1)
                    pool.wait_ge(sem("idx_v_copied"), it * 2 + head)
                if head < TT * EH:
                    pool.wait_ge(sem("idx_copied"), it * 2 + (CREDIT + head + 1))
                    pool.sem_inc(sem("gather_go"), 1)

            def gather(it, head, r, which):
                s = head % 2
                at = head * TOPK + r
                row, table, cur = {"u": (u_ring[:, r % RING, :], a["peer_u"], idx_u),
                                   "v": (v_ring[r % RING], a["peer_v"], idx_v)}[which]
                if r % 4 == 0:
                    pool.wait_ge(sem(which + "_used"), it * (2 * TOPK) + (CREDIT + at + 4 - RING))
                    pool.sem_inc(sem("gather_go"), 1)
                pool.indirect_dma_start(out=row, out_offset=None, in_=table,
                                        in_offset=bass.IndirectOffsetOnAxis(ap=cur[:, s * TOPK + r:s * TOPK + r + 1], axis=0)
                                        ).then_inc(sem(f"{which}_full{r % RING}"), 16)

            indices(0, 0)
            for r in range(TOPK):
                gather(0, 0, r, "u")
            with pool.Fori(0, TT * EH // 2 - 1) as it:
                for s in range(2):
                    indices(it, s + 1)
                    for r in range(TOPK):
                        gather(it, s + 1, r, "u")
                        gather(it, s, r, "v")
            last = TT * EH - 1
            indices(0, last)
            for r in range(TOPK):
                gather(0, last, r, "u")
                gather(0, last - 1, r, "v")
            indices(0, last + 1)
            for r in range(TOPK):
                gather(0, last, r, "v")


def pack(w, n):
    k = w.shape[0] // P
    return np.ascontiguousarray(w.reshape(k, P, n, -1).transpose(2, 1, 0, 3)).reshape(n, P, -1)


def layout(i):
    f = {k: np.asarray(v) for k, v in i.items()}
    at = np.cumsum([0, 256, 256, 256, 256, 512, 128, 128, 128, 128, 128, 128, 512, 24, 256, 256])
    rq, rk, rv, rg, nq, nkc, nvc, nks, nvs, nkw, nvw, ng, ngl, lx, lg = [np.arange(p, q) for p, q in zip(at[:-1], at[1:])]
    pairs = nq.reshape(2, 4, HD).transpose(1, 0, 2).ravel()
    order = np.concatenate([lx, lg, rq, rk, pairs, nkc, nvc, nks, nkw, rv, rg, ng])
    a = {"x": f["x"][0], "const": constants()}
    a["w1"] = np.stack([pack(f["w_in"][l][:, order], 6) for l in range(DEPTH)])
    a["w1b"] = np.stack([pack(f["w_in"][l][:, np.concatenate([nvs, nvw, ngl])], 1)[0] for l in range(DEPTH)])
    cw = f["nsa_cmp_w"].reshape(DEPTH, 2, CMP_L, HD, HD).transpose(0, 3, 1, 2, 4).reshape(DEPTH, HD, -1)
    a["cmp"] = np.ascontiguousarray(np.concatenate([cw, cw], 1))
    a["wo"] = np.stack([pack(f["w_out"][l], 2) for l in range(DEPTH)])
    a["ln_g"], a["ln_b"] = f["ln_g"], f["ln_b"]
    par = np.zeros((P, V_END), np.float32)
    for l in range(DEPTH):
        c = V_LRU + l * 16
        for b in range(2):
            r = slice(b * P, (b + 1) * P)
            par[:, c + 4 * b:c + 4 * b + 4] = f["lru_conv_w"][l][:, r].T
            for j, name in enumerate(("lru_conv_b", "lru_b_a", "lru_b_x", "lru_lambda")):
                par[:, c + 8 + 2 * j + b] = f[name][l][r]
        for b in range(2):
            c = V_POS + (l * 2 + b) * CMP_L
            pos = f["nsa_cmp_pos"][l, b].T
            par[:, c:c + CMP_L] = np.concatenate([pos, pos], 0)
        for n, name in enumerate(("lru_w_a", "lru_w_x")):
            for b in range(2):
                c = V_WG + ((l * 2 + n) * 2 + b) * HD
                par[:, c:c + HD] = f[name][l][2 * b:2 * b + 2].reshape(P, HD)
    mg = f["b_mgates_2"][0].reshape(2, 2, MH)
    par[0:8, V_MG] = mg[:, 0].ravel()
    par[0:8, V_MG + 1] = mg[:, 1].ravel()
    cond = np.stack([f["c_2"][0], f["c_ctx_2"]], 1)
    par[:, V_COND:V_END] = cond.reshape(KC, P, 2).transpose(1, 0, 2).reshape(P, -1)
    a["par"] = par
    a["ctx"] = f["ctx_2"][0]
    a["ada"] = pack(f["w_ada_2"][0], 12)
    a["b_ada"] = f["b_ada_2"]
    a["g_mix"], a["g_ffn"] = f["norm_mix_g_2"], f["norm_ffn_g_2"]
    w = f["w_in_2"][0]
    at = np.cumsum([0, 512, 512, 512, 512, 16, 512, 128, 128, 1024, 1024])
    mq, mk, mv, mo, mg, aq, ak, av, gm, ga = [np.arange(p, q) for p, q in zip(at[:-1], at[1:])]
    mg = mg.reshape(2, 2, MH)
    order = np.concatenate([mk, mv, mq, aq, mo, gm[:512], ga[:512], gm[512:], ga[512:]])
    a["w2"] = pack(w[:, order], 9)
    a["w2b"] = pack(w[:, np.concatenate([ak, av])], 1)[0]
    a["wg2"] = pack(w[:, np.concatenate([mg[:, 0].ravel(), mg[:, 1].ravel()])], 1)[0].reshape(P, KC, 16)
    a["norm_g"] = f["mlstm_norm_g_2"]
    a["q_g"], a["k_g"], a["sink"] = f["attn_q_norm_g_2"], f["attn_k_norm_g_2"], f["attn_sink_2"]
    a["br"] = pack(np.concatenate([f["w_branch_m_2"][0], f["w_branch_a_2"][0]], 0), 2)
    a["wo2"] = pack(f["w_out_2"][0], 2)
    a["pq"] = pack(f["peer_w_query_2"][0], 4)
    a["sk"] = np.ascontiguousarray(f["peer_sub_keys_2"][0].transpose(3, 0, 1, 2)).reshape(P, 16 * NKEY)
    a["peer_u"], a["peer_v"] = f["peer_u_2"][0], f["peer_v_2"][0]
    return a


def kernel(**inputs):
    import concourse.bacc as bacc
    from concourse.bass_utils import run_bass_kernel_spmd

    arrays = layout(inputs)
    nc = bacc.Bacc("TRN2", target_bir_lowering=False, num_devices=1)
    a = {k: nc.dram_tensor(k + "_in", v.shape, F32, kind="ExternalInput").ap() for k, v in arrays.items()}
    out = nc.dram_tensor("result", (S, D), F32, kind="ExternalOutput").ap()
    program(nc, a, out)
    r = run_bass_kernel_spmd(nc, [{k + "_in": v for k, v in arrays.items()}], core_ids=[0])
    return r.results[0]["result"].reshape(1, S, D)
```

```python
import concourse.bass as bass
from concourse import mybir
from contextlib import ExitStack
import numpy as np

F32 = mybir.dt.float32
I32 = mybir.dt.int32
U32 = mybir.dt.uint32
ALU = mybir.AluOpType
ACT = mybir.ActivationFunctionType
AX = mybir.AxisListType

P = 128
D = 1024
KC = D // P
S = 256
TT = S // P
DEPTH = 2
HD = 64
EPS_LN = 1e-5
EPS_RMS = 1e-6
ALPHA = (2.0 * DEPTH) ** 0.25
NEG = -1e30
CMP_N = 15
CMP_L = 32
CMP_S = 16
LRU_C = 8.0
MH = 4
MD = 128
K_SCALE = MD ** -0.5
SLOT = KC * 512
NW = 3
ARENA = 28540
SMALL = 900
NBANK = 6
NACC = 2
EH = 8
TOPK = 16
NKEY = 128
RING = 8
STEPS = 62
CREDIT = 64
ADA_ORDER = (0, 1, 2, 3, 4, 5, 10, 11, 6, 7, 8, 9)
ATANH = [1.0 / (2 * k + 1) for k in range(1, 8)]

C_ID = 0
C_TRIL = C_ID + P
C_TRIU = C_TRIL + P
C_DECAY = C_TRIU + P
C_COSA = C_DECAY + 2 * 4 * P
C_SINA = C_COSA + TT * HD
C_COSB = C_SINA + TT * HD
C_SINB = C_COSB + TT * HD
C_MM = C_SINB + TT * HD
C_CMASK = C_MM + 4 * 512
C_ANY = C_CMASK + TT * CMP_N
C_IOTA = C_ANY + TT
C_NEGHALF = C_IOTA + TOPK
C_ZERO = C_NEGHALF + 8
C_ONE = C_ZERO + P
C_END = C_ONE + 1

V_LRU = 0
V_POS = V_LRU + DEPTH * 16
V_WG = V_POS + DEPTH * 2 * CMP_L
V_MG = V_WG + DEPTH * 2 * 2 * HD
V_ADA = V_MG + 2
V_GMIX = V_ADA + 6 * KC
V_GFFN = V_GMIX + KC
V_END = V_GFFN + KC


def constants():
    c = np.zeros((P, C_END), np.float32)
    i = np.arange(P)
    c[:, C_ID:C_ID + P] = np.eye(P)
    tril = np.where(i[None, :] <= i[:, None], 0.0, NEG)
    triu = np.where(i[None, :] >= i[:, None], 0.0, NEG)
    c[:, C_TRIL:C_TRIL + P] = tril
    c[:, C_TRIU:C_TRIU + P] = triu
    for h in range(4):
        lg = np.log(1.0 - 2.0 ** (-5.0 - h))
        diff = i[None, :] - i[:, None]
        diag = np.where(diff >= 0, np.exp(np.maximum(diff, 0) * lg), 0.0) * HD ** -0.5
        off = np.exp((diff + P) * lg) * HD ** -0.5
        c[:, C_DECAY + h * P:C_DECAY + (h + 1) * P] = diag
        c[:, C_DECAY + (4 + h) * P:C_DECAY + (5 + h) * P] = off
    half = HD // 2
    pos = np.arange(S)
    inv = (1.0 / (np.float32(10000.0) ** (np.arange(half, dtype=np.float32) / half))).astype(np.float32)
    ang_a = pos.astype(np.float32)[:, None] * inv
    nf = HD // 4
    inv_b = (np.float32(10000.0) ** (-np.arange(nf, dtype=np.float32) / nf)).astype(np.float32)
    ang_b = np.concatenate([(pos // 64).astype(np.float32)[:, None] * inv_b,
                            (pos % 64).astype(np.float32)[:, None] * inv_b], 1)
    for ang, cc, cs in ((ang_a, C_COSA, C_SINA), (ang_b, C_COSB, C_SINB)):
        cos, sin = np.cos(ang), np.sin(ang)
        for t in range(TT):
            r = slice(t * P, (t + 1) * P)
            c[:, cc + t * HD:cc + (t + 1) * HD] = np.concatenate([cos[r], cos[r]], 1)
            c[:, cs + t * HD:cs + (t + 1) * HD] = np.concatenate([-sin[r], sin[r]], 1)
    full = np.full((P, P), NEG)
    zero = np.zeros((P, P))
    masks = {(0, 0): [zero, zero, tril, full], (0, 1): [zero, zero, zero, tril],
             (1, 0): [zero, zero, triu, zero], (1, 1): [zero, zero, full, triu]}
    for (d, t), m in masks.items():
        at = C_MM + (d * TT + t) * 512
        c[:, at:at + 512] = np.concatenate(m, 1)
    ends = np.arange(CMP_N) * CMP_S + CMP_L - 1
    for t in range(TT):
        tok = t * P + i
        ok = ends[None, :] <= tok[:, None]
        c[:, C_CMASK + t * CMP_N:C_CMASK + (t + 1) * CMP_N] = np.where(ok, 0.0, NEG)
        c[:, C_ANY + t] = ok.any(1)
    c[:, C_IOTA:C_IOTA + TOPK] = np.arange(TOPK)
    c[:, C_NEGHALF:C_NEGHALF + 8] = -0.5
    c[:, C_ONE] = 1.0
    return c


def view(ap, offset, dims):
    return bass.AP(ap.tensor, ap.offset + offset, [list(ap.ap[0])] + [list(d) for d in dims])


def every(ap, n, axis=1):
    dims = [list(d) for d in ap.ap]
    dims.insert(axis, [0, n])
    return bass.AP(ap.tensor, ap.offset, dims)


def program(nc, a, out):
    ctx = ExitStack()
    sems = {}

    def sem(name):
        if name not in sems:
            sems[name] = ctx.enter_context(nc.semaphore(name))
        return sems[name]

    def sb(name, width, dt=F32):
        return ctx.enter_context(nc.sbuf_tensor(name, [P, width], dt))

    with ctx:
        const = sb("const", C_END)
        par = sb("par", V_END)
        wring = sb("wring", NW * SLOT)
        x = sb("x", TT * D)
        hT_all = sb("hT", KC * 512)
        small = sb("small", SMALL)
        arena = sb("arena", ARENA)
        used = {"a": 0, "s": 0}

        def take_small(n):
            at = used["s"]
            used["s"] += n
            assert used["s"] <= SMALL
            return small[:, at:at + n]

        def take(n, at=None):
            if at is None:
                at = used["a"]
                used["a"] += n
                assert used["a"] <= ARENA, used
            return arena[:, at:at + n]

        chunks = []
        for layer in range(DEPTH):
            chunks += [("w1", layer, 1), ("w1", layer, 0), ("w1", layer, 2)]
            chunks += [("ada", 0, 6 * layer), ("w1", layer, 3), ("w1", layer, 4), ("ada", 0, 6 * layer + 1)]
            chunks += [("w1", layer, 5), ("ada", 0, 6 * layer + 2), ("w1", layer, 6), ("ada", 0, 6 * layer + 3)]
            chunks += [("cmp", layer, 0), ("ada", 0, 6 * layer + 4)]
            if layer == DEPTH - 1:
                chunks += [("w2c", 0, 0), ("w2c", 0, 1)]
            chunks += [("wo", layer, 0), ("wo", layer, 1), ("ada", 0, 6 * layer + 5)]
        chunks += [("w2c", 0, 2)]
        chunks += [("w2", 0, c) for c in (4, 0, 1, 2, 3, 5, 6, 7, 8, 9)]
        chunks += [("br", 0, 0), ("br", 0, 1), ("wo2", 0, 0), ("wo2", 0, 1)]
        chunks += [("sk", 0, 0), ("pq", 0, 0), ("pq", 0, 1), ("kept", 0, 0), ("pq", 0, 2), ("pq", 0, 3)]
        place = {c: (n % NW, n // NW) for n, c in enumerate(chunks)}
        place_of_sk = place[("sk", 0, 0)][0]

        psum = [ctx.enter_context(nc.psum_tensor(f"bank{b}", [P, 512], F32)) for b in range(NBANK + NACC)]
        bank_full = [sem(f"bank_full{b}") for b in range(NBANK + NACC)]
        bank_free = [sem(f"bank_free{b}") for b in range(NBANK + NACC)]

        ident = const[:, C_ID:C_ID + P]
        x3 = x[:, :].rearrange("p (t d) -> p t d", t=TT)
        hT = hT_all[:, :].rearrange("p (k s) -> p k s", k=KC)
        xT = hT[:, :, S:2 * S]

        blocksT = take(2 * CMP_L * CMP_N).rearrange("p (b l n) -> p b l n", b=2, l=CMP_L)
        lru_x = take(2 * (S + 3)).rearrange("p (b s) -> p b s", b=2)
        lru_gate = take(2 * S).rearrange("p (b s) -> p b s", b=2)
        rot = take(TT * 512).rearrange("p (t c) -> p t c", t=TT)
        retT = take(4 * S).rearrange("p (b s) -> p b s", b=4)
        ret_v = take(TT * S).rearrange("p (t c) -> p t c", t=TT)
        ret_g = take(TT * S).rearrange("p (t c) -> p t c", t=TT)
        ret_s = take(3 * 512).rearrange("p (j c) -> p j c", j=3)
        conv = take(2 * S).rearrange("p (b s) -> p b s", b=2)
        lru_r = take(2 * S).rearrange("p (b s) -> p b s", b=2)
        lru_i = take(2 * S).rearrange("p (b s) -> p b s", b=2)
        lru_a = take(2 * S).rearrange("p (b s) -> p b s", b=2)
        lru_t = take(2 * S).rearrange("p (b s) -> p b s", b=2)
        lru_h = take(2 * S).rearrange("p (b s) -> p b s", b=2)
        tanh_buf = take(2 * 512).rearrange("p (j c) -> p j c", j=2)
        early_end = used["a"]
        qT = take(4 * S).rearrange("p (r s) -> p r s", r=4)
        kT = take(2 * S).rearrange("p (b s) -> p b s", b=2)
        nsa_v = take(TT * 256).rearrange("p (t c) -> p t c", t=TT)
        nsa_gt = take(TT * 24).rearrange("p (t c) -> p t c", t=TT)
        nsa_g = take(TT * 512).rearrange("p (t c) -> p t c", t=TT)
        probs = take(3 * 512).rearrange("p (j c) -> p j c", j=3)
        cmp_s = take(TT * 8 * CMP_N).rearrange("p (t h n) -> p t h n", t=TT, h=8)
        probsT = take(2 * 512).rearrange("p (j c) -> p j c", j=2)
        cmpT = take(TT * 8 * P).rearrange("p (t h s) -> p t h s", t=TT, h=8)
        kcT = take(CMP_N)
        vc = take(P)
        y = take(TT * 768).rearrange("p (t c) -> p t c", t=TT)
        yT = take(KC * S).rearrange("p (k s) -> p k s", k=KC)
        ln_gb = take(2 * D).rearrange("p (j d) -> p j d", j=2)
        z = take(TT * D).rearrange("p (t d) -> p t d", t=TT)
        hc_x = z
        tmp_a = take(512)
        tmp_b = take(512)
        cond = [take(D).rearrange("p (k c) -> p k c", k=4), hT[:, 0:4, 0:S]]
        cond_tmp = [probs[:, 0:2, :].rearrange("p a (k c) -> p (a k) c", k=2),
                    y.rearrange("p t c -> p (t c)")[:, 0:D].rearrange("p (k c) -> p k c", k=4)]
        sq_out = hT[:, 4:8, 0:S]

        used["a"] = 0
        mkT = take(MH * 512).rearrange("p (h s) -> p h s", h=MH)
        mv = take(4 * 512).rearrange("p (t c) -> p t c", t=4)
        akv = take(4 * 256).rearrange("p (t c) -> p t c", t=4)
        gate_rows = take(2 * D).rearrange("p (m d) -> p m d", m=2)
        g_diag = take(D)
        rt_a = take(512)
        rt_b = take(512)
        assert used["a"] <= early_end
        aq = take(TT * 512).rearrange("p (t c) -> p t c", t=TT)
        probs2 = take(3 * 512).rearrange("p (j c) -> p j c", j=3)
        probs2T = take(2 * 512).rearrange("p (j c) -> p j c", j=2)
        hl = take(TT * D).rearrange("p (t d) -> p t d", t=TT)
        mqT = take(MH * S).rearrange("p (h s) -> p h s", h=MH)
        mo_t = take(TT * 512).rearrange("p (t c) -> p t c", t=TT)
        aqT = take(4 * S).rearrange("p (r s) -> p r s", r=4)
        akT = take(512)
        a_lat = aq
        aT = take(4 * S).rearrange("p (k s) -> p k s", k=4)
        norm_g = take(512)
        gates = take(8 * 512).rearrange("p (j c) -> p j c", j=8)
        rows_at = used["a"]
        take(8 * 512)
        rows = [arena[0:8, rows_at + j * 512:rows_at + (j + 1) * 512] for j in range(8)]
        m_lat = aqT.rearrange("p r s -> p (r s)").rearrange("p (t c) -> p t c", t=TT)
        dw = hl.rearrange("p t (j c) -> p (t j) c", j=2)
        mT = mkT[:, 0:2, :].rearrange("p a (b s) -> p (a b) s", b=2)
        mrg = arena[:, rows_at:rows_at + 2 * D].rearrange("p (t d) -> p t d", t=TT)
        mrgT = arena[:, rows_at + 2 * D:rows_at + 4 * D].rearrange("p (k s) -> p k s", k=KC)

        assert used["a"] <= ARENA
        used["a"] = 9 * D
        h2 = take(TT * D).rearrange("p (t d) -> p t d", t=TT)
        pqT = take(16 * S).rearrange("p (l s) -> p l s", l=16)
        score = take(TT * 16 * NKEY).rearrange("p (t l n) -> p t l n", t=TT, l=16)
        head_s = take(2 * NKEY)
        cand = take(TOPK * TOPK)
        hot, work = rt_b[:, 0:TOPK * TOPK], rt_b[:, TOPK * TOPK:2 * TOPK * TOPK]
        tops = take(2 * TOPK)
        topi = take(2 * TOPK).bitcast(U32)
        topf = take(2 * TOPK)
        best = take(TOPK)
        bexp = take(TOPK)
        bpos = take(TOPK).bitcast(U32)
        bhl = take(2 * TOPK).bitcast(U32)
        fhl = take(2 * TOPK)
        sel1 = take(TOPK)
        sel2 = take(TOPK)
        esum = take(4)
        idx_next = take(2 * TOPK).bitcast(I32)
        gate_next = take(2 * TOPK)
        idx_u = take(2 * TOPK).bitcast(I32)
        idx_v = take(2 * TOPK).bitcast(I32)
        dots = take(2 * TOPK)
        d_a = take(TOPK)
        d_b = take(TOPK)
        wcur = take(2 * TOPK)
        diag = take(4 * P).rearrange("p (j c) -> p j c", j=4)
        sk_tail = wring[:, (place_of_sk + 1) * SLOT - 2 * D:(place_of_sk + 1) * SLOT]
        rows_free = ([arena[:, r * D:(r + 1) * D] for r in range(6)] + [g_diag]
                     + [take(D) for _ in range(7)] + [sk_tail[:, r * D:(r + 1) * D] for r in range(2)])
        u_ring, v_ring = rows_free[:RING], rows_free[RING:]

        neg_max = take_small(4 * 2).rearrange("p (j b) -> p j b", j=4)
        sums = take_small(TT * 24).rearrange("p (t h b) -> p t h b", t=TT, h=8)
        gates3 = take_small(TT * 24).rearrange("p (t h b) -> p t h b", t=TT, h=8)
        coef = take_small(6)
        cmax = take_small(8)
        sp4 = take_small(DEPTH * 2)
        hbias = take_small(DEPTH * 4)
        stat = take_small(16)
        stat2 = take_small(16)
        var = take_small(16)
        rstd = take_small(16)
        bn = take_small(12).rearrange("p (j c) -> p j c", j=2)
        mvar = take_small(2)
        half8 = const[:, C_NEGHALF:C_NEGHALF + 8]
        sink = take_small(8)
        negsink = take_small(8)
        qk_g = take_small(2 * HD).rearrange("p (j d) -> p j d", j=2)
        nmA = take_small(TT * 8).rearrange("p (t h) -> p t h", t=TT)
        den = take_small(TT * 8).rearrange("p (t h) -> p t h", t=TT)
        es = take_small(8)
        fcol = take_small(2 * TT * 8).rearrange("p (d t c) -> p d t c", d=2, t=TT)
        mu = take_small(4)
        negmu = take_small(4)
        flo_in = take_small(4)
        flo_e = take_small(4)
        mden = take_small(4)
        mabs = take_small(4)
        mrec = take_small(4)
        wg2 = take_small(KC * 16).rearrange("p (k c) -> p k c", k=KC)
        modT = take_small(6 * KC * 2).rearrange("p (m k j) -> p m k j", m=6, k=KC)
        gate_tok = take_small(4 * 16).rearrange("p (t c) -> p t c", t=4)
        lam_a = take_small(4)
        lam_b = take_small(4)
        lam_c = take_small(4)
        lam_d = take_small(4)
        lam_e = take_small(4)
        lam_f = take_small(4)
        sumsq = take_small(8)

        jobs = {}
        count = {"rot": 0, "acc": 0}
        chunk_last = {}

        class Done:
            def __init__(self, bank, nth):
                self.bank, self.nth = bank, nth

        def full(eng, name):
            j = jobs[name]
            eng.wait_ge(bank_full[j.bank], j.nth + 1)
            return psum[j.bank]

        def free(ins, name):
            ins.then_inc(bank_free[jobs[name].bank], 1)

        def taken(eng, name):
            j = jobs[name]
            eng.wait_ge(bank_free[j.bank], j.nth + 1)

        w_full = [sem(f"w_full{s}") for s in range(NW)]

        def width(chunk):
            if chunk[0] == "w1" and chunk[2] == 4:
                return KC * 280
            if chunk[0] in ("w2", "w2c") and chunk[2] == 2:
                return KC * 256
            if chunk[0] == "sk":
                return 16 * NKEY
            return SLOT

        def slot(chunk):
            s = place[chunk][0]
            return wring[:, s * SLOT:s * SLOT + width(chunk)]

        block = ctx.enter_context(nc.Block())
        items = [(t, h) for t in range(TT) for h in range(8)]
        mitems = [(h, t) for h in range(MH) for t in range(TT)]

        @block.tensor
        def _(pe):
            def job(name, kind="rot"):
                n = count[kind]
                count[kind] += 1
                bank, nth = (n % NBANK, n // NBANK) if kind == "rot" else (NBANK + n % NACC, n // NACC)
                jobs[name] = Done(bank, nth)
                if nth:
                    pe.wait_ge(bank_free[bank], nth)
                return psum[bank]

            def finish(ins, name):
                ins.then_inc(bank_full[jobs[name].bank], 1)

            def weights(chunk):
                s, nth = place[chunk]
                pe.wait_ge(w_full[s], 16 * (nth + 1))
                return slot(chunk)

            def w_used(chunk, name):
                chunk_last[chunk] = name

            def project(name, lhs, w, cols):
                bank = job(name)
                n = len(lhs)
                for k in range(n):
                    ins = pe.matmul(bank[:, 0:cols], lhs[k], w[:, k, 0:cols], start=(k == 0), stop=(k == n - 1))
                finish(ins, name)

            def project_t(bank, at, w, col, rhs, n_tok):
                for k in range(KC):
                    ins = pe.matmul(bank[:, at:at + n_tok], w[:, k, col:col + P], rhs[:, k, :],
                                    start=(k == 0), stop=(k == KC - 1))
                return ins

            def context(n):
                if n < 4:
                    w = weights(("w2c", 0, 0)).rearrange("p (k c) -> p k c", k=KC)
                    bank = job(("mkc", n))
                    finish(project_t(bank, 0, w, n * P, hT[:, :, 0:S], S), ("mkc", n))
                    if n == 3:
                        w_used(("w2c", 0, 0), ("mkc", n))
                elif n < 8:
                    tt, half = divmod(n - 4, 2)
                    w = weights(("w2c", 0, 1)).rearrange("p (k c) -> p k c", k=KC)
                    project(("mvc", n), [hT[:, k, tt * P:(tt + 1) * P] for k in range(KC)], w[:, :, half * S:(half + 1) * S], S)
                    if n == 7:
                        w_used(("w2c", 0, 1), ("mvc", n))
                elif n < 10:
                    if n == 8:
                        pe.wait_ge(sem("in_small"), 64)
                    project(("wg", n - 8), [hT[:, k, (n - 8) * P:(n - 7) * P] for k in range(KC)], wg2, 16)
                else:
                    m, half = divmod(n - 10, 2)
                    pe.wait_ge(sem("g_diag"), m + 1)
                    bank = job(("gb", m, half))
                    finish(pe.matmul(bank[:, :], const[:, C_ONE:C_ONE + 1].to_broadcast([P, P]), g_diag[:, half * 512:(half + 1) * 512],
                                     start=True, stop=True), ("gb", m, half))

            def transposes(name, blocks):
                bank = job(name)
                for j, blk in enumerate(blocks):
                    rows_in = blk.ap[0][1]
                    cols = blk.ap[-1][1]
                    ins = pe.transpose(bank[0:cols, j * P:j * P + rows_in], blk, ident[0:rows_in, 0:rows_in])
                finish(ins, name)

            def row_blocks(name, src, t):
                for half in range(2):
                    transposes((name, t, half), [src[:, t, (4 * half + j) * P:(4 * half + j + 1) * P] for j in range(4)])

            pe.wait_ge(sem("in_ident"), 16)
            for layer in range(DEPTH):
                L = layer
                for t in range(TT):
                    if L == 0:
                        pe.wait_ge(sem(f"in_x{t}"), 16)
                    else:
                        pe.wait_ge(sem("x_next"), TT * (L - 1) + t + 1)
                    for half in range(2):
                        transposes(("xT", L, t, half),
                                   [x3[:, t, (4 * half + j) * P:(4 * half + j + 1) * P] for j in range(4)])
                    for half in range(2):
                        taken(pe, ("xT", L, t, half))
                    w = weights(("w1", L, 1)).rearrange("p (k c) -> p k c", k=KC)
                    project(("rqk", L, t), [xT[:, k, t * P:(t + 1) * P] for k in range(KC)], w, 512)
                w_used(("w1", L, 1), ("rqk", L, 1))
                w = weights(("w1", L, 0)).rearrange("p (k c) -> p k c", k=KC)
                for n, name in enumerate(("lx", "lg")):
                    bank = job((name, L))
                    for b in range(2):
                        ins = project_t(bank, b * S, w, (2 * n + b) * P, xT, S)
                    finish(ins, (name, L))
                w_used(("w1", L, 0), ("lg", L))
                w = weights(("w1", L, 2)).rearrange("p (k c) -> p k c", k=KC)
                for j in range(2):
                    bank = job(("q", L, j))
                    for b in range(2):
                        ins = project_t(bank, b * S, w, (2 * j + b) * P, xT, S)
                    finish(ins, ("q", L, j))
                w_used(("w1", L, 2), ("q", L, 1))
                w = weights(("w1", L, 3)).rearrange("p (k c) -> p k c", k=KC)
                for j, name in enumerate(("kcvc", "kskw")):
                    bank = job((name, L))
                    for b in range(2):
                        ins = project_t(bank, b * S, w, (2 * j + b) * P, xT, S)
                    finish(ins, (name, L))
                w_used(("w1", L, 3), ("kskw", L))
                if L == 0:
                    pe.wait_ge(sem("in_const"), 32)
                pe.wait_ge(sem("conv"), L + 1)
                for n, name in enumerate(("lr", "li")):
                    bank = job((name, L))
                    for b in range(2):
                        for s in range(2):
                            r = slice(s * HD, (s + 1) * HD)
                            at = V_WG + ((L * 2 + n) * 2 + b) * HD
                            ins = pe.matmul(bank[r, b * S:(b + 1) * S], par[r, at:at + HD], conv[r, b, :],
                                            start=True, stop=True)
                    finish(ins, (name, L))
                for c, name, cols in ((4, "vg", 280), (5, "rvg", 512), (6, "ng", 512)):
                    w = weights(("w1", L, c)).rearrange("p (k c) -> p k c", k=KC)
                    for t in range(TT):
                        project((name, L, t), [xT[:, k, t * P:(t + 1) * P] for k in range(KC)], w, cols)
                    w_used(("w1", L, c), (name, L, 1))
                for t in range(TT):
                    pe.wait_ge(sem("rot"), TT * L + t + 1)
                    transposes(("rT", L, t), [rot[:, t, j * P:(j + 1) * P] for j in range(4)])
                w = weights(("cmp", L, 0)).rearrange("p (b l e) -> p b l e", b=2, l=CMP_L)
                taken(pe, ("kcvc", L))
                bank = job(("kc", L))
                for g in range(2):
                    r = slice(g * HD, (g + 1) * HD)
                    for l in range(CMP_L):
                        ins = pe.matmul(bank[r, 0:CMP_N], w[r, 0, l, :], blocksT[r, 0, l, :],
                                        start=(l == 0), stop=(l == CMP_L - 1))
                finish(ins, ("kc", L))
                for g in range(2):
                    bank = job(("vc", L, g))
                    r = slice(g * HD, (g + 1) * HD)
                    for l in range(CMP_L):
                        ins = pe.matmul(bank[0:CMP_N, 0:HD], blocksT[r, 1, l, :], w[r, 1, l, :],
                                        start=(l == 0), stop=(l == CMP_L - 1))
                    finish(ins, ("vc", L, g))
                w_used(("cmp", L, 0), ("vc", L, 1))
                for t in range(TT):
                    taken(pe, ("rT", L, t))
                for j, (s, t) in enumerate(((0, 0), (0, 1), (1, 1))):
                    for odd in range(2):
                        bank = job(("rs", L, j, odd))
                        r = slice(odd * HD, (odd + 1) * HD)
                        for n in range(2):
                            ins = pe.matmul(bank[:, n * P:(n + 1) * P], retT[r, 2 + n, s * P:(s + 1) * P],
                                            retT[r, n, t * P:(t + 1) * P], start=True, stop=True)
                        finish(ins, ("rs", L, j, odd))
                taken(pe, ("kc", L))
                for j in range(2):
                    taken(pe, ("q", L, j))
                for t in range(TT):
                    for g in range(2):
                        bank = job(("nc", L, t, g))
                        r = slice(g * HD, (g + 1) * HD)
                        for h in range(4):
                            ins = pe.matmul(bank[:, h * CMP_N:(h + 1) * CMP_N], qT[r, h, t * P:(t + 1) * P],
                                            kcT[r, :], start=True, stop=True)
                        finish(ins, ("nc", L, t, g))
                for j in range(3):
                    for odd in range(2):
                        taken(pe, ("rs", L, j, odd))
                for t in range(TT):
                    taken(pe, ("rvg", L, t))
                    bank = job(("ro", L, t))
                    keys = ((0, 0),) if t == 0 else ((0, 1), (1, 2))
                    for h in range(4):
                        for n, (s, j) in enumerate(keys):
                            ins = pe.matmul(bank[:, h * HD:(h + 1) * HD], ret_s[:, j, h * P:(h + 1) * P],
                                            ret_v[:, s, h * HD:(h + 1) * HD],
                                            start=(n == 0), stop=(n == len(keys) - 1))
                    finish(ins, ("ro", L, t))
                for t in range(TT):
                    pe.wait_ge(sem("cmp_probs"), TT * L + t + 1)
                    for half in range(2):
                        bank = job(("cT", L, t, half))
                        for j in range(4):
                            ins = pe.transpose(bank[0:CMP_N, j * P:(j + 1) * P], cmp_s[:, t, 4 * half + j, :], ident)
                        finish(ins, ("cT", L, t, half))
                taken(pe, ("kskw", L))
                for g in range(2):
                    taken(pe, ("vc", L, g))
                for t in range(TT):
                    taken(pe, ("vg", L, t))
                    for half in range(2):
                        taken(pe, ("cT", L, t, half))

                def nsa_scores(i):
                    t, h = items[i]
                    nk = (t + 1) * P
                    r = slice((h // 4) * HD, (h // 4 + 1) * HD)
                    bank = job(("ns", L, i))
                    ins = pe.matmul(bank[:, 0:2 * nk].rearrange("p (b k) -> p b k", b=2),
                                    qT[r, h % 4, t * P:(t + 1) * P], kT[r, :, 0:nk], start=True, stop=True)
                    finish(ins, ("ns", L, i))

                def nsa_transposes(i):
                    t, h = items[i]
                    taken(pe, ("ns", L, i))
                    transposes(("nT", L, i), [probs[:, i % 3, j * P:(j + 1) * P] for j in range(2 * (t + 1))])

                def nsa_values(i):
                    t, h = items[i]
                    g = slice((h // 4) * HD, (h // 4 + 1) * HD)
                    if h % 2 == 0:
                        job(("no", L, i // 2), "acc")
                    bank = psum[jobs[("no", L, i // 2)].bank]
                    taken(pe, ("nT", L, i))
                    at = (h % 2) * 3 * HD
                    pe.matmul(bank[:, at:at + HD], cmpT[0:CMP_N, t, h, :], vc[0:CMP_N, g], start=True, stop=True)
                    for b in range(2):
                        for s in range(t + 1):
                            blk = b * (t + 1) + s
                            ins = pe.matmul(bank[:, at + (b + 1) * HD:at + (b + 2) * HD],
                                            probsT[:, i % 2, blk * P:(blk + 1) * P],
                                            nsa_v[:, s, b * P + g.start:b * P + g.stop],
                                            start=(s == 0), stop=(s == t))
                    if h % 2:
                        finish(ins, ("no", L, i // 2))

                nsa_scores(0)
                nsa_scores(1)
                if L == 0:
                    pe.wait_ge(sem("ctx_rows"), 2)
                    for t in range(TT):
                        row_blocks("hc", hc_x, t)
                else:
                    for t in range(TT):
                        for half in range(2):
                            taken(pe, ("hc", t, half))

                def mixed_transposes(t):
                    pe.wait_ge(sem("y_ret"), TT * L + t + 1)
                    transposes(("yT", L, t, 0), [y[:, t, j * P:(j + 1) * P] for j in range(2)])
                    pe.wait_ge(sem("y_nsa"), TT * L + t + 1)
                    transposes(("yT", L, t, 1), [y[:, t, (2 + j) * P:(3 + j) * P] for j in range(4)])

                for i in range(len(items)):
                    if i + 2 < len(items):
                        nsa_scores(i + 2)
                    if L == DEPTH - 1 and i >= 4:
                        context(i - 4)
                    if i == 10:
                        mixed_transposes(0)
                    if i >= 12:
                        if i == 12:
                            pe.wait_ge(sem("y_lru"), L + 1)
                            for half in range(2):
                                taken(pe, ("yT", L, 0, half))
                        half, q = divmod(i - 12, 2)
                        w = weights(("wo", L, half)).rearrange("p (k c) -> p k c", k=KC)
                        project(("wq", L, i - 12), [yT[:, k, 0:P] for k in range(KC)], w[:, :, q * S:(q + 1) * S], S)
                    nsa_transposes(i)
                    if i:
                        nsa_values(i - 1)
                nsa_values(len(items) - 1)
                mixed_transposes(1)
                for half in range(2):
                    taken(pe, ("yT", L, 1, half))
                for half in range(2):
                    w = weights(("wo", L, half)).rearrange("p (k c) -> p k c", k=KC)
                    project(("wo", L, half), [yT[:, k, P:2 * P] for k in range(KC)], w, 512)
                    w_used(("wo", L, half), ("wo", L, half))

                if L == DEPTH - 1:
                    context(12)
                    context(13)
                    w = weights(("w2c", 0, 2)).rearrange("p (k c) -> p k c", k=KC)
                    for tt in range(2):
                        project(("akv", tt), [hT[:, k, tt * P:(tt + 1) * P] for k in range(KC)], w, 256)
                    w_used(("w2c", 0, 2), ("akv", 1))

            hlT = hT[:, :, S:2 * S]
            w = weights(("w2", 0, 4)).rearrange("p (k c) -> p k c", k=KC)
            for t in range(TT):
                pe.wait_ge(sem("h_rows"), t + 1)
                row_blocks("hl", hl, t)
                for half in range(2):
                    taken(pe, ("hl", t, half))
                project(("aq", t), [hlT[:, k, t * P:(t + 1) * P] for k in range(KC)], w, 512)
            w_used(("w2", 0, 4), ("aq", 1))
            for tt in range(2, 4):
                project(("wg", tt), [hT[:, k, tt * P:(tt + 1) * P] for k in range(KC)], wg2, 16)
            w = weights(("w2", 0, 0)).rearrange("p (k c) -> p k c", k=KC)
            for j in range(2):
                bank = job(("mkl", j))
                for b in range(2):
                    ins = project_t(bank, b * S, w, (2 * j + b) * P, hlT, S)
                finish(ins, ("mkl", j))
            w_used(("w2", 0, 0), ("mkl", 1))
            for tt in range(4):
                taken(pe, ("wg", tt))
            for n, name in enumerate(("gi", "gf")):
                bank = job((name,))
                for tt in range(4):
                    ins = pe.transpose(bank[0:8, tt * P:(tt + 1) * P], gate_tok[:, tt, n * 8:(n + 1) * 8], ident)
                finish(ins, (name,))
            w = weights(("w2", 0, 1)).rearrange("p (k c) -> p k c", k=KC)
            for tt in range(2, 4):
                project(("mv", tt), [hT[:, k, tt * P:(tt + 1) * P] for k in range(KC)], w, 512)
            w_used(("w2", 0, 1), ("mv", 3))
            w = weights(("w2", 0, 2)).rearrange("p (k c) -> p k c", k=KC)
            for tt in range(2, 4):
                project(("akv", tt), [hT[:, k, tt * P:(tt + 1) * P] for k in range(KC)], w, 256)
            w_used(("w2", 0, 2), ("akv", 3))
            w = weights(("w2", 0, 3)).rearrange("p (k c) -> p k c", k=KC)
            for j in range(2):
                bank = job(("mq", j))
                for b in range(2):
                    ins = project_t(bank, b * S, w, (2 * j + b) * P, hlT, S)
                finish(ins, ("mq", j))
            w_used(("w2", 0, 3), ("mq", 1))
            w = weights(("w2", 0, 5)).rearrange("p (k c) -> p k c", k=KC)
            for t in range(TT):
                project(("mog", t), [hlT[:, k, t * P:(t + 1) * P] for k in range(KC)], w, 512)
            w_used(("w2", 0, 5), ("mog", 1))
            pe.wait_ge(sem("ak"), 1)
            transposes(("akT",), [akv[:, tt, 0:P] for tt in range(4)])
            for t in range(TT):
                pe.wait_ge(sem("aq"), t + 1)
                transposes(("aqT", t), [aq[:, t, j * P:(j + 1) * P] for j in range(4)])
            pe.wait_ge(sem("gate_rows"), 1)
            bank = job(("fc",))
            for d in range(2):
                for t in range(TT):
                    at = (d * TT + t) * 8
                    ins = pe.transpose(bank[:, at:at + 8], rows[3 + d][:, S + t * P:S + (t + 1) * P], ident[0:8, 0:8])
            finish(ins, ("fc",))
            taken(pe, ("akT",))
            taken(pe, ("aqT", 0))
            taken(pe, ("aqT", 1))

            def attn_scores(i):
                t, h = items[i]
                r = slice((h // 4) * HD, (h // 4 + 1) * HD)
                bank = job(("as", i))
                finish(pe.matmul(bank[:, :], aqT[r, h % 4, t * P:(t + 1) * P], akT[r, :], start=True, stop=True),
                       ("as", i))

            def attn_values(i):
                t, h = items[i]
                if h == 0:
                    job(("ao", t), "acc")
                bank = psum[jobs[("ao", t)].bank]
                taken(pe, ("aT_", i))
                for s in range(4):
                    at = P + (h // 4) * HD
                    ins = pe.matmul(bank[:, h * HD:(h + 1) * HD], probs2T[:, i % 2, s * P:(s + 1) * P],
                                    akv[:, s, at:at + HD], start=(s == 0), stop=(s == 3))
                if h == 7:
                    finish(ins, ("ao", t))

            def branch_gate(n):
                c, t, q = n // 4, (n // 2) % 2, n % 2
                w = weights(("w2", 0, 6 + c)).rearrange("p (k c) -> p k c", k=KC)
                project(("gate", n), [hlT[:, k, t * P:(t + 1) * P] for k in range(KC)], w[:, :, q * S:(q + 1) * S], S)
                if n % 4 == 3:
                    w_used(("w2", 0, 6 + c), ("gate", n))

            def branch(name, src, half, t):
                wb = weights(("br", 0, half)).rearrange("p (k c) -> p k c", k=KC)
                k0 = 0 if name == "bm" else 4
                project((name, half, t), [src[:, k, t * P:(t + 1) * P] for k in range(4)], wb[:, k0:k0 + 4, :], 512)

            attn_scores(0)
            attn_scores(1)
            for i in range(len(items)):
                if i + 2 < len(items):
                    attn_scores(i + 2)
                if 2 <= i < 14:
                    branch_gate(i - 2)
                taken(pe, ("as", i))
                transposes(("aT_", i), [probs2[:, i % 3, j * P:(j + 1) * P] for j in range(4)])
                if i:
                    attn_values(i - 1)
            attn_values(len(items) - 1)

            for n in range(4):
                taken(pe, ("mkc", n))
                taken(pe, ("mvc", 4 + n))
            for j in range(2):
                taken(pe, ("mkl", j))
                taken(pe, ("mv", 2 + j))
                taken(pe, ("mq", j))

            def key_rows(h):
                for d in range(2):
                    c = d * 4 + h
                    bank = job(("G", d, h))
                    finish(pe.matmul(bank[:, :], ident[0:8, c:c + 1].to_broadcast([8, P]), rows[5 + d],
                                     start=True, stop=True), ("G", d, h))

            def mlstm_scores(h):
                for t in range(TT):
                    bank = job(("qk", h, t))
                    finish(pe.matmul(bank[:, :], mqT[:, h, t * P:(t + 1) * P], mkT[:, h, :], start=True, stop=True),
                           ("qk", h, t))

            def mlstm_values(i):
                h, t = mitems[i]
                pe.wait_ge(sem("mlstm_s"), i + 1)
                transposes(("mT_", i), [probs2[:, i % 2, j * P:(j + 1) * P] for j in range(4)])
                if h == 0:
                    job(("mo", t), "acc")
                bank = psum[jobs[("mo", t)].bank]
                taken(pe, ("mT_", i))
                for s in range(4):
                    ins = pe.matmul(bank[:, h * P:(h + 1) * P], probs2T[:, i % 2, s * P:(s + 1) * P],
                                    mv[:, s, h * P:(h + 1) * P], start=(s == 0), stop=(s == 3))
                if h == MH - 1:
                    finish(ins, ("mo", t))

            key_rows(0)
            mlstm_scores(0)
            for h in range(MH):
                if h + 1 < MH:
                    key_rows(h + 1)
                for t in range(TT):
                    i = TT * h + t
                    if i < 4:
                        branch_gate(12 + i)
                    else:
                        if i == 4:
                            taken(pe, ("aT", 0))
                            taken(pe, ("aT", 1))
                        branch("ba", aT, (i - 4) // 2, i % 2)
                    if i == 1:
                        for t_ in range(TT):
                            taken(pe, ("ao", t_))
                            transposes(("aT", t_), [a_lat[:, t_, j * P:(j + 1) * P] for j in range(4)])
                    mlstm_values(i)
                if h + 1 < MH:
                    mlstm_scores(h + 1)
            for t in range(TT):
                pe.wait_ge(sem("m_lat"), t + 1)
                transposes(("mT", t), [m_lat[:, t, j * P:(j + 1) * P] for j in range(4)])
            for t in range(TT):
                taken(pe, ("mT", t))
            for half in range(2):
                for t in range(TT):
                    branch("bm", mT, half, t)
                w_used(("br", 0, half), ("bm", half, 1))
            for t in range(TT):
                for half in range(2):
                    pe.wait_ge(sem("mrg"), half * TT + t + 1)
                    transposes(("gT", t, half), [mrg[:, t, (4 * half + j) * P:(4 * half + j + 1) * P] for j in range(4)])
            for t in range(TT):
                for half in range(2):
                    taken(pe, ("gT", t, half))
            for t in range(TT):
                for half in range(2):
                    w = weights(("wo2", 0, half)).rearrange("p (k c) -> p k c", k=KC)
                    project(("wo2", half, t), [mrgT[:, k, t * P:(t + 1) * P] for k in range(KC)], w, 512)
                    if t == 1 and half == 0:
                        pe.wait_ge(sem("h_rows"), 3)
                        row_blocks("pT", h2, 0)
            for half in range(2):
                w_used(("wo2", 0, half), ("wo2", half, 1))
            sub = weights(("sk", 0, 0)).rearrange("p (l n) -> p l n", l=16)

            def key_scores(t, j):
                bank = job(("ps", t, j))
                for b in range(4):
                    ins = pe.matmul(bank[:, b * P:(b + 1) * P], pqT[:, 4 * j + b, t * P:(t + 1) * P],
                                    sub[:, 4 * j + b, :], start=True, stop=True)
                finish(ins, ("ps", t, j))

            w = weights(("pq", 0, 0)).rearrange("p (k c) -> p k c", k=KC)
            for t in range(TT):
                if t:
                    pe.wait_ge(sem("h_rows"), 4)
                    row_blocks("pT", h2, t)
                for half in range(2):
                    taken(pe, ("pT", t, half))
                bank = job(("pq0", t))
                for b in range(4):
                    ins = project_t(bank, b * P, w, b * P, xT[:, :, t * P:(t + 1) * P], P)
                finish(ins, ("pq0", t))
                taken(pe, ("pq0", t))
                if t == 0:
                    key_scores(0, 0)
            w_used(("pq", 0, 0), ("pq0", 1))
            for t in range(TT):
                for half in range(2):
                    transposes(("h2", t, half), [xT[:, 4 * half + j, t * P:(t + 1) * P] for j in range(4)])
            for c in range(1, 4):
                w = weights(("pq", 0, c)).rearrange("p (k c) -> p k c", k=KC)
                for j in range(2):
                    bank = job(("pq", 2 * c + j))
                    for b in range(2):
                        ins = project_t(bank, b * S, w, (2 * j + b) * P, xT, S)
                    finish(ins, ("pq", 2 * c + j))
                w_used(("pq", 0, c), ("pq", 2 * c + 1))
                for j in range(2):
                    taken(pe, ("pq", 2 * c + j))
                key_scores(0, c)
            for c in range(4):
                key_scores(1, c)
            w_used(("sk", 0, 0), ("ps", 1, 3))
            for t in range(TT):
                for half in range(2):
                    taken(pe, ("h2", t, half))
            for t in range(TT):
                sums_of = [job(("pv", t, half)) for half in range(2)]
                for half in range(2):
                    pe.matmul(sums_of[half][:, :], const[0:1, C_ZERO:C_ZERO + P], h2[0:1, t, half * 512:(half + 1) * 512],
                              start=True, stop=False)
                with pe.Fori(0, EH // 2) as it:
                    for n in range(2 * TOPK):
                        at = t * EH * TOPK + n
                        pe.wait_ge(sem(f"v_full{n % RING}"), it * (16 * 2 * TOPK // RING) + 16 * (at // RING + 1))
                        pe.wait_ge(sem("diag_ready"), it * (2 * TOPK) + (CREDIT + at + 1))
                        for half in range(2):
                            ins = pe.matmul(sums_of[half][:, :], diag[:, n % 4, :], v_ring[n % RING][:, half * 512:(half + 1) * 512],
                                            start=False, stop=False, skip_group_check=True)
                        ins.then_inc(sem("v_used"), 1)
                for half in range(2):
                    finish(pe.matmul(sums_of[half][:, :], const[0:1, C_ZERO:C_ZERO + P], h2[0:1, t, half * 512:(half + 1) * 512],
                                     start=False, stop=True), ("pv", t, half))

        @block.sync
        def _(sp):
            sp.dma_start(ident, a["const"][:, C_ID:C_ID + P]).then_inc(sem("in_ident"), 16)
            for t in range(TT):
                sp.dma_start(x3[:, t, :], a["x"][t * P:(t + 1) * P, :]).then_inc(sem(f"in_x{t}"), 16)
            for chunk in chunks:
                s, nth = place[chunk]
                if chunk[0] == "kept":
                    continue
                if nth:
                    last = chunks[chunks.index(chunk) - NW]
                    if last[0] == "ada":
                        sp.wait_ge(sem("ada_used"), last[2] + 1)
                    else:
                        full(sp, chunk_last[last])
                kind, L, c = chunk
                dst = slot(chunk)
                src = {"cmp": lambda: a["cmp"][L], "w1": lambda: a["w1b"][L] if c == 4 else a["w1"][L, c if c < 4 else c - 1],
                       "wo": lambda: a["wo"][L, c], "ada": lambda: a["ada"][ADA_ORDER[c]],
                       "w2": lambda: a["w2b"] if c == 2 else a["w2"][c if c < 2 else c - 1],
                       "w2c": lambda: a["w2b"] if c == 2 else a["w2"][c],
                       "br": lambda: a["br"][c], "wo2": lambda: a["wo2"][c], "pq": lambda: a["pq"][c],
                       "sk": lambda: a["sk"]}[kind]()
                sp.dma_start(dst, src).then_inc(w_full[s], 16)
                if kind == "w1" and c == 3:
                    if L:
                        sp.wait_ge(sem("x_next"), TT * L)
                    for j, name in enumerate(("ln_g", "ln_b")):
                        sp.dma_start(ln_gb[:, j, :], a[name][L:L + 1, :].to_broadcast([P, D])).then_inc(sem("in_ln"), 16)
                if chunk == ("w1", 0, 1):
                    sp.dma_start(par[:, :], a["par"]).then_inc(sem("in_const"), 16)
                    sp.dma_start(const[:, P:], a["const"][:, P:]).then_inc(sem("in_const"), 16)
                if chunk == ("w1", 0, 2):
                    sp.dma_start(wg2, a["wg2"]).then_inc(sem("in_small"), 16)
                    sp.dma_start(sink, a["sink"].to_broadcast([P, 8])).then_inc(sem("in_small"), 16)
                    sp.dma_start(qk_g[:, 0, :], a["q_g"].to_broadcast([P, HD])).then_inc(sem("in_small"), 16)
                    sp.dma_start(qk_g[:, 1, :], a["k_g"].to_broadcast([P, HD])).then_inc(sem("in_small"), 16)
                    for j in range(2):
                        sp.dma_start(cond[j], a["cond"][j:j + 1, :].to_broadcast([P, D]).rearrange("p (k c) -> p k c", k=4)
                                     ).then_inc(sem("in_cond"), 16)
                    sp.dma_start(hc_x, a["ctx"].rearrange("(t p) d -> p t d", p=P)).then_inc(sem("in_ctx"), 16)
                if chunk == ("w2", 0, 3):
                    sp.wait_ge(sem("x_next"), TT * DEPTH)
                    sp.dma_start(norm_g, a["norm_g"].to_broadcast([P, 512])).then_inc(sem("in_norm_g"), 16)
            for t in range(TT):
                sp.wait_ge(sem("result"), t + 1)
                sp.dma_start(out[t * P:(t + 1) * P, :], x3[:, t, :]).then_inc(sem("stored"), 16)
            sp.wait_ge(sem("stored"), 16 * TT)

        @block.scalar
        def _(act):
            def link(ins, name, counts={}):
                counts[name] = counts.get(name, 0) + 1
                ins.then_inc(sem(name), 1)
                act.wait_ge(sem(name), counts[name])

            def copy(dst, src, scale=1.0):
                return act.activation(dst, src, ACT.Copy, scale=scale)

            def gate_columns(tt):
                bank = full(act, ("wg", tt))
                free(copy(gate_tok[:, tt, :], bank[:, 0:16]), ("wg", tt))

            def modulated(name, t, half, shift, j, at):
                bank = full(act, (name, t, half))
                for b in range(4):
                    k = 4 * half + b
                    ins = act.activation(hT[:, k, at + t * P:at + (t + 1) * P], bank[:, b * P:(b + 1) * P], ACT.Identity,
                                         scale=modT[:, shift + 1, k, j:j + 1], bias=modT[:, shift, k, j:j + 1])
                free(ins, (name, t, half))

            def gate_diagonal(m):
                if m == 0:
                    act.wait_ge(sem("ada_bias"), 3)
                for k in range(KC):
                    ins = copy(g_diag[:, k * P:(k + 1) * P], ident, modT[:, 3 * m + 2, k, 0:1])
                ins.then_inc(sem("g_diag"), 1)

            def context(n):
                if n < 4:
                    bank = full(act, ("mkc", n))
                    free(copy(mkT[:, n, 0:S], bank[:, 0:S], K_SCALE), ("mkc", n))
                elif n < 8:
                    tt, half = divmod(n - 4, 2)
                    bank = full(act, ("mvc", n))
                    free(copy(mv[:, tt, half * S:(half + 1) * S], bank[:, 0:S]), ("mvc", n))
                    if n == 7:
                        gate_diagonal(0)
                elif n < 10:
                    gate_columns(n - 8)
                else:
                    m, half = divmod(n - 10, 2)
                    bank = full(act, ("gb", m, half))
                    free(copy(gate_rows[:, m, half * 512:(half + 1) * 512], bank[:, :]), ("gb", m, half))
                    if n == 11:
                        gate_diagonal(1)

            def branch_gate(n):
                bank = full(act, ("gate", n))
                free(act.activation(gates[:, n // 2, (n % 2) * S:(n % 2 + 1) * S], bank[:, 0:S], ACT.Tanh, scale=0.5), ("gate", n))

            for L in range(DEPTH):
                for t in range(TT):
                    bank = full(act, ("xT", L, t, 0))
                    free(copy(xT[:, 0:4, t * P:(t + 1) * P], bank[:, :].rearrange("p (j s) -> p j s", j=4)), ("xT", L, t, 0))
                if L == 0:
                    act.wait_ge(sem("lam_abs"), 1)
                    act.activation(lam_c, lam_b, ACT.Exp, scale=-1.0).then_inc(sem("lam_exp"), 1)
                    act.wait_ge(sem("in_cond"), 32)
                    for j in range(2):
                        act.activation(cond_tmp[j], cond[j], ACT.Tanh, scale=0.5).then_inc(sem("cond_tanh"), 1)
                    act.wait_ge(sem("lru_pad"), 1)
                bank = full(act, ("lx", L))
                free(copy(lru_x[:, :, 3:3 + S], bank[:, :].rearrange("p (b s) -> p b s", b=2)), ("lx", L))
                bank = full(act, ("lg", L))
                act.activation(tanh_buf[:, 0, :], bank[:, :], ACT.Tanh, scale=0.5).then_inc(sem("lg_tanh"), 1)
                for j in range(2):
                    bank = full(act, ("q", L, j))
                    free(copy(qT[:, 2 * j:2 * j + 2, :], bank[:, :].rearrange("p (b s) -> p b s", b=2), HD ** -0.5), ("q", L, j))
                bank = full(act, ("kskw", L))
                free(copy(kT, bank[:, :].rearrange("p (b s) -> p b s", b=2)), ("kskw", L))
                for name, dst, col in (("lr", lru_r, 0), ("li", lru_i, 2)):
                    bank = full(act, (name, L))
                    for b in range(2):
                        ins = act.activation(dst[:, b, :], bank[:, b * S:(b + 1) * S], ACT.Tanh, scale=0.5,
                                             bias=hbias[:, L * 4 + col + b:L * 4 + col + b + 1])
                    free(ins, (name, L))
                for t in range(TT):
                    bank = full(act, ("vg", L, t))
                    copy(nsa_v[:, t, :], bank[:, 0:256])
                    free(act.activation(nsa_gt[:, t, :], bank[:, 256:280], ACT.Tanh, scale=0.5), ("vg", L, t))
                if L == 0:
                    act.wait_ge(sem("in_ctx"), 16)
                    for t in range(TT):
                        act.activation(sq_out, hc_x[:, t, :].rearrange("p (k c) -> p k c", k=4), ACT.Square,
                                       accum_out=sumsq[:, t:t + 1]).then_inc(sem("rms_sq"), 1)
                        act.wait_ge(sem("rms_sq"), t + 1)
                act.wait_ge(sem("lru_la"), L + 1)
                act.activation(lru_a, lru_r, ACT.Exp).then_inc(sem("lru_a"), 1)
                act.activation(lru_t, lru_r, ACT.Tanh).then_inc(sem("lru_a"), 1)
                for t in range(TT):
                    bank = full(act, ("rvg", L, t))
                    copy(ret_v[:, t, :], bank[:, 0:S])
                    if t:
                        taken(act, ("lg", L))
                    act.activation(tanh_buf[:, 1 - t, 0:S], bank[:, S:2 * S], ACT.Tanh, scale=0.5).then_inc(sem("rg_tanh"), 1)
                for t in range(TT):
                    bank = full(act, ("ng", L, t))
                    taken(act, ("rvg", L, t))
                    act.activation(tanh_buf[:, 1 - t, :], bank[:, :], ACT.Tanh, scale=0.5).then_inc(sem("ng_tanh"), 1)
                for t in range(TT):
                    bank = full(act, ("rT", L, t))
                    free(copy(retT[:, :, t * P:(t + 1) * P], bank[:, :].rearrange("p (j s) -> p j s", j=4)), ("rT", L, t))
                act.wait_ge(sem("lru_v"), L + 1)
                act.activation(lru_t, lru_t, ACT.Sqrt).then_inc(sem("lru_sq"), 1)
                bank = full(act, ("kc", L))
                free(copy(kcT, bank[:, 0:CMP_N]), ("kc", L))
                for g in range(2):
                    bank = full(act, ("vc", L, g))
                    free(copy(vc[0:CMP_N, g * HD:(g + 1) * HD], bank[0:CMP_N, 0:HD]), ("vc", L, g))
                for t in range(TT):
                    act.wait_ge(sem("cmp_sub"), TT * L + t + 1)
                    act.activation(cmp_s[:, t, :, :], cmp_s[:, t, :, :], ACT.Exp).then_inc(sem("cmp_probs"), 1)
                for t in range(TT):
                    for half in range(2):
                        bank = full(act, ("cT", L, t, half))
                        free(copy(cmpT[0:CMP_N, t, 4 * half:4 * half + 4, :],
                                  bank[0:CMP_N, :].rearrange("p (j s) -> p j s", j=4)), ("cT", L, t, half))

                def exps(i):
                    t, h = items[i]
                    nk = (t + 1) * P
                    bank = full(act, ("ns", L, i))
                    act.wait_ge(sem("nsa_max"), 16 * L + i + 1)
                    for b in range(2):
                        ins = act.activation(probs[:, i % 3, b * nk:(b + 1) * nk], bank[:, b * nk:(b + 1) * nk],
                                             ACT.Exp, bias=neg_max[:, i % 4, b:b + 1],
                                             accum_out=sums[:, t, h, b + 1:b + 2])
                    free(ins, ("ns", L, i))

                def mixed_transposed(t):
                    for half, (k0, n) in enumerate(((0, 2), (2, 4))):
                        bank = full(act, ("yT", L, t, half))
                        free(copy(yT[:, k0:k0 + n, t * P:(t + 1) * P],
                                  bank[:, 0:n * P].rearrange("p (j s) -> p j s", j=n)), ("yT", L, t, half))

                exps(0)
                exps(1)
                if L == 0:
                    act.wait_ge(sem("mix_gain"), 1)
                    for t in range(TT):
                        modulated("hc", t, 0, 0, 1, 0)
                for i in range(len(items)):
                    if i + 2 < len(items):
                        exps(i + 2)
                    if L == DEPTH - 1 and i >= 4:
                        if i == 4:
                            act.wait_ge(sem("y_lru"), DEPTH)
                            act.wait_ge(sem("y_ret"), TT * DEPTH)
                        context(i - 4)
                    if i == 10:
                        mixed_transposed(0)
                    if i % 2:
                        bank = full(act, ("nT", L, i))
                        n = 2 * (items[i][0] + 1) * P
                        free(copy(probsT[:, 1, 0:n], bank[:, 0:n]), ("nT", L, i))
                mixed_transposed(1)
                if L == DEPTH - 1:
                    context(12)
                    context(13)
                    for tt in range(2):
                        bank = full(act, ("akv", tt))
                        free(copy(akv[:, tt, :], bank[:, 0:256]), ("akv", tt))

            for t in range(TT):
                act.wait_ge(sem("x_next"), TT * (DEPTH - 1) + t + 1)
                act.activation(hl[:, t, :], x3[:, t, :], ACT.Square, accum_out=sumsq[:, 2 + t:3 + t]).then_inc(sem("rms_sq"), 1)
                if t == 1:
                    modulated("hl", 0, 0, 0, 0, S)
            modulated("hl", 1, 0, 0, 0, S)
            for tt in range(2, 4):
                gate_columns(tt)
            for j in range(2):
                bank = full(act, ("mkl", j))
                free(copy(mkT[:, 2 * j:2 * j + 2, S:2 * S], bank[:, :].rearrange("p (b s) -> p b s", b=2), K_SCALE), ("mkl", j))
            for n, name in enumerate(("gi", "gf")):
                bank = full(act, (name,))
                free(act.activation(rows[n], bank[0:8, :], ACT.Identity, bias=par[0:8, V_MG + n:V_MG + n + 1]), (name,))
            taken(act, ("gf",))
            link(act.activation(rt_a[0:8, :], rows[1], ACT.Abs), "fgate_abs")
            act.activation(rt_a[0:8, :], rt_a[0:8, :], ACT.Exp, scale=-1.0).then_inc(sem("fgate_exp"), 1)
            for tt in range(2, 4):
                bank = full(act, ("mv", tt))
                free(copy(mv[:, tt, :], bank[:, :]), ("mv", tt))
            for j in range(2):
                bank = full(act, ("mq", j))
                free(copy(mqT[:, 2 * j:2 * j + 2, :], bank[:, :].rearrange("p (b s) -> p b s", b=2)), ("mq", j))
            for t in range(TT):
                bank = full(act, ("mog", t))
                free(act.activation(mo_t[:, t, :], bank[:, :], ACT.Tanh, scale=0.5), ("mog", t))
            bank = full(act, ("akT",))
            free(copy(akT, bank[:, :]), ("akT",))
            for t in range(TT):
                bank = full(act, ("aqT", t))
                free(copy(aqT[:, :, t * P:(t + 1) * P], bank[:, :].rearrange("p (j s) -> p j s", j=4)), ("aqT", t))
            bank = full(act, ("fc",))
            free(copy(fcol.rearrange("p d t c -> p (d t c)"), bank[:, 0:2 * TT * 8]), ("fc",))

            def attn_exp(i):
                t, h = items[i]
                bank = full(act, ("as", i))
                act.wait_ge(sem("attn_max"), i + 1)
                free(act.activation(probs2[:, i % 3, :], bank[:, :], ACT.Exp, bias=nmA[:, t, h:h + 1],
                                    accum_out=den[:, t, h:h + 1]), ("as", i))

            attn_exp(0)
            attn_exp(1)
            for i in range(len(items)):
                if i + 2 < len(items):
                    attn_exp(i + 2)
                if 2 <= i < 14:
                    branch_gate(i - 2)
                if i % 2:
                    bank = full(act, ("aT_", i))
                    free(copy(probs2T[:, 1, :], bank[:, :]), ("aT_", i))
                if i % 8 == 7:
                    t = i // 8
                    act.wait_ge(sem("sink_sub"), t + 1)
                    act.activation(es, es, ACT.Exp).then_inc(sem("sink_exp"), 1)
            for h in range(MH):
                act.wait_ge(sem("mlstm_mu"), h + 1)
                for j in range(4):
                    act.activation(dw[:, j, :], dw[:, j, :], ACT.Exp, bias=negmu[:, j:j + 1]).then_inc(sem("mlstm_w"), 1)
                act.activation(flo_e, flo_in, ACT.Exp).then_inc(sem("mlstm_w"), 1)
                for t in range(TT):
                    i = TT * h + t
                    if i < 4:
                        branch_gate(12 + i)
                    if i == 1:
                        for t_ in range(TT):
                            bank = full(act, ("aT", t_))
                            free(copy(aT[:, :, t_ * P:(t_ + 1) * P], bank[:, :].rearrange("p (j s) -> p j s", j=4)), ("aT", t_))
                    bank = full(act, ("mT_", i))
                    free(copy(probs2T[:, i % 2, :], bank[:, :]), ("mT_", i))
            for t in range(TT):
                bank = full(act, ("mo", t))
                act.activation(dw[:, t, :], bank[:, :], ACT.Square).then_inc(sem("mlstm_sq"), 1)
            for t in range(TT):
                bank = full(act, ("mT", t))
                free(copy(mT[:, :, t * P:(t + 1) * P], bank[:, :].rearrange("p (j s) -> p j s", j=4)), ("mT", t))
            for t in range(TT):
                bank = full(act, ("gT", t, 0))
                free(copy(mrgT[:, 0:4, t * P:(t + 1) * P], bank[:, :].rearrange("p (j s) -> p j s", j=4)), ("gT", t, 0))
            for t in range(TT):
                act.wait_ge(sem("x1"), t + 1)
                act.activation(h2[:, t, :], x3[:, t, :], ACT.Square, accum_out=sumsq[:, t:t + 1]).then_inc(sem("rms_sq"), 1)
                if t == 1:
                    modulated("pT", 0, 0, 3, 0, S)

            def key_scores(t, j):
                bank = full(act, ("ps", t, j))
                free(copy(score[:, t, 4 * j:4 * j + 4, :], bank[:, :].rearrange("p (b n) -> p b n", b=4)), ("ps", t, j))
                taken(act, ("ps", t, j))
                act.sem_inc(sem("scores"), 1)

            def choice_exp(n):
                act.wait_ge(sem("top_sub"), n + 1)
                act.activation(bexp, best, ACT.Exp, bias=esum[:, 0:1], accum_out=esum[:, 1:2]).then_inc(sem("top_exp"), 1)

            for t in range(TT):
                if t:
                    modulated("pT", t, 0, 3, 0, S)
                    modulated("pT", t, 1, 3, 0, S)
                bank = full(act, ("pq0", t))
                free(copy(pqT[:, 0:4, t * P:(t + 1) * P], bank[:, :].rearrange("p (b s) -> p b s", b=4)), ("pq0", t))
                if t == 0:
                    key_scores(0, 0)
            for t in range(TT):
                for half in range(2):
                    bank = full(act, ("h2", t, half))
                    free(copy(h2[:, t, half * 512:(half + 1) * 512], bank[:, :]), ("h2", t, half))
            for c in range(1, 4):
                if c < 3:
                    choice_exp(c - 1)
                for j in range(2 * c, 2 * c + 2):
                    bank = full(act, ("pq", j))
                    free(copy(pqT[:, 2 * j:2 * j + 2, :], bank[:, :].rearrange("p (b s) -> p b s", b=2)), ("pq", j))
                key_scores(0, c)
            for c in range(4):
                key_scores(1, c)
            act.sem_inc(sem("diag_ready"), CREDIT)
            def expert_head(it, head, more):
                s = head % 2
                act.wait_ge(sem("gelu_in"), it * 2 + (head + 1))
                act.activation(d_b, d_a, ACT.Tanh).then_inc(sem("gelu_tanh"), 1)
                if more:
                    act.wait_ge(sem("top_sub"), it * 2 + (head + 3))
                    act.activation(bexp, best, ACT.Exp, bias=esum[:, 0:1], accum_out=esum[:, 1:2]).then_inc(sem("top_exp"), 1)
                act.wait_ge(sem("w_ready"), it * 2 + (head + 1))
                for r in range(TOPK):
                    at = head * TOPK + r
                    act.wait_ge(sem("v_used"), it * (2 * TOPK) + (CREDIT + at + 1 - 4))
                    act.activation(diag[:, r % 4, :], ident, ACT.Copy, scale=wcur[:, s * TOPK + r:s * TOPK + r + 1]
                                   ).then_inc(sem("diag_ready"), 1)

            with act.Fori(0, TT * EH // 2 - 1) as it:
                for s in range(2):
                    expert_head(it, s, True)
            for s in range(2):
                expert_head(0, TT * EH - 2 + s, False)

        @block.vector
        def _(dve):
            counts = {}

            def link(ins, name="dve_step"):
                counts[name] = counts.get(name, 0) + 1
                ins.then_inc(sem(name), 1)
                dve.wait_ge(sem(name), counts[name])

            def tt(o, p, q, op):
                return dve.tensor_tensor(o, p, q, op)

            def ts(o, p, s1, op0, s2=None, op1=None):
                if op1 is None:
                    return dve.tensor_scalar(o, p, s1, None, op0)
                return dve.tensor_scalar(o, p, s1, s2, op0, op1)

            def stt(o, p, s, q, op0, op1):
                return dve.scalar_tensor_tensor(o, p, s, q, op0, op1)

            def inverse_root(cols):
                dve.sem_inc(sem("var_ready"), 1)
                root_back()

            def root_back():
                counts["root"] = counts.get("root", 0) + 1
                dve.wait_ge(sem("root_done"), counts["root"])

            def log1p_half(e, s, s2, yv):
                link(ts(s, e, 2.0, ALU.add))
                link(dve.reciprocal(s, s))
                link(tt(s, e, s, ALU.mult))
                link(tt(s2, s, s, ALU.mult))
                link(ts(yv, s2, ATANH[-1], ALU.mult))
                for c in reversed(ATANH[:-1]):
                    link(stt(yv, yv, c, s2, ALU.add, ALU.mult))
                link(stt(yv, yv, 1.0, s, ALU.add, ALU.mult))

            link(dve.memset(lru_x[:, :, 0:3], 0.0), "lru_pad")
            def preamble():
                dve.wait_ge(sem("in_const"), 32)
                lru_par = par[:, V_LRU:V_LRU + DEPTH * 16].rearrange("p (l c) -> p l c", l=DEPTH)
                lam = lru_par[:, :, 14:16]

                def lb(v):
                    return v.rearrange("p (l b) -> p l b", l=DEPTH)

                link(ts(lb(lam_a), lam, -1.0, ALU.mult))
                link(tt(lb(lam_b), lb(lam_a), lam, ALU.max), "lam_abs")
                link(ts(hbias.rearrange("p (l b) -> p l b", l=DEPTH), lru_par[:, :, 10:14], 0.5, ALU.mult))
                dve.wait_ge(sem("lam_exp"), 1)
                log1p_half(lam_c, lam_d, lam_e, lam_f)
                link(ts(lam_a, lam_a, 0.0, ALU.max))
                link(stt(lam_a, lam_f, 2.0, lam_a, ALU.mult, ALU.add))
                link(ts(sp4, lam_a, -LRU_C / 2, ALU.mult))

            def modulation(n):
                c = ADA_ORDER[n]
                w_slot, nth = place[("ada", 0, n)]
                dve.wait_ge(w_full[w_slot], 16 * (nth + 1))
                w = slot(("ada", 0, n)).rearrange("p (b k c) -> p b k c", b=4, k=4)
                for b in range(4):
                    m, k = divmod(4 * c + b, KC)
                    for j in (1, 0) if m < 2 else (0,):
                        out_ = cond_tmp[0] if j else w[:, b]
                        ins = dve.tensor_tensor_reduce(out=out_, in0=w[:, b], in1=cond[j], scale=1.0, scalar=0.0, op0=ALU.mult,
                                                       op1=ALU.add, accum_out=modT[:, m, k, j:j + 1])
                        if j:
                            link(ins)
                link(ins, "ada_used")

            def add_bias(m0, m1):
                bias = par[:, V_ADA + m0 * KC:V_ADA + m1 * KC]
                v = modT[:, m0:m1, :, :].rearrange("p m k j -> p (m k) j")
                if m0 < 2:
                    link(stt(v, v, 0.5, every(bias, 2, 2), ALU.mult, ALU.add), "ada_bias")
                else:
                    link(stt(v[:, :, 0], v[:, :, 0], 0.5, bias, ALU.mult, ALU.add), "ada_bias")

            def gain(m, at, name):
                n = 2 if m < 2 else 1
                link(stt(modT[:, m, :, 0:n], modT[:, m, :, 0:n], 1.0, every(par[:, at:at + KC], n, 2), ALU.add, ALU.mult), name)

            def modulated(name, t, half, shift, j, at):
                bank = full(dve, (name, t, half))
                for b in range(4):
                    k = 4 * half + b
                    ins = ts(hT[:, k, at + t * P:at + (t + 1) * P], bank[:, b * P:(b + 1) * P], modT[:, shift + 1, k, j:j + 1], ALU.mult,
                             modT[:, shift, k, j:j + 1], ALU.add)
                free(ins, (name, t, half))

            def rope(dst, src, n, cos, sin, name):
                t1, t2 = rope_tmp
                v1 = t1[:, 0:n * HD].rearrange("p (n d) -> p n d", n=n)
                v2 = t2[:, 0:n * HD].rearrange("p (n a d) -> p n a d", n=n, a=2)
                tt(v1, src, every(cos, n), ALU.mult)
                swapped = src.rearrange("p n (a d) -> p n a d", a=2)[:, :, ::-1, :]
                ins = tt(v2, swapped, every(sin.rearrange("p (a d) -> p a d", a=2), n), ALU.mult)
                name[0](ins)
                link(tt(dst, v1, t2[:, 0:n * HD].rearrange("p (n d) -> p n d", n=n), ALU.add), name[1])

            for L in range(DEPTH):
                rope_tmp = (tmp_a, tmp_b)
                for t in range(TT):
                    bank = full(dve, ("xT", L, t, 1))
                    free(dve.tensor_copy(xT[:, 4:8, t * P:(t + 1) * P], bank[:, :].rearrange("p (j s) -> p j s", j=4)), ("xT", L, t, 1))
                if L == 0:
                    dve.wait_ge(sem("in_const"), 32)
                for t in range(TT):
                    bank = full(dve, ("rqk", L, t))
                    rope(rot[:, t, :].rearrange("p (n d) -> p n d", n=8), bank[:, :].rearrange("p (n d) -> p n d", n=8), 8,
                         const[:, C_COSA + t * HD:C_COSA + (t + 1) * HD], const[:, C_SINA + t * HD:C_SINA + (t + 1) * HD],
                         (lambda ins, nm=("rqk", L, t): (free(ins, nm), taken(dve, nm)), "rot"))
                if L == 0:
                    preamble()
                taken(dve, ("lx", L))
                pc = V_LRU + L * 16
                for w in range(4):
                    for b in range(2):
                        tap = par[:, pc + b * 4 + w:pc + b * 4 + w + 1]
                        src = lru_x[:, b, w:w + S]
                        if w == 0:
                            ins = ts(conv[:, b, :], src, tap, ALU.mult, par[:, pc + 8 + b:pc + 9 + b], ALU.add)
                        else:
                            ins = stt(conv[:, b, :], src, tap, conv[:, b, :], ALU.mult, ALU.add)
                        if b == 1:
                            link(ins, "conv" if w == 3 else "dve_step")
                dve.wait_ge(sem("lg_tanh"), L + 1)
                bank = full(dve, ("lg", L))
                free(stt(lru_gate.rearrange("p b s -> p (b s)"), tanh_buf[:, 0, :], 1.0, bank[:, :], ALU.add, ALU.mult), ("lg", L))
                if L == 0:
                    dve.wait_ge(sem("cond_tanh"), 2)
                    for j in range(2):
                        link(stt(cond[j], cond_tmp[j], 1.0, cond[j], ALU.add, ALU.mult))
                modulation(6 * L)
                bank = full(dve, ("kcvc", L))
                for b in range(2):
                    ins = tt(blocksT[:, b, :, :], view(bank[:, :], b * S, [[1, CMP_L], [CMP_S, CMP_N]]),
                             every(par[:, V_POS + (L * 2 + b) * CMP_L:V_POS + (L * 2 + b + 1) * CMP_L], CMP_N, 2), ALU.add)
                free(ins, ("kcvc", L))
                modulation(6 * L + 1)
                if L == 0:
                    dve.wait_ge(sem("rms_sq"), 2)
                    link(ts(var[:, 0:2], sumsq[:, 0:2], 1.0 / D, ALU.mult, EPS_RMS, ALU.add))
                    inverse_root(2)
                    for t in range(TT):
                        link(ts(hc_x[:, t, :], hc_x[:, t, :], rstd[:, t:t + 1], ALU.mult), "ctx_rows")
                else:
                    add_bias(2, 3)
                    add_bias(5, 6)
                taken(dve, ("lr", L))
                for b in range(2):
                    ins = ts(lru_r[:, b, :], lru_r[:, b, :], 1.0, ALU.add, sp4[:, L * 2 + b:L * 2 + b + 1], ALU.mult)
                link(ins, "lru_la")
                taken(dve, ("li", L))
                link(stt(lru_i, lru_i, 1.0, conv, ALU.add, ALU.mult))
                dve.wait_ge(sem("lru_a"), 2 * (L + 1))
                link(ts(lru_r, lru_t, -1.0, ALU.mult, 1.0, ALU.add))
                link(dve.reciprocal(lru_r, lru_r))
                link(stt(lru_t, lru_t, -2.0, lru_r, ALU.mult, ALU.mult), "lru_v")
                modulation(6 * L + 2)
                for t in range(TT):
                    dve.wait_ge(sem("rg_tanh"), TT * L + t + 1)
                    bank = full(dve, ("rvg", L, t))
                    free(stt(ret_g[:, t, :], tanh_buf[:, 1 - t, 0:S], 1.0, bank[:, S:2 * S], ALU.add, ALU.mult), ("rvg", L, t))
                for t in range(TT):
                    dve.wait_ge(sem("ng_tanh"), TT * L + t + 1)
                    bank = full(dve, ("ng", L, t))
                    free(stt(nsa_g[:, t, :], tanh_buf[:, 1 - t, :], 1.0, bank[:, :], ALU.add, ALU.mult), ("ng", L, t))
                for t in range(TT):
                    taken(dve, ("vg", L, t))
                    link(ts(gates3[:, t, :, :].rearrange("p h b -> p (h b)"), nsa_gt[:, t, :], 1.0, ALU.add))
                    link(ts(gates3[:, t, :, 0], gates3[:, t, :, 0], const[:, C_ANY + t:C_ANY + t + 1], ALU.mult))
                modulation(6 * L + 3)
                if L == 0:
                    add_bias(0, 2)
                    gain(1, V_GMIX, "mix_gain")
                for j in range(3):
                    at = C_DECAY + (4 * P if j == 1 else 0)
                    for odd in range(2):
                        bank = full(dve, ("rs", L, j, odd))
                        free(tt(ret_s[:, j, :].rearrange("p (n o s) -> p n o s", n=2, o=2)[:, :, odd, :],
                                bank[:, 0:2 * P].rearrange("p (n s) -> p n s", n=2),
                                const[:, at:at + 4 * P].rearrange("p (n o s) -> p n o s", n=2, o=2)[:, :, odd, :],
                                ALU.mult), ("rs", L, j, odd))
                modulation(6 * L + 4)
                for t in range(TT):
                    cm = const[:, C_CMASK + t * CMP_N:C_CMASK + (t + 1) * CMP_N]
                    for g in range(2):
                        bank = full(dve, ("nc", L, t, g))
                        free(tt(cmp_s[:, t, 4 * g:4 * g + 4, :], bank[:, 0:4 * CMP_N].rearrange("p (h n) -> p h n", h=4),
                                every(cm, 4), ALU.add), ("nc", L, t, g))
                        taken(dve, ("nc", L, t, g))
                    link(dve.tensor_reduce(cmax, cmp_s[:, t, :, :], AX.X, ALU.max))
                    link(tt(cmp_s[:, t, :, :], cmp_s[:, t, :, :], every(cmax, CMP_N, 2), ALU.subtract), "cmp_sub")
                for t in range(TT):
                    bank = full(dve, ("ro", L, t))
                    free(dve.tensor_copy(y[:, t, 0:S], bank[:, 0:S]), ("ro", L, t))
                for t in range(TT):
                    dve.wait_ge(sem("cmp_probs"), TT * L + t + 1)
                    link(dve.tensor_reduce(sums[:, t, :, 0], cmp_s[:, t, :, :], AX.X, ALU.add))

                def lru_scan():
                    dve.wait_ge(sem("lru_sq"), L + 1)
                    link(stt(lru_i, lru_i, 0.5, lru_t, ALU.mult, ALU.mult))
                    for b in range(2):
                        ins = dve.tensor_tensor_scan(lru_h[:, b, :], lru_a[:, b, :], lru_i[:, b, :], 0.0, ALU.mult, ALU.add)
                    link(ins)
                    link(stt(yT[:, 6:8, :], lru_h, 0.5, lru_gate, ALU.mult, ALU.mult), "y_lru")

                def retention(t):
                    heads = y[:, t, 0:S].rearrange("p (h d) -> p h d", h=4)
                    centred = tmp_a[:, 0:S].rearrange("p (h d) -> p h d", h=4)
                    squares = tmp_b[:, 0:S].rearrange("p (h d) -> p h d", h=4)
                    taken(dve, ("ro", L, t))
                    link(dve.tensor_reduce(stat[:, 0:4], heads, AX.X, ALU.add))
                    link(ts(stat[:, 0:4], stat[:, 0:4], -1.0 / HD, ALU.mult))
                    link(tt(centred, heads, every(stat[:, 0:4], HD, 2), ALU.add))
                    link(tt(squares, centred, centred, ALU.mult))
                    link(dve.tensor_reduce(stat2[:, 0:4], squares, AX.X, ALU.add))
                    link(ts(var[:, 0:4], stat2[:, 0:4], 1.0 / HD, ALU.mult, EPS_LN, ALU.add))
                    inverse_root(4)
                    link(tt(squares, centred, every(rstd[:, 0:4], HD, 2), ALU.mult))
                    link(stt(y[:, t, 0:S], tmp_b[:, 0:S], 0.5, ret_g[:, t, :], ALU.mult, ALU.mult), "y_ret")

                def layer_norm(t):
                    for j in range(2):
                        ins = dve.bn_stats(bn[:, j, :], z[:, t, j * 512:(j + 1) * 512])
                    link(ins)
                    link(dve.bn_aggr(mvar, bn))
                    link(ts(var[:, 0:1], mvar[:, 1:2], EPS_LN, ALU.add))
                    dve.sem_inc(sem("var_ready"), 1)
                    link(stt(z[:, t, :], z[:, t, :], mvar[:, 0:1], ln_gb[:, 0, :], ALU.subtract, ALU.mult))
                    root_back()
                    link(stt(x3[:, t, :], z[:, t, :], rstd[:, 0:1], ln_gb[:, 1, :], ALU.mult, ALU.add), "x_next")

                def nsa_max(i):
                    t, h = items[i]
                    nk = (t + 1) * P
                    bank = full(dve, ("ns", L, i))
                    b3 = bank[:, 0:2 * nk].rearrange("p (b k) -> p b k", b=2)
                    link(tt(b3[:, :, t * P:nk], b3[:, :, t * P:nk], every(const[:, C_TRIL:C_TRIL + P], 2), ALU.add))
                    link(dve.tensor_reduce(neg_max[:, i % 4, :], b3, AX.X, ALU.max, negate=True), "nsa_max")

                def nsa_out(j):
                    t, h = items[2 * j]
                    bank = full(dve, ("no", L, j))
                    s6 = sums[:, t, h:h + 2, :].rearrange("p h b -> p (h b)")
                    link(dve.reciprocal(coef, s6))
                    link(tt(coef, coef, gates3[:, t, h:h + 2, :].rearrange("p h b -> p (h b)"), ALU.mult))
                    o6 = tmp_a[:, 0:6 * HD].rearrange("p (n d) -> p n d", n=6)
                    free(tt(o6, bank[:, 0:6 * HD].rearrange("p (n d) -> p n d", n=6), every(coef, HD, 2), ALU.mult), ("no", L, j))
                    taken(dve, ("no", L, j))
                    link(dve.tensor_reduce(tmp_b[:, 0:2 * HD].rearrange("p (h d) -> p h d", h=2),
                                           tmp_a[:, 0:6 * HD].rearrange("p (h b d) -> p h d b", h=2, b=3), AX.X, ALU.add))
                    ins = stt(y[:, t, S + h * HD:S + (h + 2) * HD], tmp_b[:, 0:2 * HD], 0.25, nsa_g[:, t, h * HD:(h + 2) * HD],
                              ALU.mult, ALU.mult)
                    link(ins, "y_nsa" if h == 6 else "dve_step")

                nsa_max(0)
                nsa_max(1)
                if L == 0:
                    for t in range(TT):
                        modulated("hc", t, 1, 0, 1, 0)
                for i in range(len(items)):
                    if i + 2 < len(items):
                        nsa_max(i + 2)
                    if i == 0:
                        lru_scan()
                    if i in (1, 3):
                        retention(i // 2)
                    if i >= 13:
                        q = i - 13
                        bank = full(dve, ("wq", L, q))
                        c = slice(q * S, (q + 1) * S)
                        free(stt(z[:, 0, c], x3[:, 0, c], ALPHA, bank[:, 0:S], ALU.mult, ALU.add), ("wq", L, q))
                    if i % 2 == 0:
                        bank = full(dve, ("nT", L, i))
                        n = 2 * (items[i][0] + 1) * P
                        free(dve.tensor_copy(probsT[:, 0, 0:n], bank[:, 0:n]), ("nT", L, i))
                        if i:
                            nsa_out(i // 2 - 1)
                nsa_out(len(items) // 2 - 1)
                bank = full(dve, ("wq", L, 3))
                free(stt(z[:, 0, 3 * S:4 * S], x3[:, 0, 3 * S:4 * S], ALPHA, bank[:, 0:S], ALU.mult, ALU.add), ("wq", L, 3))
                dve.wait_ge(sem("in_ln"), 32 * (L + 1))
                for q in range(4):
                    taken(dve, ("wq", L, q))
                layer_norm(0)
                modulation(6 * L + 5)
                if L:
                    add_bias(3, 5)
                    gain(4, V_GFFN, "ffn_gain")
                for half in range(2):
                    bank = full(dve, ("wo", L, half))
                    c = slice(half * 512, (half + 1) * 512)
                    free(stt(z[:, 1, c], x3[:, 1, c], ALPHA, bank[:, :], ALU.mult, ALU.add), ("wo", L, half))
                    taken(dve, ("wo", L, half))
                layer_norm(1)

            def rms_rows(dst, t, ss, squares):
                dve.wait_ge(sem("rms_sq"), squares)
                link(ts(var[:, 0:1], ss, 1.0 / D, ALU.mult, EPS_RMS, ALU.add))
                inverse_root(1)
                link(ts(dst[:, t, :], x3[:, t, :], rstd[:, 0:1], ALU.mult), "h_rows")

            for t in range(TT):
                rms_rows(hl, t, sumsq[:, 2 + t:3 + t], 3 + t)
                modulated("hl", t, 1, 0, 0, S)
            for t in range(TT):
                bank = full(dve, ("aq", t))
                free(dve.tensor_copy(aq[:, t, :], bank[:, :]), ("aq", t))
            dve.wait_ge(sem("fgate_exp"), 1)
            log1p_half(rt_a[0:8, :], rt_b[0:8, :], rows[7], rows[2])
            link(ts(rows[1], rows[1], 0.0, ALU.min))
            link(stt(rows[2], rows[2], -2.0, rows[1], ALU.mult, ALU.add))
            link(dve.memset(rows[7], 0.0))
            link(dve.tensor_tensor_scan(rows[3], rows[2], rows[7], 0.0, ALU.add, ALU.add))
            link(dve.tensor_tensor_scan(rows[4][:, S - 1::-1], rows[2][:, S - 1::-1], rows[7][:, 0:S], 0.0, ALU.add, ALU.add))
            link(dve.tensor_tensor_scan(rows[4][:, 2 * S - 1:S - 1:-1], rows[2][:, 2 * S - 1:S - 1:-1], rows[7][:, 0:S],
                                        rows[4][:, 0:1], ALU.add, ALU.add))
            link(tt(rows[5], rows[0], rows[3], ALU.subtract))
            link(tt(rows[6], rows[0], rows[4], ALU.subtract), "gate_rows")
            for r in range(2, 4):
                bank = full(dve, ("akv", r))
                free(dve.tensor_copy(akv[:, r, :], bank[:, 0:256]), ("akv", r))
            for r in range(4):
                taken(dve, ("akv", r))
            dve.wait_ge(sem("in_small"), 64)
            rope_tmp = (rt_a, rt_b)
            k4 = akv[:, :, 0:P].rearrange("p t (n d) -> p t n d", n=2)
            sq4 = rt_a.rearrange("p (t n d) -> p t n d", t=4, n=2)
            link(tt(sq4, k4, k4, ALU.mult))
            link(dve.tensor_reduce(stat[:, 0:8], rt_a.rearrange("p (n d) -> p n d", n=8), AX.X, ALU.add))
            link(ts(var[:, 0:8], stat[:, 0:8], 1.0 / HD, ALU.mult, EPS_RMS, ALU.add))
            inverse_root(8)
            link(tt(k4, k4, every(rstd[:, 0:8].rearrange("p (t n) -> p t n", t=4), HD, 3), ALU.mult))
            link(tt(k4, k4, every(every(qk_g[:, 1, :], 2), 4), ALU.mult))
            for t in range(TT):
                src = akv[:, 2 + t, 0:P].rearrange("p (n d) -> p n d", n=2)
                rope(src, src, 2, const[:, C_COSB + t * HD:C_COSB + (t + 1) * HD], const[:, C_SINB + t * HD:C_SINB + (t + 1) * HD],
                     (link, "ak" if t else "dve_step"))
            for t in range(TT):
                taken(dve, ("aq", t))
                q3 = aq[:, t, :].rearrange("p (n d) -> p n d", n=8)
                s3 = rt_a.rearrange("p (n d) -> p n d", n=8)
                link(tt(s3, q3, q3, ALU.mult))
                link(dve.tensor_reduce(stat[:, 0:8], s3, AX.X, ALU.add))
                link(ts(var[:, 0:8], stat[:, 0:8], 1.0 / HD, ALU.mult, EPS_RMS, ALU.add))
                inverse_root(8)
                link(tt(q3, q3, every(rstd[:, 0:8], HD, 2), ALU.mult))
                link(stt(q3, q3, HD ** -0.5, every(qk_g[:, 0, :], 8), ALU.mult, ALU.mult))
                cos = const[:, C_COSB + t * HD:C_COSB + (t + 1) * HD]
                sin = const[:, C_SINB + t * HD:C_SINB + (t + 1) * HD]
                tt(s3, q3, every(cos, 8), ALU.mult)
                link(tt(rt_b.rearrange("p (n a d) -> p n a d", n=8, a=2),
                        q3.rearrange("p n (a d) -> p n a d", a=2)[:, :, ::-1, :],
                        every(sin.rearrange("p (a d) -> p a d", a=2), 8), ALU.mult))
                link(tt(aq[:, t, :].rearrange("p (r g d) -> p g r d", r=4, g=2),
                        rt_a.rearrange("p (g r d) -> p g r d", g=2, r=4),
                        rt_b.rearrange("p (g r d) -> p g r d", g=2, r=4), ALU.add), "aq")
            link(ts(negsink, sink, -1.0, ALU.mult))

            def attn_max(i):
                t, h = items[i]
                bank = full(dve, ("as", i))
                edge, m = (slice(3 * P, 4 * P), C_TRIL) if t == 0 else (slice(2 * P, 3 * P), C_TRIU)
                link(tt(bank[:, edge], bank[:, edge], const[:, m:m + P], ALU.add))
                link(dve.tensor_reduce(stat[:, 0:1], bank[:, :], AX.X, ALU.max, negate=True))
                link(tt(nmA[:, t, h:h + 1], stat[:, 0:1], negsink[:, h:h + 1], ALU.min), "attn_max")

            def attn_out(t):
                bank = full(dve, ("ao", t))
                free(tt(a_lat[:, t, :].rearrange("p (h d) -> p h d", h=8), bank[:, :].rearrange("p (h d) -> p h d", h=8),
                        every(es, HD, 2), ALU.mult), ("ao", t))
                taken(dve, ("ao", t))

            attn_max(0)
            attn_max(1)
            for i in range(len(items)):
                if i + 2 < len(items):
                    attn_max(i + 2)
                if i % 2 == 0:
                    bank = full(dve, ("aT_", i))
                    free(dve.tensor_copy(probs2T[:, 0, :], bank[:, :]), ("aT_", i))
                    if i == 8:
                        attn_out(0)
                if i % 8 == 7:
                    t = i // 8
                    link(tt(es, nmA[:, t, :], sink, ALU.add), "sink_sub")
                    dve.wait_ge(sem("sink_exp"), t + 1)
                    link(tt(es, es, den[:, t, :], ALU.add))
                    link(dve.reciprocal(es, es))
            attn_out(1)
            taken(dve, ("fc",))
            full(dve, ("aT_", 15))
            for h in range(MH):
                for d in range(2):
                    bank = full(dve, ("G", d, h))
                    for t in range(TT):
                        m = C_MM + (d * TT + t) * 512
                        j = d * TT + t
                        ins = dve.tensor_tensor_reduce(out=dw[:, j, :], in0=bank[:, :], in1=const[:, m:m + 512], scale=1.0,
                                                       scalar=0.0, op0=ALU.add, op1=ALU.max, accum_out=mu[:, j:j + 1])
                    free(ins, ("G", d, h))
                    taken(dve, ("G", d, h))
                link(ts(negmu, mu, -1.0, ALU.mult))
                ft = view(fcol, h, [[TT * 8 + 4, 2], [8, TT]])
                link(stt(flo_in.rearrange("p (d t) -> p d t", d=2), ft, -1.0, negmu.rearrange("p (d t) -> p d t", d=2),
                         ALU.mult, ALU.add), "mlstm_mu")
                dve.wait_ge(sem("mlstm_w"), 5 * (h + 1))
                for t in range(TT):
                    bank = full(dve, ("qk", h, t))
                    for d in range(2):
                        j = d * TT + t
                        ins = dve.tensor_tensor_reduce(out=dw[:, j, :], in0=bank[:, :], in1=dw[:, j, :], scale=1.0,
                                                       scalar=0.0, op0=ALU.mult, op1=ALU.add, accum_out=mden[:, j:j + 1])
                    free(ins, ("qk", h, t))
                    taken(dve, ("qk", h, t))
                link(stt(mabs, mden, -1.0, mden, ALU.mult, ALU.max))
                link(tt(mabs, mabs, flo_e, ALU.max))
                link(dve.reciprocal(mrec, mabs))
                for t in range(TT):
                    i = TT * h + t
                    if i >= 2:
                        full(dve, ("mT_", i - 2))
                    link(ts(probs2[:, i % 2, :], dw[:, t, :], mrec[:, t:t + 1], ALU.mult))
                    link(stt(probs2[:, i % 2, :], dw[:, TT + t, :], mrec[:, TT + t:TT + t + 1], probs2[:, i % 2, :],
                             ALU.mult, ALU.add), "mlstm_s")
                    if i >= 4:
                        half = (i - 4) // 2
                        bank = full(dve, ("ba", half, t))
                        free(stt(mrg[:, t, half * 512:(half + 1) * 512], gates[:, half * 4 + 2 + t, :], 1.0, bank[:, :],
                                 ALU.add, ALU.mult), ("ba", half, t))
            for t in range(TT):
                dve.wait_ge(sem("mlstm_sq"), t + 1)
                link(dve.tensor_reduce(stat[:, 0:4], dw[:, t, :].rearrange("p (h d) -> p h d", h=MH), AX.X, ALU.add))
                link(ts(var[:, 0:4], stat[:, 0:4], 1.0 / MD, ALU.mult, EPS_RMS, ALU.add))
                inverse_root(4)
                bank = full(dve, ("mo", t))
                free(tt(rt_a.rearrange("p (h d) -> p h d", h=MH), bank[:, :].rearrange("p (h d) -> p h d", h=MH),
                        every(rstd[:, 0:4], MD, 2), ALU.mult), ("mo", t))
                taken(dve, ("mo", t))
                link(stt(rt_a, rt_a, 0.5, norm_g, ALU.mult, ALU.mult))
                taken(dve, ("mog", t))
                if t == 0:
                    dve.wait_ge(sem("in_norm_g"), 16)
                link(stt(m_lat[:, t, :], mo_t[:, t, :], 1.0, rt_a, ALU.add, ALU.mult), "m_lat")
            for half in range(2):
                c = slice(half * 512, (half + 1) * 512)
                for t in range(TT):
                    bank = full(dve, ("bm", half, t))
                    free(stt(rt_b, gates[:, half * 4 + t, :], 1.0, bank[:, :], ALU.add, ALU.mult), ("bm", half, t))
                    taken(dve, ("bm", half, t))
                    link(tt(mrg[:, t, c], mrg[:, t, c], rt_b, ALU.add), "mrg")
            for t in range(TT):
                bank = full(dve, ("gT", t, 1))
                free(dve.tensor_copy(mrgT[:, 4:8, t * P:(t + 1) * P], bank[:, :].rearrange("p (j s) -> p j s", j=4)), ("gT", t, 1))
            for t in range(TT):
                for half in range(2):
                    c = slice(half * 512, (half + 1) * 512)
                    bank = full(dve, ("wo2", half, t))
                    free(stt(rt_a, bank[:, :], 0.5, gate_rows[:, 0, c], ALU.mult, ALU.mult), ("wo2", half, t))
                    taken(dve, ("wo2", half, t))
                    link(tt(x3[:, t, c], x3[:, t, c], rt_a, ALU.add), "x1" if half else "dve_step")
                rms_rows(h2, t, sumsq[:, t:t + 1], 4 + t + 1)
                if t == 0:
                    modulated("pT", t, 1, 3, 0, S)
            def step(ins):
                body["n"] += 1
                ins.then_inc(sem("expert_step"), 1)
                dve.wait_ge(sem("expert_step"), body["it"] * STEPS + (body["base"] + body["n"]))

            def step_go(ins):
                step(ins)
                dve.sem_inc(sem("top_go"), 1)

            def top16(values, indices, src, scratch):
                step_go(dve.max(values[:, 0:8], src))
                step_go(dve.max_index(indices[:, 0:8], values[:, 0:8], src))
                step_go(dve.match_replace(scratch, values[:, 0:8], src, -3e38))
                step_go(dve.max(values[:, 8:16], scratch))
                step(dve.max_index(indices[:, 8:16], values[:, 8:16], scratch))

            def choose(it, head):
                s = head % 2
                flat = score.rearrange("p t l n -> p (t l n)")
                step_go(dve.tensor_copy(head_s, flat[:, bass.ds(it * (4 * NKEY) + head * 2 * NKEY, 2 * NKEY)]))
                for half in range(2):
                    k = slice(half * TOPK, (half + 1) * TOPK)
                    if half:
                        dve.sem_inc(sem("top_go"), 1)
                    top16(tops[:, k], topi[:, k], head_s[:, half * NKEY:(half + 1) * NKEY], work[:, 0:NKEY])
                step(dve.tensor_copy(topf, topi))
                step_go(tt(cand.rearrange("p (a b) -> p a b", a=TOPK), every(tops[:, 0:TOPK], TOPK, 2),
                        every(tops[:, TOPK:2 * TOPK], TOPK), ALU.add))
                top16(best, bpos, cand, work)
                ts(bhl[:, 0:TOPK], bpos, 4, ALU.logical_shift_right)
                step(ts(bhl[:, TOPK:2 * TOPK], bpos, TOPK - 1, ALU.bitwise_and))
                step(dve.tensor_copy(fhl, bhl))
                hot3 = hot.rearrange("p (k a) -> p k a", k=TOPK)
                iota = const[:, C_IOTA:C_IOTA + TOPK]
                for half, dst in enumerate((sel1, sel2)):
                    k = slice(half * TOPK, (half + 1) * TOPK)
                    step(tt(hot3, every(fhl[:, k], TOPK, 2), every(iota, TOPK), ALU.is_equal))
                    step(tt(hot3, hot3, every(topf[:, k], TOPK), ALU.mult))
                    step(dve.tensor_reduce(dst, hot3, AX.X, ALU.add))
                dve.wait_ge(sem("idx_copied"), it * 2 + (CREDIT + head + 1 - 2))
                stt(idx_next[:, s * TOPK:(s + 1) * TOPK], sel1, float(NKEY), sel2, ALU.mult, ALU.add).then_inc(sem("idx_ready"), 1)
                ts(esum[:, 0:1], best[:, 0:1], -1.0, ALU.mult).then_inc(sem("top_sub"), 1)
                dve.wait_ge(sem("top_exp"), it * 2 + (head + 1))
                step(dve.reciprocal(esum[:, 2:3], esum[:, 1:2]))
                step(ts(gate_next[:, s * TOPK:(s + 1) * TOPK], bexp, esum[:, 2:3], ALU.mult, 0.5, ALU.mult))

            def weigh(it, t, head):
                s = head % 2
                for r in range(TOPK):
                    at = head * TOPK + r
                    dve.wait_ge(sem(f"u_full{r % RING}"), it * (16 * 2 * TOPK // RING) + 16 * (at // RING + 1))
                    row = u_ring[r % RING]
                    dve.tensor_tensor_reduce(out=row, in0=row, in1=h2[:, t, :], scale=1.0, scalar=0.0, op0=ALU.mult,
                                             op1=ALU.add, accum_out=dots[:, s * TOPK + r:s * TOPK + r + 1]).then_inc(sem("u_used"), 1)
                dve.wait_ge(sem("u_used"), it * (2 * TOPK) + (CREDIT + (head + 1) * TOPK))
                hd = dots[:, s * TOPK:(s + 1) * TOPK]
                wv = wcur[:, s * TOPK:(s + 1) * TOPK]
                step(tt(d_a, hd, hd, ALU.mult))
                step(ts(d_a, d_a, 0.044715, ALU.mult, 1.0, ALU.add))
                stt(d_a, d_a, 0.7978845608028654, hd, ALU.mult, ALU.mult).then_inc(sem("gelu_in"), 1)
                dve.wait_ge(sem("gelu_tanh"), it * 2 + (head + 1))
                step(stt(d_b, d_b, 1.0, hd, ALU.add, ALU.mult))
                dve.wait_ge(sem("diag_ready"), it * (2 * TOPK) + (CREDIT + (head - 1) * TOPK))
                tt(wv, d_b, gate_next[:, s * TOPK:(s + 1) * TOPK], ALU.mult).then_inc(sem("w_ready"), 1)
                dve.wait_ge(sem("w_ready"), it * 2 + (head + 1))

            def result(t):
                for half in range(2):
                    c = slice(half * 512, (half + 1) * 512)
                    bank = full(dve, ("pv", t, half))
                    free(tt(rt_a, bank[:, :], gate_rows[:, 1, c], ALU.mult), ("pv", t, half))
                    taken(dve, ("pv", t, half))
                    link(tt(x3[:, t, c], x3[:, t, c], rt_a, ALU.add), "result" if half else "dve_step")

            dve.sem_inc(sem("u_used"), CREDIT)
            body = {"it": 0, "base": 0, "n": 0}
            for head in range(2):
                dve.wait_ge(sem("scores"), 1)
                choose(0, head)
            for t in range(TT):
                for half in range(2):
                    taken(dve, ("h2", t, half))
            before = body["n"]
            for t in range(TT):
                with dve.Fori(0, EH // 2 - t) as it:
                    body.update(it=it, base=before + t * (EH // 2) * STEPS, n=0)
                    dve.wait_ge(sem("scores"), it + (t * EH // 2 + 2))
                    for s in range(2):
                        weigh(it, t, t * EH + s)
                        choose(it, t * EH + s + 2)
                    assert body["n"] == STEPS, body
            result(0)
            body.update(it=0, base=before + (TT * EH // 2 - 1) * STEPS, n=0)
            for s in range(2):
                weigh(0, TT - 1, TT * EH - 2 + s)
            result(1)

        @block.gpsimd
        def _(pool):
            asked = [0]

            def root(cols):
                asked[0] += 1
                pool.wait_ge(sem("var_ready"), asked[0])
                pool.tensor_tensor(rstd[:, 0:cols], var[:, 0:cols], half8[:, 0:cols], ALU.pow).then_inc(sem("root_done"), 1)

            pool.wait_ge(sem("in_const"), 32)
            for cols in (2, 4, 4, 1, 1):
                root(cols)
            for cols in (4, 4, 1, 1):
                root(cols)
            for cols in (1, 1, 8, 8, 8, 4, 4, 1, 1):
                root(cols)
            pool.sem_inc(sem("v_used"), CREDIT)
            pool.sem_inc(sem("idx_copied"), CREDIT)

            def indices(it, head):
                if head < TT * EH:
                    pool.wait_ge(sem("idx_ready"), it * 2 + (head + 1))
                    pool.wait_ge(sem("u_used"), it * (2 * TOPK) + (CREDIT + (head - 1) * TOPK))
                    s = head % 2
                    pool.sem_inc(sem("gather_go"), 1)
                    pool.tensor_copy(idx_u[:, s * TOPK:(s + 1) * TOPK], idx_next[:, s * TOPK:(s + 1) * TOPK]
                                     ).then_inc(sem("idx_copied"), 1)
                if head:
                    s = (head - 1) % 2
                    pool.wait_ge(sem("v_used"), it * (2 * TOPK) + (CREDIT + (head - 2) * TOPK))
                    pool.sem_inc(sem("gather_go"), 1)
                    pool.tensor_copy(idx_v[:, s * TOPK:(s + 1) * TOPK], idx_u[:, s * TOPK:(s + 1) * TOPK]
                                     ).then_inc(sem("idx_v_copied"), 1)
                    pool.wait_ge(sem("idx_v_copied"), it * 2 + head)
                if head < TT * EH:
                    pool.wait_ge(sem("idx_copied"), it * 2 + (CREDIT + head + 1))
                    pool.sem_inc(sem("gather_go"), 1)

            def gather(it, head, r, which):
                s = head % 2
                at = head * TOPK + r
                row, table, cur = {"u": (u_ring[r % RING], a["peer_u"], idx_u),
                                   "v": (v_ring[r % RING], a["peer_v"], idx_v)}[which]
                if r % 4 == 0:
                    pool.wait_ge(sem(which + "_used"), it * (2 * TOPK) + (CREDIT + at + 4 - RING))
                    pool.sem_inc(sem("gather_go"), 1)
                pool.indirect_dma_start(out=row, out_offset=None, in_=table,
                                        in_offset=bass.IndirectOffsetOnAxis(ap=cur[:, s * TOPK + r:s * TOPK + r + 1], axis=0)
                                        ).then_inc(sem(f"{which}_full{r % RING}"), 16)

            indices(0, 0)
            for r in range(TOPK):
                gather(0, 0, r, "u")
            with pool.Fori(0, TT * EH // 2 - 1) as it:
                for s in range(2):
                    indices(it, s + 1)
                    for r in range(TOPK):
                        gather(it, s + 1, r, "u")
                        gather(it, s, r, "v")
            last = TT * EH - 1
            indices(0, last)
            for r in range(TOPK):
                gather(0, last, r, "u")
                gather(0, last - 1, r, "v")
            indices(0, last + 1)
            for r in range(TOPK):
                gather(0, last, r, "v")


def pack(w, n):
    k = w.shape[0] // P
    return np.ascontiguousarray(w.reshape(k, P, n, -1).transpose(2, 1, 0, 3)).reshape(n, P, -1)


def layout(i):
    f = {k: np.asarray(v) for k, v in i.items()}
    at = np.cumsum([0, 256, 256, 256, 256, 512, 128, 128, 128, 128, 128, 128, 512, 24, 256, 256])
    rq, rk, rv, rg, nq, nkc, nvc, nks, nvs, nkw, nvw, ng, ngl, lx, lg = [np.arange(p, q) for p, q in zip(at[:-1], at[1:])]
    pairs = nq.reshape(2, 4, HD).transpose(1, 0, 2).ravel()
    order = np.concatenate([lx, lg, rq, rk, pairs, nkc, nvc, nks, nkw, rv, rg, ng])
    a = {"x": f["x"][0], "const": constants()}
    a["w1"] = np.stack([pack(f["w_in"][l][:, order], 6) for l in range(DEPTH)])
    a["w1b"] = np.stack([pack(f["w_in"][l][:, np.concatenate([nvs, nvw, ngl])], 1)[0] for l in range(DEPTH)])
    cw = f["nsa_cmp_w"].reshape(DEPTH, 2, CMP_L, HD, HD).transpose(0, 3, 1, 2, 4).reshape(DEPTH, HD, -1)
    a["cmp"] = np.ascontiguousarray(np.concatenate([cw, cw], 1))
    a["wo"] = np.stack([pack(f["w_out"][l], 2) for l in range(DEPTH)])
    a["ln_g"], a["ln_b"] = f["ln_g"], f["ln_b"]
    par = np.zeros((P, V_END), np.float32)
    for l in range(DEPTH):
        c = V_LRU + l * 16
        for b in range(2):
            r = slice(b * P, (b + 1) * P)
            par[:, c + 4 * b:c + 4 * b + 4] = f["lru_conv_w"][l][:, r].T
            for j, name in enumerate(("lru_conv_b", "lru_b_a", "lru_b_x", "lru_lambda")):
                par[:, c + 8 + 2 * j + b] = f[name][l][r]
        for b in range(2):
            c = V_POS + (l * 2 + b) * CMP_L
            pos = f["nsa_cmp_pos"][l, b].T
            par[:, c:c + CMP_L] = np.concatenate([pos, pos], 0)
        for n, name in enumerate(("lru_w_a", "lru_w_x")):
            for b in range(2):
                c = V_WG + ((l * 2 + n) * 2 + b) * HD
                par[:, c:c + HD] = f[name][l][2 * b:2 * b + 2].reshape(P, HD)
    mg = f["b_mgates_2"][0].reshape(2, 2, MH)
    par[0:8, V_MG] = mg[:, 0].ravel()
    par[0:8, V_MG + 1] = mg[:, 1].ravel()
    par[:, V_ADA:V_GMIX] = f["b_ada_2"][0].reshape(6 * KC, P).T
    par[:, V_GMIX:V_GFFN] = f["norm_mix_g_2"][0].reshape(KC, P).T
    par[:, V_GFFN:V_END] = f["norm_ffn_g_2"][0].reshape(KC, P).T
    a["par"] = par
    a["ctx"] = f["ctx_2"][0]
    a["cond"] = np.stack([f["c_2"][0], f["c_ctx_2"]])
    a["ada"] = np.ascontiguousarray(f["w_ada_2"][0].T.reshape(12, 4, P, D).transpose(0, 2, 1, 3)).reshape(12, P, -1)
    w = f["w_in_2"][0]
    at = np.cumsum([0, 512, 512, 512, 512, 16, 512, 128, 128, 1024, 1024])
    mq, mk, mv, mo, mg, aq, ak, av, gm, ga = [np.arange(p, q) for p, q in zip(at[:-1], at[1:])]
    mg = mg.reshape(2, 2, MH)
    order = np.concatenate([mk, mv, mq, aq, mo, gm[:512], ga[:512], gm[512:], ga[512:]])
    a["w2"] = pack(w[:, order], 9)
    a["w2b"] = pack(w[:, np.concatenate([ak, av])], 1)[0]
    a["wg2"] = pack(w[:, np.concatenate([mg[:, 0].ravel(), mg[:, 1].ravel()])], 1)[0].reshape(P, KC, 16)
    a["norm_g"] = f["mlstm_norm_g_2"]
    a["q_g"], a["k_g"], a["sink"] = f["attn_q_norm_g_2"], f["attn_k_norm_g_2"], f["attn_sink_2"]
    a["br"] = pack(np.concatenate([f["w_branch_m_2"][0], f["w_branch_a_2"][0]], 0), 2)
    a["wo2"] = pack(f["w_out_2"][0], 2)
    a["pq"] = pack(f["peer_w_query_2"][0], 4)
    a["sk"] = np.ascontiguousarray(f["peer_sub_keys_2"][0].transpose(3, 0, 1, 2)).reshape(P, 16 * NKEY)
    a["peer_u"], a["peer_v"] = f["peer_u_2"][0], f["peer_v_2"][0]
    return a


def kernel(**inputs):
    import concourse.bacc as bacc
    from concourse.bass_utils import run_bass_kernel_spmd

    arrays = layout(inputs)
    nc = bacc.Bacc("TRN2", target_bir_lowering=False, num_devices=1)
    a = {k: nc.dram_tensor(k + "_in", v.shape, F32, kind="ExternalInput").ap() for k, v in arrays.items()}
    out = nc.dram_tensor("result", (S, D), F32, kind="ExternalOutput").ap()
    program(nc, a, out)
    r = run_bass_kernel_spmd(nc, [{k + "_in": v for k, v in arrays.items()}], core_ids=[0])
    return r.results[0]["result"].reshape(1, S, D)
```
